# Optimizing a Trainium2 kernel written in Bass

```python
import jax, jax.numpy as jnp
from jax import lax
import numpy as np

D_MODEL = 1024
BATCH = 1
SEQ = 128
DEPTH = 1
DEC_BATCH = 1
DEC_SEQ = 2048
PAST_LEN = 256

GRID_W = 64
CHUNK = 128
D_A = 1024
H_A = 4
DH_A = D_A // H_A
D_B = 1024
G_B = 4
DG_B = D_B // G_B
N_IF = 2 * 2 * H_A
N_IN = 5 * D_A + N_IF + 3 * D_B + 2 * D_MODEL
EPS = 1e-6

kernel_name = "hybrid_mlstm_gmlp_diffusion_step"

def rmsnorm(x, g):
    xf = x.astype(jnp.float32)
    y = xf * lax.rsqrt(jnp.mean(xf * xf, axis=-1, keepdims=True) + EPS)
    return (y * g.astype(jnp.float32)).astype(x.dtype)

def split_cols(p):
    sizes = (D_A, D_A, D_A, D_A, D_A, N_IF, D_B, D_B, D_B, D_MODEL, D_MODEL)
    outs, start = [], 0
    for s in sizes:
        outs.append(p[..., start:start + s])
        start += s
    return outs

def mlstm_chunked(q, k, v, li, lf, C0, n0, m0, n_chunks):
    B, H, T, d = q.shape
    L = T // n_chunks
    q = q.reshape(B, H, n_chunks, L, d)
    k = k.reshape(B, H, n_chunks, L, d)
    v = v.reshape(B, H, n_chunks, L, d)
    li = li.reshape(B, H, n_chunks, L)
    lf = lf.reshape(B, H, n_chunks, L)
    b = jnp.cumsum(lf, axis=-1)
    bL = b[..., -1]
    w = bL[..., None] - b + li
    m_loc = jnp.max(w, axis=-1)
    e = jnp.exp(w - m_loc[..., None])
    C_loc = jnp.einsum('bhcs,bhcsv,bhcsk->bhcvk', e, v, k)
    n_loc = jnp.einsum('bhcs,bhcsk->bhck', e, k)

    def step(carry, inp):
        C, n, m = carry
        bL_c, ml_c, Cl_c, nl_c = inp
        m_new = jnp.maximum(bL_c + m, ml_c)
        sp = jnp.exp(bL_c + m - m_new)
        sl = jnp.exp(ml_c - m_new)
        C_new = sp[..., None, None] * C + sl[..., None, None] * Cl_c
        n_new = sp[..., None] * n + sl[..., None] * nl_c
        return (C_new, n_new, m_new), (C, n, m)

    mv = lambda t: jnp.moveaxis(t, 2, 0)
    (Cf, nf, mf), (Cs, ns, ms) = lax.scan(step, (C0, n0, m0), (mv(bL), mv(m_loc), mv(C_loc), mv(n_loc)))
    Cs = jnp.moveaxis(Cs, 0, 2)
    ns = jnp.moveaxis(ns, 0, 2)
    ms = jnp.moveaxis(ms, 0, 2)

    a = b + ms[..., None]
    Dm = b[..., :, None] - b[..., None, :] + li[..., None, :]
    causal = jnp.tril(jnp.ones((L, L), dtype=bool))
    Dm = jnp.where(causal, Dm, -jnp.inf)
    m_t = jnp.maximum(a, jnp.max(Dm, axis=-1))
    S = jnp.einsum('bhctd,bhcsd->bhcts', q, k) * jnp.exp(Dm - m_t[..., None])
    sc = jnp.exp(a - m_t)
    num = jnp.einsum('bhcts,bhcsv->bhctv', S, v) + sc[..., None] * jnp.einsum('bhcvk,bhctk->bhctv', Cs, q)
    den = jnp.sum(S, axis=-1) + sc * jnp.einsum('bhck,bhctk->bhct', ns, q)
    h = num / jnp.maximum(jnp.abs(den), jnp.exp(-m_t))[..., None]
    return h.reshape(B, H, T, d), (Cf, nf, mf)

def mlstm_bidir(q, k, v, if_pre, C0, n0, m0, n_chunks):
    li = jnp.transpose(if_pre[:, :, :, 0, :], (0, 2, 3, 1))
    lf = jax.nn.log_sigmoid(jnp.transpose(if_pre[:, :, :, 1, :], (0, 2, 3, 1)))
    h_f, (Cf, nf, mf) = mlstm_chunked(q, k, v, li[:, 0], lf[:, 0], C0[:, 0], n0[:, 0], m0[:, 0], n_chunks)
    rev = lambda t: jnp.flip(t, axis=2)
    h_b, (Cb, nb, mb) = mlstm_chunked(rev(q), rev(k), rev(v), jnp.flip(li[:, 1], -1), jnp.flip(lf[:, 1], -1),
                                      C0[:, 1], n0[:, 1], m0[:, 1], n_chunks)
    h = h_f + rev(h_b)
    return h, jnp.stack([Cf, Cb], axis=1), jnp.stack([nf, nb], axis=1), jnp.stack([mf, mb], axis=1)

def spatial_gate(v, g_sgu, w_s, b_s, n_chunks):
    B, T, _ = v.shape
    vn = rmsnorm(v, g_sgu).reshape(B, n_chunks, T // n_chunks, G_B, DG_B)
    s = jnp.einsum('gts,bcsgd->bctgd', w_s, vn) + jnp.transpose(b_s)[:, :, None]
    return s.reshape(B, T, D_B)

def mixer_layer(x, mod, C0, n0, m0, n_chunks, norm_g, w_in, b_if, g_sgu, w_s, b_s, w_proj_a, w_proj_b, w_out):
    B, T, _ = x.shape
    shift, scale, gate = jnp.split(mod, 3, axis=-1)
    h = rmsnorm(x, norm_g) * (1 + scale[:, None]) + shift[:, None]
    q, k, v, o, z_a, g_if, u, v_b, z_b, g_a, g_b = split_cols(h @ w_in)
    heads = lambda t: jnp.transpose(t.reshape(B, T, H_A, DH_A), (0, 2, 1, 3)).astype(jnp.float32)
    if_pre = (g_if.reshape(B, T, 2, 2, H_A) + b_if).astype(jnp.float32)
    h_a, Cn, nn_, mn = mlstm_bidir(heads(q) * (DH_A ** -0.5), heads(k), heads(v), if_pre, C0, n0, m0, n_chunks)
    h_a = jnp.transpose(h_a, (0, 2, 1, 3)).reshape(B, T, D_A).astype(x.dtype)
    y_a = jax.nn.sigmoid(o) * h_a * jax.nn.silu(z_a)
    y_b = u * spatial_gate(v_b, g_sgu, w_s, b_s, n_chunks) * jax.nn.silu(z_b)
    merged = jax.nn.sigmoid(g_a) * (y_a @ w_proj_a) + jax.nn.sigmoid(g_b) * (y_b @ w_proj_b)
    return x + gate[:, None] * (merged @ w_out), Cn, nn_, mn

def setup_inputs(seed: int = 0) -> dict:
    key = jax.random.key(seed)
    ks = jax.random.split(key, 20)
    nrm = lambda k, shape, s: jax.random.normal(k, shape, jnp.float32) * s
    f_bias = jnp.linspace(3.0, 6.0, H_A, dtype=jnp.float32)
    b_if = jnp.stack([nrm(ks[9], (DEPTH, 2, H_A), 0.1),
                      f_bias + nrm(ks[10], (DEPTH, 2, H_A), 0.1)], axis=2)
    return {
        "x_prompt": nrm(ks[0], (BATCH, SEQ, D_MODEL), 1.0),
        "x_sample": nrm(ks[1], (DEC_BATCH, DEC_SEQ, D_MODEL), 1.0),
        "c": nrm(ks[2], (DEC_BATCH, D_MODEL), 1.0),
        "state_C": nrm(ks[3], (DEC_BATCH, DEPTH, 2, H_A, DH_A, DH_A), 0.5),
        "state_n": nrm(ks[4], (DEC_BATCH, DEPTH, 2, H_A, DH_A), 0.5),
        "state_m": nrm(ks[5], (DEC_BATCH, DEPTH, 2, H_A), 1.0),
        "c_ctx": nrm(ks[6], (D_MODEL,), 1.0),
        "norm_g": 1.0 + nrm(ks[7], (DEPTH, D_MODEL), 0.02),
        "w_ada": nrm(ks[8], (DEPTH, D_MODEL, 3 * D_MODEL), 0.5 * D_MODEL ** -0.5),
        "b_ada": nrm(ks[11], (DEPTH, 3 * D_MODEL), 0.02),
        "w_in": nrm(ks[12], (DEPTH, D_MODEL, N_IN), D_MODEL ** -0.5),
        "b_if": b_if,
        "g_sgu": 1.0 + nrm(ks[13], (DEPTH, D_B), 0.02),
        "w_s": nrm(ks[14], (DEPTH, G_B, CHUNK, CHUNK), CHUNK ** -0.5),
        "b_s": 1.0 + nrm(ks[15], (DEPTH, G_B, CHUNK), 0.1),
        "w_proj_a": nrm(ks[16], (DEPTH, D_A, D_MODEL), D_A ** -0.5),
        "w_proj_b": nrm(ks[17], (DEPTH, D_B, D_MODEL), D_B ** -0.5),
        "w_out": nrm(ks[18], (DEPTH, D_MODEL, D_MODEL), D_MODEL ** -0.5),
        "norm_f": 1.0 + nrm(ks[19], (D_MODEL,), 0.02),
    }

def reference(x_prompt, x_sample, c, state_C, state_n, state_m, c_ctx, norm_g, w_ada, b_ada, w_in, b_if,
              g_sgu, w_s, b_s, w_proj_a, w_proj_b, w_out, norm_f):
    Bp, Tp, _ = x_prompt.shape
    Bs, Ts, _ = x_sample.shape
    rows = Ts // GRID_W
    nc_ctx = Tp // CHUNK
    nc_lat = (rows * GRID_W) // CHUNK
    f32 = jnp.float32
    C_ctx = jnp.zeros((Bp, 2, H_A, DH_A, DH_A), f32)
    n_ctx = jnp.zeros((Bp, 2, H_A, DH_A), f32)
    m_ctx = jnp.zeros((Bp, 2, H_A), f32)
    xp, xs = x_prompt, x_sample
    new_C, new_n, new_m = [], [], []
    for l in range(DEPTH):
        lw = (norm_g[l], w_in[l], b_if[l], g_sgu[l], w_s[l], b_s[l], w_proj_a[l], w_proj_b[l], w_out[l])
        mod_ctx = jax.nn.silu(c_ctx)[None] @ w_ada[l] + b_ada[l]
        mod_lat = jax.nn.silu(c) @ w_ada[l] + b_ada[l]
        xp, Cn, nn_, mn = mixer_layer(xp, mod_ctx, C_ctx, n_ctx, m_ctx, nc_ctx, *lw)
        new_C.append(Cn.astype(x_prompt.dtype))
        new_n.append(nn_.astype(x_prompt.dtype))
        new_m.append(mn.astype(x_prompt.dtype))
        xs, _, _, _ = mixer_layer(xs, mod_lat, state_C[:, l].astype(f32), state_n[:, l].astype(f32),
                                  state_m[:, l].astype(f32), nc_lat, *lw)
    y_prompt = rmsnorm(xp, norm_f)
    y_sample = rmsnorm(xs, norm_f)
    new_state_C = jnp.stack(new_C, axis=1)
    new_state_n = jnp.stack(new_n, axis=1)
    new_state_m = jnp.stack(new_m, axis=1)
    return (y_prompt, y_sample, new_state_C, new_state_n, new_state_m)


_drawn_inputs = setup_inputs


def setup_inputs(seed=0):
    import zlib

    import numpy as np

    out = dict(_drawn_inputs(seed))
    spreads = {}
    factors = {'state_C': 8.0,
     'state_n': 4.378,
     'state_m': 6.591,
     'g_sgu': 8.0,
     'b_s': 4.942,
     'norm_f': 2.84}
    for name, (base, spread) in spreads.items():
        noise = np.random.default_rng([zlib.crc32(name.encode()), seed]).standard_normal(out[name].shape)
        drawn = base * np.exp(spread * noise) if base else spread * noise
        out[name] = __import__('jax').numpy.asarray(drawn.astype(out[name].dtype))
    for name, factor in factors.items():
        out[name] = (out[name] * factor).astype(out[name].dtype)
    return out
```

```python
from contextlib import ExitStack

import concourse.bass as bass
from concourse import mybir

F32 = mybir.dt.float32
F32R = mybir.dt.float32r
ALU = mybir.AluOpType
ACT = mybir.ActivationFunctionType

P = 128
D = 1024
KT = D // P
H = 4
DH = D // H
HT = DH // P
N_IF = 2 * 2 * H
CTX = 1
LAT = 16
NC = CTX + LAT
TOK = NC * P
EPS = 1e-6
MASKED = -1.0e30
BLOCKS = [(b * 512, min(512, TOK - b * 512)) for b in range((TOK + 511) // 512)]
NB = len(BLOCKS)
DE = DH + 1

Q0, K0, V0, O0, Z0 = (i * D for i in range(5))
IF0 = 5 * D
U0, VB0, ZB0, GA0, GB0 = (IF0 + N_IF + i * D for i in range(5))


def wait(eng, sem, value):
    if not (isinstance(value, int) and value <= 0):
        eng.wait_ge(sem, value)


passed = []


def wait_alone(eng, sem, value):
    if not isinstance(value, int):
        eng.wait_ge(sem, value)
        eng.sem_inc(passed[-1], 1)
    elif value > 0:
        eng.wait_ge(sem, value)


def build(nc, x_prompt, x_sample, c, state_C, state_n, state_m, c_ctx, norm_g, w_ada, b_ada, w_in, b_if,
          g_sgu, w_s, b_s, w_proj_a, w_proj_b, w_out, norm_f,
          y_prompt, y_sample, new_C, new_n, new_m):
    top = ExitStack()
    held = []

    def sem(name, software_dma=False):
        if software_dma:
            return top.enter_context(nc.semaphore(name))
        made = nc.semaphore(name)
        held.append((made, made.__enter__()))
        return held[-1][1]

    def stage_end():
        with nc.Block() as block:
            @block.gpsimd
            def _(pool):
                for _, s in held:
                    pool.sem_clear(s)
        while held:
            held.pop()[0].__exit__(None, None, None)

    def sb(stack, name, shape, dt=F32):
        return stack.enter_context(nc.sbuf_tensor(name, shape, dt))

    def ps(stack, name, shape):
        return stack.enter_context(nc.psum_tensor(name, shape, F32))

    def dram(name, shape):
        return nc.dram_tensor(name, shape, F32, kind="Internal").ap()

    w_in2 = w_in[0]
    qT_d, kT_d, gateA_d, u_d, sga_d, sgb_d, m_d = (
        dram(n, [KT, P, TOK]) for n in
        ("qT_d", "kT_d", "gateA_d", "u_d", "sga_d", "sgb_d", "m_d"))
    v_d = dram("v_d", [TOK, D])
    vb_d = dram("vb_d", [TOK, D])
    if_d = dram("if_d", [N_IF, TOK])
    cols_d = dram("cols_d", [6 * H, TOK])
    r_d = dram("r_d", [2 * H, TOK])
    sp_d = dram("sp_d", [2 * H, NC])
    gate_d = dram("gate_d", [2, D])

    with top:
        passed.append(top.enter_context(nc.semaphore("passed")))
        ident = sb(top, "ident", [P, P])
        mask = sb(top, "mask", [P, 2, P])
        modT = sb(top, "modT", [P, 3 * KT, 2])
        modA = sb(top, "modA", [P, KT, 2])
        with ExitStack() as st:
            cT = sb(st, "cT", [P, KT, 2])
            csig = sb(st, "csig", [P, KT, 2])
            csil = sb(st, "csil", [P, KT, 2])
            wada = sb(st, "wada", [P, 2, KT, 512])
            badaT = sb(st, "badaT", [P, 3 * KT])
            gT = sb(st, "gT", [P, KT])
            psmod = ps(st, "psmod", [P, 3 * KT, 2])
            const_made = sem("const_made")
            c_loaded = sem("c_loaded")
            sig_done = sem("sig_done")
            silu_done = sem("silu_done")
            wada_loaded = [sem(f"wada_loaded{s}") for s in range(2)]
            mod_mm = [sem(f"mod_mm{s}") for s in range(2)]
            mod_biased = sem("mod_biased")
            mod_ready = sem("mod_ready")
            gate_stored = sem("gate_stored")
            GRP = 4
            with nc.Block() as block:
                @block.gpsimd
                def _(pool):
                    nc.gpsimd.memset(ident[:, :], 0.0).then_inc(const_made, 1)
                    nc.gpsimd.memset(mask[:, :, :], 0.0).then_inc(const_made, 1)
                    pool.wait_ge(const_made, 2)
                    nc.gpsimd.affine_select(out=ident[:, :], in_=ident[:, :], compare_op=ALU.not_equal,
                                            fill=1.0, base=0, pattern=[[-1, P]],
                                            channel_multiplier=1).then_inc(const_made, 1)
                    nc.gpsimd.affine_select(out=mask[:, 0, :], in_=mask[:, 0, :], compare_op=ALU.is_ge,
                                            fill=MASKED, base=0, pattern=[[1, P]],
                                            channel_multiplier=-1).then_inc(const_made, 1)
                    nc.gpsimd.affine_select(out=mask[:, 1, :], in_=mask[:, 1, :], compare_op=ALU.is_ge,
                                            fill=MASKED, base=0, pattern=[[-1, P]],
                                            channel_multiplier=1).then_inc(const_made, 1)

                @block.sync
                def _(sp):
                    with nc.allow_non_contiguous_dma("vectors onto partitions"):
                        sp.dma_start(cT[:, :, 0], c_ctx.rearrange("(k p) -> p k", p=P)).then_inc(c_loaded, 16)
                        sp.dma_start(cT[:, :, 1], c[0].rearrange("(k p) -> p k", p=P)).then_inc(c_loaded, 16)
                        sp.dma_start(badaT[:, :], b_ada[0].rearrange("(k p) -> p k", p=P)).then_inc(c_loaded, 16)
                        sp.dma_start(gT[:, :], norm_g[0].rearrange("(k p) -> p k", p=P)).then_inc(c_loaded, 16)
                    for g in range(6):
                        s = g % 2
                        if g >= 2:
                            sp.wait_ge(mod_mm[s], g // 2)
                        sp.dma_start(wada[:, s, :, :],
                                     w_ada[0][:, g * 512:(g + 1) * 512].rearrange("(k p) n -> p k n", p=P)
                                     ).then_inc(wada_loaded[s], 16)
                    sp.wait_ge(mod_ready, 1)
                    with nc.allow_non_contiguous_dma("gate rows"):
                        for j in range(2):
                            sp.dma_start(gate_d[j].rearrange("(k p) -> p k", p=P),
                                         modT[:, 2 * KT:, j]).then_inc(gate_stored, 16)
                    sp.wait_ge(gate_stored, 32)

                @block.scalar
                def _(act):
                    act.wait_ge(c_loaded, 64)
                    nc.scalar.activation(csig[:, :, :], cT[:, :, :], ACT.Sigmoid).then_inc(sig_done, 1)

                @block.tensor
                def _(pe):
                    pe.wait_ge(silu_done, 1)
                    for g in range(6):
                        s = g % 2
                        pe.wait_ge(wada_loaded[s], 16 * (g // 2 + 1))
                        for n in range(GRP):
                            for k in range(KT):
                                last = nc.tensor.matmul(psmod[:, g * GRP + n, :], wada[:, s, k, n * P:(n + 1) * P],
                                                        csil[:, k, :], start=(k == 0), stop=(k == KT - 1))
                        last.then_inc(mod_mm[s], 1)

                @block.vector
                def _(dve):
                    dve.wait_ge(sig_done, 1)
                    nc.vector.tensor_tensor(csil[:, :, :], cT[:, :, :], csig[:, :, :], ALU.mult).then_inc(silu_done, 1)
                    dve.wait_ge(mod_mm[1], 3)
                    nc.vector.tensor_tensor(modT[:, :, :], psmod[:, :, :],
                                            badaT[:, :].unsqueeze(2).broadcast_to([P, 3 * KT, 2]),
                                            ALU.add).then_inc(mod_biased, 1)
                    dve.wait_ge(mod_biased, 1)
                    for j in range(2):
                        nc.vector.scalar_tensor_tensor(out=modA[:, :, j], in0=modT[:, KT:2 * KT, j], scalar=1.0,
                                                       in1=gT[:, :], op0=ALU.add, op1=ALU.mult
                                                       ).then_inc(mod_ready, 1)

        stage_end()
        with ExitStack() as st:
            hsp = sb(st, "hsp", [P, 2, KT, TOK], F32R)
            norm_phase(nc, sem, sb, ps, x_prompt, x_sample, ident, modT, modA, hsp)
            stage_end()
            streamed_products(nc, sem, sb, ps, "p", hsp, [
                Phase("if", w_in2, [IF0], [if_d]),
                Phase("qk", w_in2, [Q0, K0], [qT_d, kT_d]),
                Phase("oz", w_in2, [O0, Z0], [gateA_d]),
                Phase("uz", w_in2, [U0, ZB0], [u_d]),
                Phase("gg", w_in2, [GA0, GB0], [sga_d, sgb_d]),
                Phase("nat", w_in2, [V0, VB0], [v_d, vb_d])])
            stage_end()
        cols = sb(top, "cols", [P, NC, 6 * H])
        spb = sb(top, "spb", [P, 2 * H, NC])
        gate_phase(nc, sem, sb, ps, if_d, b_if, state_m, cols_d, r_d, sp_d, new_m, ident, cols, spb)
        stage_end()
        with ExitStack() as st:
            ysp = sb(st, "ysp", [P, 2, KT, TOK], F32R)
            sgu_phase(nc, sem, sb, ps, vb_d, u_d, w_s, b_s, g_sgu, ident, ysp)
            stage_end()
            streamed_products(nc, sem, sb, ps, "b", ysp, [Phase("mg", w_proj_b[0], [0], [m_d], gain=sgb_d)])
            stage_end()
            mlstm_phase(nc, sem, sb, ps, qT_d, kT_d, v_d, gateA_d, r_d, state_C, state_n, new_C, new_n,
                        ident, mask, cols, spb, ysp)
            stage_end()
            streamed_products(nc, sem, sb, ps, "a", ysp,
                              [Phase("mg", w_proj_a[0], [0], [m_d], gain=sga_d, add=True)])
            stage_end()
        out_phase(nc, sem, sb, ps, m_d, w_out[0], gate_d, x_prompt, x_sample, norm_f, y_prompt, y_sample)


def norm_phase(nc, sem, sb, ps, x_prompt, x_sample, ident, modT, modA, hsp):
    half_made = sem("n_half_made")
    x_loaded = [sem(f"n_x_loaded{s}") for s in range(2)]
    sq_done = [sem(f"n_sq_done{s}") for s in range(2)]
    var_done = [sem(f"n_var_done{s}") for s in range(2)]
    rstd_done = [sem(f"n_rstd_done{s}") for s in range(2)]
    scaled = [sem(f"n_scaled{s}") for s in range(2)]
    turned = [sem(f"n_turned{s}") for s in range(2)]
    mod_mul = [sem(f"n_mod_mul{s}") for s in range(2)]
    mod_add = [sem(f"n_mod_add{s}") for s in range(2)]
    hi_done = [sem(f"n_hi_done{s}") for s in range(2)]
    lo_done = [sem(f"n_lo_done{s}") for s in range(2)]
    with ExitStack() as st:
        xt = sb(st, "n_xt", [P, 2, D])
        sq = sb(st, "n_sq", [P, D])
        ss = sb(st, "n_ss", [P, 2, 4])
        hx = sb(st, "n_hx", [P, 2, KT, P])
        pt = [ps(st, f"n_pt{s}", [P, KT, P]) for s in range(2)]

        def chunks(eng, step):
            step(0, 0, None, 0, 0)
            with eng.Fori(0, LAT // 2) as i:
                step(1, i, 2 * i, 1, (2 * i + CTX) * P)
                step(0, i + 1, 2 * i + 1, 1, (2 * i + 1 + CTX) * P)

        with nc.Block() as block:
            @block.sync
            def _(sp):
                def step(s, n, c, stream, t0):
                    wait_alone(sp, turned[s], n)
                    src = x_prompt[0] if c is None else x_sample[0][bass.ds(c * P, P), :]
                    sp.dma_start(xt[:, s, :], src).then_inc(x_loaded[s], 16)
                chunks(sp, step)

            @block.gpsimd
            def _(pool):
                def step(s, n, c, stream, t0):
                    pool.wait_ge(var_done[s], n + 1)
                    nc.gpsimd.tensor_tensor(ss[:, s, 2:3], ss[:, s, 1:2], ss[:, s, 3:4], ALU.pow).then_inc(rstd_done[s], 1)
                nc.gpsimd.memset(ss[:, :, 3:4], -0.5).then_inc(half_made, 1)
                pool.wait_ge(half_made, 1)
                chunks(pool, step)

            @block.scalar
            def _(act):
                def step(s, n, c, stream, t0):
                    act.wait_ge(x_loaded[s], (n + 1) * 16)
                    nc.scalar.activation(sq[:, :], xt[:, s, :], ACT.Square, accum_out=ss[:, s, 0:1]).then_inc(sq_done[s], 1)
                    act.wait_ge(mod_add[s], n + 1)
                    nc.scalar.activation(hsp[:, 0, :, bass.ds(t0, P)], hx[:, s, :, :], ACT.Copy).then_inc(hi_done[s], 1)
                chunks(act, step)

            @block.vector
            def _(dve):
                def step(s, n, c, stream, t0):
                    dve.wait_ge(sq_done[s], n + 1)
                    nc.vector.tensor_scalar(ss[:, s, 1:2], ss[:, s, 0:1], 1.0 / D, EPS, ALU.mult, ALU.add).then_inc(var_done[s], 1)
                    dve.wait_ge(rstd_done[s], n + 1)
                    nc.vector.tensor_scalar(xt[:, s, :], xt[:, s, :], ss[:, s, 2:3], None, ALU.mult).then_inc(scaled[s], 1)
                    dve.wait_ge(turned[s], n + 1)
                    wait(dve, lo_done[s], n)
                    nc.vector.tensor_tensor(hx[:, s, :, :], pt[s][:, :, :],
                                            modA[:, :, stream:stream + 1].broadcast_to([P, KT, P]), ALU.mult).then_inc(mod_mul[s], 1)
                    dve.wait_ge(mod_mul[s], n + 1)
                    nc.vector.tensor_tensor(hx[:, s, :, :], hx[:, s, :, :],
                                            modT[:, 0:KT, stream:stream + 1].broadcast_to([P, KT, P]), ALU.add).then_inc(mod_add[s], 1)
                    dve.wait_ge(hi_done[s], n + 1)
                    nc.vector.tensor_tensor(hsp[:, 1, :, bass.ds(t0, P)], hx[:, s, :, :],
                                            hsp[:, 0, :, bass.ds(t0, P)].bitcast(F32), ALU.subtract).then_inc(lo_done[s], 1)
                chunks(dve, step)

            @block.tensor
            def _(pe):
                def step(s, n, c, stream, t0):
                    pe.wait_ge(scaled[s], n + 1)
                    wait(pe, mod_mul[s], n)
                    for k in range(KT):
                        last = nc.tensor.transpose(pt[s][:, k, :], xt[:, s, k * P:(k + 1) * P], ident[:, :])
                    last.then_inc(turned[s], 1)
                chunks(pe, step)


NP = 4
SETS = 2


class Phase:

    def __init__(self, kind, w, cols, outs, gain=None, add=False):
        self.kind, self.w, self.cols, self.outs, self.gain, self.add = kind, w, cols, outs, gain, add
        self.iters = {"if": 1, "nat": H, "mg": KT // (2 * SETS)}.get(kind, KT // SETS)
        blocks = (NC + 1) // 2 if kind == "nat" else NB
        self.last = blocks - 1
        self.steps = [(e, b) for e in ((1,) if kind == "if" else (0, 1)) for b in range(blocks)]
        self.n_ready = 1 if kind in ("if", "oz", "uz") else 2
        self.n_sig = {"oz": 2, "uz": 1, "mg": 32}.get(kind, 0)
        self.n_part = {"oz": 1, "uz": 1}.get(kind, 0)
        self.n_stored = 16 if kind in ("if", "oz", "uz", "nat") else 32

    def columns(self, e, i):
        if self.kind == "if":
            at = [IF0, IF0 + P]
        elif self.kind == "nat":
            at = [self.cols[e] + DH * i, self.cols[e] + DH * i + P]
        elif self.kind == "mg":
            at = [(4 * i + 2 * e) * P, (4 * i + 2 * e + 1) * P]
        else:
            at = [c0 + (2 * i + e) * P for c0 in self.cols]
        return [self.w[:, bass.ds(a, P)] for a in at]


class Count:

    def __init__(self, base, per):
        self.base, self.per = base, per

    def at(self, i, more=0):
        return self.base + more + (self.per * i if self.per else 0)


class Step:
    def __init__(self, e, b, p, done, ready, sig, part, stored):
        self.e, self.b, self.p = e, b, p
        self.done, self.ready, self.sig, self.part, self.stored = done, ready, sig, part, stored


def plan(phases):
    names = ("done", "ready", "sig", "part", "stored")
    base = {n: [0] * NP for n in names}
    used = [0] * SETS
    out = []
    for ph in phases:
        def adds(n, b):
            return {"done": 0 if b == ph.last else 1, "ready": ph.n_ready, "sig": ph.n_sig,
                    "part": ph.n_part, "stored": ph.n_stored}[n]
        per = {n: [sum(adds(n, b) for _, b in ph.steps if b % NP == p) for p in range(NP)] for n in names}
        so_far = {n: [0] * NP for n in names}
        steps = []
        for e, b in ph.steps:
            p = b % NP
            steps.append(Step(e, b, p, *(Count(base[n][p] + so_far[n][p], per[n][p]) for n in names)))
            for n in names:
                so_far[n][p] += adds(n, b)
        out.append((ph, steps, list(used)))
        for n in names:
            for p in range(NP):
                base[n][p] += per[n][p] * ph.iters
        for e in {e for e, _ in ph.steps}:
            used[e] += ph.iters
    return out, base["stored"]


def streamed_products(nc, sem, sb, ps, tag, res, phases):
    planned, stored_total = plan(phases)
    raw_loaded = sem(f"{tag}_raw_loaded")
    w_hi = sem(f"{tag}_w_hi")
    w_all_lo = sem(f"{tag}_w_lo")
    w_used = [sem(f"{tag}_w_used{e}") for e in range(SETS)]
    blk_done = [sem(f"{tag}_blk_done{p}") for p in range(NP)]
    ready = [sem(f"{tag}_ready{p}") for p in range(NP)]
    sig = [sem(f"{tag}_sig{p}") for p in range(NP)]
    part = [sem(f"{tag}_part{p}") for p in range(NP)]
    stored = [sem(f"{tag}_stored{p}", software_dma=True) for p in range(NP)]
    starts_with_if = phases[0].kind == "if"

    with ExitStack() as st:
        raw = sb(st, f"{tag}_raw", [P, KT, 2 * P])
        wsp = sb(st, f"{tag}_wsp", [P, SETS, 2, KT, 2 * P], F32R)
        stage = sb(st, f"{tag}_stage", [P, NP, 2, 512])
        bank = [[ps(st, f"{tag}_ps{p}{s}", [P, 512]) for s in range(2)] for p in range(NP)]

        def walk(eng, body):
            for ph, steps, used in planned:
                if ph.iters == 1:
                    for s in steps:
                        body(ph, s, 0, used)
                else:
                    with eng.Fori(0, ph.iters) as i:
                        for s in steps:
                            body(ph, s, i, used)

        def wait_products(eng, ph, s, i, used):
            if s.b == ph.last:
                eng.wait_ge(w_used[s.e], used[s.e] + i + 1)
            else:
                eng.wait_ge(blk_done[s.p], s.done.at(i, 1))

        def look_ahead(ph, s, i, used, split):
            if s.b != 1:
                return
            if ph.kind == "if":
                split(0, used[0], 1)
            elif s.e == 0:
                split(1, used[1] + i, used[0] + used[1] + 2 * i + 1)
            else:
                split(0, used[0] + i + 1, used[0] + used[1] + 2 * i + 2)

        with nc.Block() as block:
            @block.sync
            def _(sp):
                def load(n, columns):
                    wait_alone(sp, w_all_lo, n)
                    for h, src in enumerate(columns):
                        sp.dma_start(raw[:, :, h * P:(h + 1) * P],
                                     src.rearrange("(k p) n -> p k n", p=P)).then_inc(raw_loaded, 16)
                first = phases[0]
                load(0, first.columns(1 if starts_with_if else 0, 0))
                for at, (ph, steps, used) in enumerate(planned):
                    follow = phases[at + 1] if at + 1 < len(phases) else ph
                    n = used[0] + used[1]
                    if ph.kind == "if":
                        load(1, follow.columns(0, 0))
                        continue
                    if ph.iters > 1:
                        with sp.Fori(0, ph.iters - 1) as i:
                            load(n + 2 * i + 1, ph.columns(1, i))
                            load(n + 2 * i + 2, ph.columns(0, i + 1))
                    i = ph.iters - 1
                    load(n + 2 * i + 1, ph.columns(1, i))
                    load(n + 2 * i + 2, follow.columns(0, 0))

            @block.scalar
            def _(act):
                def split(e, n, n_all):
                    act.wait_ge(raw_loaded, 32 * (n_all + 1))
                    wait(act, w_used[e], n)
                    nc.scalar.activation(wsp[:, e, 0, :, :], raw[:, :, :], ACT.Copy).then_inc(w_hi, 1)

                def body(ph, s, i, used):
                    look_ahead(ph, s, i, used, split)
                    r, kind = s.p, ph.kind
                    if kind == "if":
                        return
                    if kind == "mg":
                        wait(act, stored[r], s.stored.at(i))
                        t0, width = BLOCKS[s.b]
                        for h in range(2):
                            act.dma_start(stage[:, r, h, 0:width],
                                          ph.gain[bass.ds(4 * i + 2 * s.e + h, 1), :, t0:t0 + width]
                                          .rearrange("a p t -> p (a t)")).then_inc(sig[r], 16)
                        return
                    wait_products(act, ph, s, i, used)
                    wait(act, stored[r], s.stored.at(i))
                    width = DH if kind == "nat" else BLOCKS[s.b][1]
                    A, B = (bank[r][h][:, 0:width] for h in range(2))
                    s0, s1 = (stage[:, r, h, 0:width] for h in range(2))
                    if kind == "nat":
                        alone = s.b == ph.last
                        nc.scalar.activation(s0, A, ACT.Copy).then_inc(ready[r], 2 if alone else 1)
                    elif kind == "qk":
                        nc.scalar.activation(s0, A, ACT.Copy, scale=DH ** -0.5).then_inc(ready[r], 1)
                    elif kind == "gg":
                        nc.scalar.activation(s0, A, ACT.Sigmoid).then_inc(ready[r], 1)
                        nc.scalar.activation(s1, B, ACT.Sigmoid).then_inc(ready[r], 1)
                    elif kind == "oz":
                        nc.scalar.activation(s0, A, ACT.Sigmoid).then_inc(sig[r], 1)
                        nc.scalar.activation(s1, B, ACT.Sigmoid).then_inc(sig[r], 1)
                    else:
                        nc.scalar.activation(s1, B, ACT.Sigmoid).then_inc(sig[r], 1)
                split(1 if starts_with_if else 0, 0, 0)
                walk(act, body)

            @block.vector
            def _(dve):
                def split(e, n, n_all):
                    dve.wait_ge(w_hi, n_all + 1)
                    nc.vector.tensor_tensor(wsp[:, e, 1, :, :], raw[:, :, :],
                                            wsp[:, e, 0, :, :].bitcast(F32), ALU.subtract).then_inc(w_all_lo, 1)

                def body(ph, s, i, used):
                    look_ahead(ph, s, i, used, split)
                    r, kind = s.p, ph.kind
                    width = DH if kind == "nat" else BLOCKS[s.b][1]
                    A, B = (bank[r][h][:, 0:width] for h in range(2))
                    s0, s1 = (stage[:, r, h, 0:width] for h in range(2))
                    if kind == "if":
                        wait_products(dve, ph, s, i, used)
                        wait(dve, stored[r], s.stored.at(i))
                        nc.vector.tensor_copy(stage[0:N_IF, r, 0, 0:width], bank[r][0][0:N_IF, 0:width]
                                              ).then_inc(ready[r], 1)
                    elif kind == "qk" or kind == "nat":
                        if kind == "nat" and s.b == ph.last:
                            return
                        wait_products(dve, ph, s, i, used)
                        wait(dve, stored[r], s.stored.at(i))
                        nc.vector.tensor_copy(s1, B).then_inc(ready[r], 1)
                    elif kind == "oz":
                        dve.wait_ge(sig[r], s.sig.at(i, 2))
                        nc.vector.tensor_tensor(s1, s1, B, ALU.mult).then_inc(part[r], 1)
                        dve.wait_ge(part[r], s.part.at(i, 1))
                        nc.vector.tensor_tensor(s0, s0, s1, ALU.mult).then_inc(ready[r], 1)
                    elif kind == "uz":
                        dve.wait_ge(sig[r], s.sig.at(i, 1))
                        nc.vector.tensor_tensor(s1, s1, B, ALU.mult).then_inc(part[r], 1)
                        dve.wait_ge(part[r], s.part.at(i, 1))
                        nc.vector.tensor_tensor(s0, s1, A, ALU.mult).then_inc(ready[r], 1)
                    elif kind == "mg":
                        dve.wait_ge(sig[r], s.sig.at(i, 32))
                        wait_products(dve, ph, s, i, used)
                        nc.vector.tensor_tensor(s0, s0, A, ALU.mult).then_inc(ready[r], 1)
                        nc.vector.tensor_tensor(s1, s1, B, ALU.mult).then_inc(ready[r], 1)
                split(1 if starts_with_if else 0, 0, 0)
                walk(dve, body)

            @block.tensor
            def _(pe):
                def body(ph, s, i, used):
                    if s.b == 0:
                        loads = (0 if ph.kind == "if" else used[0] + used[1] + 2 * i + s.e)
                        pe.wait_ge(w_all_lo, loads + 1)
                    wait(pe, ready[s.p], s.ready.at(i))
                    for h in range(1 if ph.kind == "if" else 2):
                        if ph.kind == "nat" and 2 * s.b + h >= NC:
                            continue
                        for k in range(KT):
                            for j, (wp, rp) in enumerate(((1, 0), (0, 1), (0, 0))):
                                flags = dict(start=(k == 0 and j == 0), stop=(k == KT - 1 and j == 2))
                                if ph.kind == "nat":
                                    t0 = (2 * s.b + h) * P
                                    last = nc.tensor.matmul(bank[s.p][h][:, 0:DH], res[:, rp, k, t0:t0 + P],
                                                            wsp[:, s.e, wp, k, :], **flags)
                                else:
                                    t0, width = BLOCKS[s.b]
                                    last = nc.tensor.matmul(bank[s.p][h][:, 0:width],
                                                            wsp[:, s.e, wp, k, h * P:(h + 1) * P],
                                                            res[:, rp, k, t0:t0 + width], **flags)
                    last.then_inc(w_used[s.e] if s.b == ph.last else blk_done[s.p], 1)
                walk(pe, body)

            @block.gpsimd
            def _(pool):
                def body(ph, s, i, used):
                    r, kind = s.p, ph.kind
                    wait_alone(pool, ready[r], s.ready.at(i, ph.n_ready))
                    if kind == "if":
                        t0, width = BLOCKS[s.b]
                        pool.dma_start(ph.outs[0][:, t0:t0 + width], stage[0:N_IF, r, 0, 0:width]
                                       ).then_inc(stored[r], 16)
                    elif kind == "nat":
                        n = min(2, NC - 2 * s.b)
                        pool.dma_start(ph.outs[s.e][2 * s.b * P:(2 * s.b + n) * P, bass.ds(DH * i, DH)]
                                       .rearrange("(c p) n -> p c n", p=P),
                                       stage[:, r, 0:n, 0:DH]).then_inc(stored[r], 16)
                    else:
                        t0, width = BLOCKS[s.b]
                        for h in range(ph.n_stored // 16):
                            out = ph.outs[0] if kind == "mg" else ph.outs[h]
                            tile = 4 * i + 2 * s.e + h if kind == "mg" else 2 * i + s.e
                            more = dict(accum_op=ALU.add) if ph.add else {}
                            pool.dma_start(out[bass.ds(tile, 1), :, t0:t0 + width].rearrange("a p t -> p (a t)"),
                                           stage[:, r, h, 0:width], **more).then_inc(stored[r], 16)
                walk(pool, body)
                for p in range(NP):
                    pool.wait_ge(stored[p], stored_total[p])


def gate_phase(nc, sem, sb, ps, if_d, b_if, state_m, cols_d, r_d, sp_d, new_m, ident, cols, spb):
    loaded = sem("g_loaded")
    chain = sem("g_chain")
    const_rows = sem("g_const")
    stored = sem("g_stored")
    back = sem("g_back")
    turned = sem("g_turned")
    taken = sem("g_taken")
    dsts = []
    with ExitStack() as st:
        li = sb(st, "g_li", [H, TOK])
        lf = sb(st, "g_lf", [H, TOK])
        t1 = sb(st, "g_t1", [H, TOK])
        keep = sb(st, "g_keep", [H, 2, NC, P])
        outs = [[sb(st, f"g_{n}{d}", [H, TOK]) for n in ("u", "sc", "em", "r")] for d in range(2)]
        m = sb(st, "g_m", [H, TOK])
        b = sb(st, "g_b", [H, TOK])
        ms = sb(st, "g_ms", [H, NC])
        spr = [sb(st, f"g_sp{d}", [H, NC]) for d in range(2)]
        bias = sb(st, "g_bias", [H, 2, 2])
        m0 = sb(st, "g_m0", [H, 2])
        mctx = sb(st, "g_mctx", [H, 2])
        rows = sb(st, "g_rows", [6 * H, TOK])
        pt = [ps(st, f"g_pt{s}", [P, 6 * H]) for s in range(2)]
        n_steps = 15
        per_dir_loads = 32

        def ch(x):
            return x.rearrange("h (c t) -> h c t", t=P)

        with nc.Block() as block:
            @block.gpsimd
            def _(pool):
                nc.gpsimd.memset(keep[:, :, :, :], 1.0).then_inc(const_rows, 1)
                pool.wait_ge(const_rows, 1)
                nc.gpsimd.memset(keep[:, 0, :, 0:1], 0.0).then_inc(const_rows, 1)
                nc.gpsimd.memset(keep[:, 1, :, P - 1:P], 0.0).then_inc(const_rows, 1)

            @block.sync
            def _(sp):
                with nc.allow_non_contiguous_dma("small vectors"):
                    sp.dma_start(bias[:, :, :], b_if[0].rearrange("d g h -> h d g")).then_inc(loaded, 16)
                    sp.dma_start(m0[:, :], state_m[0, 0].rearrange("d h -> h d")).then_inc(loaded, 16)
                for d in range(2):
                    if d:
                        sp.wait_ge(chain, n_steps)
                    sp.dma_start(li[:, :], if_d[2 * H * d:2 * H * d + H, :]).then_inc(loaded, 16)
                    sp.dma_start(lf[:, :], if_d[2 * H * d + H:2 * H * (d + 1), :]).then_inc(loaded, 16)
                for d in range(2):
                    sp.wait_ge(chain, n_steps * (d + 1))
                    for q in range(3):
                        sp.dma_start(cols_d[(2 * q + d) * H:(2 * q + d + 1) * H, :], outs[d][q][:, :]).then_inc(stored, 16)
                    sp.dma_start(r_d[d * H:(d + 1) * H, :], outs[d][3][:, :]).then_inc(stored, 16)
                    sp.dma_start(sp_d[d * H:(d + 1) * H, :], spr[d][:, :]).then_inc(stored, 16)
                with nc.allow_non_contiguous_dma("small vectors"):
                    sp.dma_start(new_m[0, 0].rearrange("d h -> h d"), mctx[:, :]).then_inc(stored, 16)
                sp.wait_ge(stored, 11 * 16)
                sp.dma_start(rows[:, :], cols_d).then_inc(back, 16)
                sp.dma_start(spb[:, :, :], sp_d.rearrange("(a d) c -> a d c", a=1).broadcast_to([P, 2 * H, NC])
                             ).then_inc(back, 16)
                sp.wait_ge(back, 32)

            @block.tensor
            def _(pe):
                pe.wait_ge(back, 32)
                for c in range(NC):
                    if c >= 2:
                        pe.wait_ge(taken, c - 1)
                    nc.tensor.transpose(pt[c % 2][:, :], rows[:, c * P:(c + 1) * P],
                                        ident[0:6 * H, 0:6 * H]).then_inc(turned, 1)

            def step_list(d):
                pass
            @block.scalar
            def _(act):
                for d in range(2):
                    n0 = n_steps * d
                    act.wait_ge(chain, n0 + 3)
                    nc.scalar.activation(t1[:, :], t1[:, :], ACT.Exp, scale=-1.0).then_inc(chain, 1)
                    act.wait_ge(chain, n0 + 4)
                    nc.scalar.activation(t1[:, :], t1[:, :], ACT.Ln, bias=1.0).then_inc(chain, 1)
                    act.wait_ge(chain, n0 + 12)
                    nc.scalar.activation(outs[d][1][:, :], outs[d][1][:, :], ACT.Exp).then_inc(chain, 1)
                    act.wait_ge(chain, n0 + 13)
                    nc.scalar.activation(outs[d][2][:, :], m[:, :], ACT.Exp, scale=-1.0).then_inc(chain, 1)

            @block.vector
            def _(dve):
                dve.wait_ge(const_rows, 3)
                for d in range(2):
                    n0 = n_steps * d
                    u, sc, em, r = outs[d]
                    bf, bi = bias[:, d, 1:2], bias[:, d, 0:1]

                    def rev(x):
                        return x[:, ::-1] if d else x
                    lat, ctx = slice(CTX * P, TOK), slice(0, CTX * P)
                    dve.wait_ge(loaded, 32 + 32 * (d + 1))
                    nc.vector.tensor_scalar(lf[:, :], lf[:, :], bf, None, ALU.add).then_inc(chain, 1)
                    dve.wait_ge(chain, n0 + 1)
                    nc.vector.tensor_scalar(li[:, :], li[:, :], bi, None, ALU.add).then_inc(chain, 1)
                    nc.vector.scalar_tensor_tensor(out=t1[:, :], in0=lf[:, :], scalar=-1.0, in1=lf[:, :],
                                                   op0=ALU.mult, op1=ALU.max).then_inc(chain, 1)
                    dve.wait_ge(chain, n0 + 5)
                    nc.vector.scalar_tensor_tensor(out=lf[:, :], in0=lf[:, :], scalar=0.0, in1=t1[:, :],
                                                   op0=ALU.min, op1=ALU.subtract).then_inc(chain, 1)
                    dve.wait_ge(chain, n0 + 6)
                    nc.vector.tensor_tensor_scan(rev(b[:, :]), rev(keep[:, d, :, :].rearrange("h c t -> h (c t)")),
                                                 rev(lf[:, :]), 0.0, ALU.mult, ALU.add).then_inc(chain, 1)
                    nc.vector.tensor_tensor_scan(rev(m[:, ctx]), rev(lf[:, ctx]), rev(li[:, ctx]), 0.0,
                                                 ALU.add, ALU.max).then_inc(chain, 1)
                    nc.vector.tensor_tensor_scan(rev(m[:, lat]), rev(lf[:, lat]), rev(li[:, lat]), m0[:, d:d + 1],
                                                 ALU.add, ALU.max).then_inc(chain, 1)
                    dve.wait_ge(chain, n0 + 9)
                    end = 0 if d else P - 1
                    firsts, rest, before = ((CTX + LAT - 1, slice(CTX, NC - 1), slice(CTX + 1, NC)) if d else
                                            (CTX, slice(CTX + 1, NC), slice(CTX, NC - 1)))
                    nc.vector.memset(ms[:, 0:CTX], 0.0)
                    nc.vector.tensor_copy(ms[:, firsts:firsts + 1], m0[:, d:d + 1])
                    nc.vector.tensor_copy(ms[:, rest], ch(m[:, :])[:, before, end])
                    nc.vector.tensor_copy(mctx[:, d:d + 1], m[:, end:end + 1])
                    nc.vector.tensor_tensor(u[:, :], li[:, :], b[:, :], ALU.subtract)
                    nc.vector.tensor_tensor(r[:, :], b[:, :], m[:, :], ALU.subtract).then_inc(chain, 2)
                    dve.wait_ge(chain, n0 + 11)
                    nc.vector.tensor_tensor(ch(sc[:, :]), ch(r[:, :]), ms[:, :].unsqueeze(2).broadcast_to([H, NC, P]),
                                            ALU.add).then_inc(chain, 1)
                    dve.wait_ge(chain, n0 + 14)
                    nc.vector.tensor_copy(spr[d][:, :], ch(sc[:, :])[:, :, end]).then_inc(chain, 1)
                    dve.wait_ge(chain, n0 + 15)
                for c in range(NC):
                    dve.wait_ge(turned, c + 1)
                    nc.vector.tensor_copy(cols[:, c, :], pt[c % 2][:, :]).then_inc(taken, 1)


def sgu_phase(nc, sem, sb, ps, vb_d, u_d, w_s, b_s, g_sgu, ident, ysp):
    def two(name):
        return [sem(f"s_{name}{s}") for s in range(2)]
    half_made = sem("s_half_made")
    const_loaded, w_turned, w_taken = sem("s_const"), sem("s_w_turned"), sem("s_w_taken")
    v_loaded, u_loaded, sq_done, var_done, rstd_done, v_scaled, mixed, mix_read, biased, gated, hi_done, lo_done = (
        two(n) for n in ("v_loaded", "u_loaded", "sq_done", "var_done", "rstd_done", "v_scaled", "mixed",
                         "mix_read", "biased", "gated", "hi_done", "lo_done"))
    with ExitStack() as st:
        ws = sb(st, "s_ws", [P, H, P])
        wsT = sb(st, "s_wsT", [P, H, P])
        bsb = sb(st, "s_bsb", [P, H, P])
        gcol = sb(st, "s_gcol", [P, KT])
        vt = sb(st, "s_vt", [P, 2, D])
        ut = sb(st, "s_ut", [P, 2, KT, P])
        sq = sb(st, "s_sq", [P, D])
        ss = sb(st, "s_ss", [P, 2, 4])
        yt = sb(st, "s_yt", [P, 2, KT, P])
        pm = [ps(st, f"s_pm{s}", [P, KT, P]) for s in range(2)]
        pw = ps(st, "s_pw", [P, H, P])

        def chunks(eng, step):
            step(0, 0, 0)
            with eng.Fori(0, (NC - 1) // 2) as i:
                step(1, i, 2 * i + 1)
                step(0, i + 1, 2 * i + 2)

        with nc.Block() as block:
            @block.sync
            def _(sp):
                sp.dma_start(ws[:, :, :], w_s[0].rearrange("g t s -> t g s")).then_inc(const_loaded, 16)
                sp.dma_start(bsb[:, :, :], b_s[0].rearrange("(a g) t -> a g t", a=1).broadcast_to([P, H, P])
                             ).then_inc(const_loaded, 16)
                with nc.allow_non_contiguous_dma("vector onto partitions"):
                    sp.dma_start(gcol[:, :], g_sgu[0].rearrange("(k p) -> p k", p=P)).then_inc(const_loaded, 16)

                def step(s, n, c):
                    wait_alone(sp, mixed[s], n)
                    sp.dma_start(vt[:, s, :], vb_d[bass.ds(c * P, P), :]).then_inc(v_loaded[s], 16)
                    wait_alone(sp, gated[s], n)
                    sp.dma_start(ut[:, s, :, :], u_d[:, :, bass.ds(c * P, P)].rearrange("k p t -> p k t")
                                 ).then_inc(u_loaded[s], 16)
                chunks(sp, step)

            @block.gpsimd
            def _(pool):
                def step(s, n, c):
                    wait_alone(pool, var_done[s], n + 1)
                    nc.gpsimd.tensor_tensor(ss[:, s, 2:3], ss[:, s, 1:2], ss[:, s, 3:4], ALU.pow).then_inc(rstd_done[s], 1)
                nc.gpsimd.memset(ss[:, :, 3:4], -0.5).then_inc(half_made, 1)
                pool.wait_ge(half_made, 1)
                chunks(pool, step)

            @block.scalar
            def _(act):
                def step(s, n, c):
                    act.wait_ge(v_loaded[s], 16 * n + 16)
                    nc.scalar.activation(sq[:, :], vt[:, s, :], ACT.Square, accum_out=ss[:, s, 0:1]).then_inc(sq_done[s], 1)
                    act.wait_ge(rstd_done[s], n + 1)
                    nc.scalar.activation(vt[:, s, :], vt[:, s, :], ACT.Copy, scale=ss[:, s, 2:3]).then_inc(v_scaled[s], 1)
                    act.wait_ge(gated[s], n + 1)
                    nc.scalar.activation(ysp[:, 0, :, bass.ds(c * P, P)], yt[:, s, :, :], ACT.Copy).then_inc(hi_done[s], 1)
                chunks(act, step)

            @block.tensor
            def _(pe):
                pe.wait_ge(const_loaded, 48)
                for g in range(H):
                    last = nc.tensor.transpose(pw[:, g, :], ws[:, g, :], ident[:, :])
                last.then_inc(w_turned, 1)
                pe.wait_ge(w_taken, 1)

                def step(s, n, c):
                    pe.wait_ge(v_scaled[s], n + 1)
                    wait(pe, mix_read[s], n)
                    for k in range(KT):
                        last = nc.tensor.matmul(pm[s][:, k, :], vt[:, s, k * P:(k + 1) * P], wsT[:, k // HT, :],
                                                start=True, stop=True)
                    last.then_inc(mixed[s], 1)
                chunks(pe, step)

            @block.vector
            def _(dve):
                dve.wait_ge(w_turned, 1)
                nc.vector.tensor_copy(wsT[:, :, :], pw[:, :, :]).then_inc(w_taken, 1)

                def step(s, n, c):
                    dve.wait_ge(sq_done[s], n + 1)
                    nc.vector.tensor_scalar(ss[:, s, 1:2], ss[:, s, 0:1], 1.0 / D, EPS, ALU.mult, ALU.add).then_inc(var_done[s], 1)
                    dve.wait_ge(mixed[s], n + 1)
                    wait(dve, lo_done[s], n)
                    for k in range(KT):
                        last = nc.vector.scalar_tensor_tensor(out=yt[:, s, k, :], in0=pm[s][:, k, :], scalar=gcol[:, k:k + 1],
                                                              in1=bsb[:, k // HT, :], op0=ALU.mult, op1=ALU.add)
                    last.then_inc(mix_read[s], 1)
                    dve.wait_ge(mix_read[s], n + 1)
                    dve.wait_ge(u_loaded[s], 16 * n + 16)
                    nc.vector.tensor_tensor(yt[:, s, :, :], yt[:, s, :, :], ut[:, s, :, :], ALU.mult).then_inc(gated[s], 1)
                    dve.wait_ge(hi_done[s], n + 1)
                    nc.vector.tensor_tensor(ysp[:, 1, :, bass.ds(c * P, P)], yt[:, s, :, :],
                                            ysp[:, 0, :, bass.ds(c * P, P)].bitcast(F32), ALU.subtract).then_inc(lo_done[s], 1)
                chunks(dve, step)


def mlstm_phase(nc, sem, sb, ps, qT_d, kT_d, v_d, gate_d, r_d, state_C, state_n, new_C, new_n,
                ident, mask, cols, spb, ysp):
    def per(name, n=2):
        return [sem(f"m_{name}{d}") for d in range(n)]
    SL = 3
    in_loaded = [[sem(f"m_in_loaded{d}{s}") for s in range(SL)] for d in range(2)]
    g_loaded = per("g_loaded")
    st_loaded, st_turned, st_taken = sem("m_st_loaded"), sem("m_st_turned"), sem("m_st_taken")
    ones_made = sem("m_ones")
    sk_done, s_read, arg_done, e_done, p_done, ke_done = (per(n) for n in (
        "sk_done", "s_read", "arg_done", "e_done", "p_done", "ke_done"))
    inter_done, inter_read, intra_done, x_done, den_done, rec_done = (per(n) for n in (
        "inter_done", "inter_read", "intra_done", "x_done", "den_done", "rec_done"))
    c_done = [[sem(f"m_c_done{d}{s}") for s in range(SL)] for d in range(2)]
    neg_done, c_updated, h_done, hT_done, y_done, hi_done, lo_done = (per(n) for n in (
        "neg_done", "c_updated", "h_done", "hT_done", "y_done", "hi_done", "lo_done"))
    ctx_c_taken, ctx_stored = sem("m_ctx_c_taken"), sem("m_ctx_stored", software_dma=True)
    STEPS = NC
    HALF = LAT // 2

    with ExitStack() as st:
        qt = sb(st, "m_qt", [P, 2, SL, HT, P])
        kt = sb(st, "m_kt", [P, 2, SL, HT, P])
        vt = sb(st, "m_vt", [P, 2, SL, DE])
        rt = sb(st, "m_rt", [P, 2, SL, P])
        gt = sb(st, "m_gt", [P, 2, HT, P])
        pr = sb(st, "m_pr", [P, 2, P])
        ke = sb(st, "m_ke", [P, 2, DH])
        it = sb(st, "m_it", [P, 2, DE])
        xt = sb(st, "m_xt", [P, 2, DE])
        dn = sb(st, "m_dn", [P, 2, 2])
        yt = sb(st, "m_yt", [P, 2, HT, P])
        cc = sb(st, "m_cc", [P, HT, DE])
        hst = sb(st, "m_hst", [P, NC, DH])
        C = sb(st, "m_C", [P, 2 * H, HT, DE])
        psk = [ps(st, f"m_psk{d}", [P, 3, P]) for d in range(2)]
        pin = [ps(st, f"m_pin{d}", [P, DE]) for d in range(2)]
        pnu = [ps(st, f"m_pnu{d}", [P, DE]) for d in range(2)]
        pc = ps(st, "m_pc", [P, 2, 512])

        raw = hst[:, 0:2 * HT, :].rearrange("p (j a) k -> p j a k", a=HT)
        if True:
            with nc.Block() as block:
                @block.sync
                def _(sp):
                    with nc.allow_non_contiguous_dma("normalisers"):
                        for j in range(2 * H):
                            d, h = j // H, j % H
                            sp.dma_start(C[:, j, :, DH], state_n[0, 0, d, h].rearrange("(a p) -> p a", p=P)
                                         ).then_inc(ones_made, 16)
                    for j in range(2 * H):
                        if j >= 2:
                            sp.wait_ge(st_turned, j - 1)
                        sp.dma_start(raw[:, j % 2, :, :], state_C[0, 0, j // H, j % H].rearrange("(a p) k -> p a k", p=P)
                                     ).then_inc(in_loaded[0][j % 2], 16)

                    sp.wait_ge(ones_made, 2 * H * 16)

                @block.gpsimd
                def _(pool):
                    nc.gpsimd.memset(vt[:, :, :, DH:DE], 1.0).then_inc(st_loaded, 1)
                    wait_alone(pool, st_loaded, 1)

                @block.tensor
                def _(pe):
                    for j in range(2 * H):
                        pe.wait_ge(in_loaded[0][j % 2], 16 * (j // 2 + 1))
                        if j >= 2:
                            pe.wait_ge(st_taken, j - 1)
                        for a in range(HT):
                            for b in range(HT):
                                last = nc.tensor.transpose(pc[:, j % 2, b * DH + a * P:b * DH + (a + 1) * P],
                                                           raw[:, j % 2, a, b * P:(b + 1) * P], ident[:, :])
                        last.then_inc(st_turned, 1)

                @block.vector
                def _(dve):
                    for j in range(2 * H):
                        dve.wait_ge(st_turned, j + 1)
                        nc.vector.tensor_copy(C[:, j, :, 0:DH], pc[:, j % 2, :].rearrange("p (b v) -> p b v", b=HT)
                                              ).then_inc(st_taken, 1)
        def head_walk(eng, ctx_step, lat_pair):
            with eng.Fori(0, H) as h:
                ctx_step(h)
                for half in range(2):
                    with eng.Fori(half * (HALF // 2), (half + 1) * (HALF // 2)) as i:
                        lat_pair(h, i, half)

        class Where:
            def __init__(self, d, h, i, sub, half):
                self.d, self.h = d, h
                if sub is None:
                    self.s, self.uses, self.n, self.l, self.c = 2, h, h * STEPS, h * LAT, 0
                    self.f = h * (HALF + d)
                    self.join, self.ctx = d == 1, True
                else:
                    self.s, self.uses = sub, h * HALF + i
                    self.l = h * LAT + 2 * i + sub
                    self.n = h * STEPS + 1 + 2 * i + sub
                    self.c = CTX + 2 * i + sub if d == 0 else NC - 1 - 2 * i - sub
                    self.join, self.ctx = half == 1, False
                    self.f = h * (HALF + d) + d + (2 * i + sub - HALF if half else 0)

        def walk(eng, stages):
            def ctx_step(h):
                for f in stages:
                    for d in range(2):
                        f(Where(d, h, 0, None, 0))

            def lat_pair(h, i, half):
                for sub in range(2):
                    for f in stages:
                        for d in range(2):
                            f(Where(d, h, i, sub, half))
            head_walk(eng, ctx_step, lat_pair)

        with nc.Block() as block:
            @block.sync
            def _(sp):
                def load(w):
                    d, s, c, h = w.d, w.s, w.c, w.h
                    wait_alone(sp, c_done[d][s], w.uses)
                    base = [(qt[:, d, s, :, :], qT_d[bass.ds(HT * h, HT), :, bass.ds(c * P, P)].rearrange("a p t -> p a t")),
                            (kt[:, d, s, :, :], kT_d[bass.ds(HT * h, HT), :, bass.ds(c * P, P)].rearrange("a p t -> p a t")),
                            (vt[:, d, s, 0:DH], v_d[bass.ds(c * P, P), bass.ds(h * DH, DH)]),
                            (rt[:, d, s, :], r_d[bass.ds(H * d + h, 1), bass.ds(c * P, P)].broadcast_to([P, P]))]
                    for dst, src in base:
                        sp.dma_start(dst, src).then_inc(in_loaded[d][s], 16)
                    if w.join:
                        wait_alone(sp, y_done[d], w.f)
                        sp.dma_start(gt[:, d, :, :], gate_d[bass.ds(HT * h, HT), :, bass.ds(c * P, P)].rearrange("a p t -> p a t")
                                     ).then_inc(g_loaded[d], 16)
                walk(sp, [load])

            def loaded(eng, w):
                base = 16 * H if w.d == 0 and not w.ctx else 0
                eng.wait_ge(in_loaded[w.d][w.s], base + 64 * w.uses + 64)

            @block.tensor
            def _(pe):
                def front(w):
                    d, s = w.d, w.s
                    loaded(pe, w)
                    wait(pe, ke_done[d], w.n)
                    for a in range(HT):
                        nc.tensor.matmul(psk[d][:, 0, :], kt[:, d, s, a, :], qt[:, d, s, a, :], start=(a == 0), stop=(a == HT - 1))
                    for a in range(HT):
                        last = nc.tensor.transpose(psk[d][:, 1 + a, :], kt[:, d, s, a, :], ident[:, :])
                    last.then_inc(sk_done[d], 1)
                    if not w.ctx:
                        wait(pe, c_updated[d], w.l)
                        wait(pe, inter_read[d], w.l)
                        for a in range(HT):
                            last = nc.tensor.matmul(pin[d][:, :], qt[:, d, s, a, :],
                                                    C[:, bass.ds(H * d + w.h, 1), a, :].rearrange("p a n -> p (a n)"),
                                                    start=(a == 0), stop=(a == HT - 1))
                        last.then_inc(inter_done[d], 1)

                def middle(w):
                    d, s = w.d, w.s
                    pe.wait_ge(p_done[d], w.n + 1)
                    wait(pe, x_done[d], w.n)
                    wait(pe, y_done[d], w.f)
                    nc.tensor.matmul(pnu[d][:, :], pr[:, d, :], vt[:, d, s, :], start=True, stop=True).then_inc(intra_done[d], 1)
                    pe.wait_ge(ke_done[d], w.n + 1)
                    if w.ctx and d == 0:
                        wait(pe, c_updated[1], w.l)
                    elif w.ctx:
                        pe.wait_ge(ctx_c_taken, 2 * w.h + 1)
                    elif d == 0:
                        pe.wait_ge(ctx_c_taken, 2 * w.h + 2)
                        wait(pe, c_updated[1], w.l)
                    else:
                        pe.wait_ge(c_updated[0], w.l + 1)
                    for a in range(HT):
                        if w.ctx:
                            nc.tensor.matmul(pc[:, a, 0:DH], vt[:, d, s, a * P:(a + 1) * P], ke[:, d, :], start=True, stop=True)
                            last = nc.tensor.matmul(pc[:, a, DH:DE], ke[:, d, a * P:(a + 1) * P], vt[:, d, s, DH:DE],
                                                    start=True, stop=True)
                        else:
                            last = nc.tensor.matmul(pc[:, a, 0:DE], ke[:, d, a * P:(a + 1) * P], vt[:, d, s, :],
                                                    start=True, stop=True)
                    last.then_inc(c_done[d][s], 1)

                def back(w):
                    d = w.d
                    if w.join:
                        pe.wait_ge(h_done[d], w.n + 1)
                        for a in range(HT):
                            last = nc.tensor.transpose(pnu[d][:, a * P:(a + 1) * P], xt[:, d, a * P:(a + 1) * P], ident[:, :])
                        last.then_inc(hT_done[d], 1)
                walk(pe, [front, middle, back])

            def col(w, q):
                return cols[:, bass.ds(w.c, 1), bass.ds((2 * q + w.d) * H + w.h, 1)].rearrange("p a b -> p (a b)")

            @block.vector
            def _(dve):
                def args(w):
                    d, s = w.d, w.s
                    loaded(dve, w)
                    dve.sem_inc(passed[-1], 1)
                    nc.vector.scalar_tensor_tensor(out=rt[:, d, s, :], in0=rt[:, d, s, :], scalar=col(w, 0), in1=mask[:, d, :],
                                                   op0=ALU.add, op1=ALU.add).then_inc(arg_done[d], 1)

                def probs(w):
                    d = w.d
                    dve.wait_ge(sk_done[d], w.n + 1)
                    dve.wait_ge(e_done[d], w.n + 1)
                    wait(dve, intra_done[d], w.n)
                    nc.vector.tensor_tensor(pr[:, d, :], psk[d][:, 0, :], rt[:, d, w.s, :], ALU.mult).then_inc(p_done[d], 1)

                def update(w):
                    d = w.d
                    dve.wait_ge(c_done[d][w.s], w.uses + 1)
                    if w.ctx:
                        if d == 0:
                            wait(dve, ctx_stored, 64 * w.h)
                        else:
                            dve.wait_ge(ctx_stored, 64 * w.h + 32)
                        nc.vector.tensor_copy(cc[:, :, :], pc[:, :, 0:DE]).then_inc(ctx_c_taken, 1)
                    else:
                        dve.wait_ge(inter_done[d], w.l + 1)
                        Cs = C[:, bass.ds(H * d + w.h, 1), :, :].rearrange("p a b n -> p (a b) n")
                        nc.vector.scalar_tensor_tensor(out=Cs, in0=Cs,
                                                       scalar=spb[:, bass.ds(H * d + w.h, 1), bass.ds(w.c, 1)].rearrange("p a b -> p (a b)"),
                                                       in1=pc[:, :, 0:DE], op0=ALU.mult, op1=ALU.add).then_inc(c_updated[d], 1)

                def num(w):
                    d = w.d
                    dve.wait_ge(intra_done[d], w.n + 1)
                    if w.ctx:
                        nc.vector.tensor_copy(xt[:, d, :], pnu[d][:, :]).then_inc(x_done[d], 1)
                    else:
                        dve.wait_ge(inter_read[d], w.l + 1)
                        nc.vector.tensor_tensor(xt[:, d, :], pnu[d][:, :], it[:, d, :], ALU.add).then_inc(x_done[d], 1)
                    dve.wait_ge(x_done[d], w.n + 1)
                    nc.vector.scalar_tensor_tensor(out=dn[:, d, 1:2], in0=xt[:, d, DH:DE], scalar=-1.0, in1=col(w, 2),
                                                   op0=ALU.mult, op1=ALU.max).then_inc(neg_done[d], 1)
                    dve.wait_ge(neg_done[d], w.n + 1)
                    nc.vector.tensor_tensor(dn[:, d, 0:1], dn[:, d, 1:2], xt[:, d, DH:DE], ALU.max).then_inc(den_done[d], 1)
                    dve.wait_ge(den_done[d], w.n + 1)
                    nc.vector.reciprocal(dn[:, d, 1:2], dn[:, d, 0:1]).then_inc(rec_done[d], 1)

                def out(w):
                    d = w.d
                    dve.wait_ge(rec_done[d], w.n + 1)
                    mine = hst[:, bass.ds(w.c, 1), :].rearrange("p a n -> p (a n)")
                    if w.join:
                        if w.ctx:
                            dve.wait_ge(h_done[0], w.h * STEPS + 1)
                        else:
                            dve.wait_ge(h_done[1 - d], w.h * STEPS + 1 + HALF)
                        nc.vector.scalar_tensor_tensor(out=xt[:, d, 0:DH], in0=xt[:, d, 0:DH], scalar=dn[:, d, 1:2], in1=mine,
                                                       op0=ALU.mult, op1=ALU.add).then_inc(h_done[d], 1)
                    else:
                        nc.vector.tensor_scalar(mine, xt[:, d, 0:DH], dn[:, d, 1:2], None, ALU.mult).then_inc(h_done[d], 1)

                def gated(w):
                    d = w.d
                    if w.join:
                        dve.wait_ge(hT_done[d], w.f + 1)
                        dve.wait_ge(g_loaded[d], 16 * w.f + 16)
                        wait(dve, lo_done[d], w.f)
                        nc.vector.tensor_tensor(yt[:, d, :, :], pnu[d][:, 0:DH].rearrange("p (a t) -> p a t", a=HT),
                                                gt[:, d, :, :], ALU.mult).then_inc(y_done[d], 1)

                def low(w):
                    d = w.d
                    if w.join:
                        dve.wait_ge(hi_done[d], w.f + 1)
                        nc.vector.tensor_tensor(ysp[:, 1, bass.ds(HT * w.h, HT), bass.ds(w.c * P, P)], yt[:, d, :, :],
                                                ysp[:, 0, bass.ds(HT * w.h, HT), bass.ds(w.c * P, P)].bitcast(F32),
                                                ALU.subtract).then_inc(lo_done[d], 1)
                walk(dve, [args, probs, update, num, out, gated, low])

            @block.scalar
            def _(act):
                def exps(w):
                    d = w.d
                    act.wait_ge(arg_done[d], w.n + 1)
                    nc.scalar.activation(rt[:, d, w.s, :], rt[:, d, w.s, :], ACT.Exp).then_inc(e_done[d], 1)

                def inter(w):
                    d = w.d
                    if not w.ctx:
                        act.wait_ge(inter_done[d], w.l + 1)
                        wait(act, x_done[d], w.n)
                        nc.scalar.activation(it[:, d, :], pin[d][:, :], ACT.Copy, scale=col(w, 1)).then_inc(inter_read[d], 1)

                def keys(w):
                    d = w.d
                    act.wait_ge(p_done[d], w.n + 1)
                    if w.ctx or w.s == 0:
                        wait(act, c_done[d][1], w.h * HALF if w.ctx else w.uses)
                        if not w.ctx:
                            act.wait_ge(c_done[d][2], w.h + 1)
                    else:
                        act.wait_ge(c_done[d][0], w.uses + 1)
                    end = 0 if d else P - 1
                    nc.scalar.activation(ke[:, d, :], psk[d][:, 1:3, :].rearrange("p a t -> p (a t)"), ACT.Copy,
                                         scale=rt[:, d, w.s, end:end + 1]).then_inc(ke_done[d], 1)

                def high(w):
                    d = w.d
                    if w.join:
                        act.wait_ge(y_done[d], w.f + 1)
                        nc.scalar.activation(ysp[:, 0, bass.ds(HT * w.h, HT), bass.ds(w.c * P, P)], yt[:, d, :, :],
                                             ACT.Copy).then_inc(hi_done[d], 1)
                walk(act, [exps, keys, inter, high])

            @block.gpsimd
            def _(pool):
                with pool.Fori(0, H) as h:
                    for d in range(2):
                        wait_alone(pool, ctx_c_taken, 2 * h + d + 1)
                        pool.dma_start(new_C[0, 0, d][bass.ds(h, 1)].rearrange("a (v p) k -> p (a v) k", p=P),
                                       cc[:, :, 0:DH]).then_inc(ctx_stored, 16)
                        with nc.allow_non_contiguous_dma("normalisers"):
                            pool.dma_start(new_n[0, 0, d][bass.ds(h, 1)].rearrange("a (v p) -> p (a v)", p=P),
                                           cc[:, :, DH]).then_inc(ctx_stored, 16)
                pool.wait_ge(ctx_stored, 64 * H)


def out_phase(nc, sem, sb, ps, m_d, w_out, gate_d, x_prompt, x_sample, norm_f, y_prompt, y_sample):
    def two(name):
        return [sem(f"o_{name}{s}") for s in range(2)]
    half_made = sem("o_half_made")
    w_loaded, w_hi, w_lo, const_loaded = two("w_loaded"), sem("o_w_hi"), sem("o_w_lo"), sem("o_const")
    m_loaded, x_loaded, m_hi, m_lo, prod, gated, added, sq_done, var_done, rstd_done, out_done = (
        two(n) for n in ("m_loaded", "x_loaded", "m_hi", "m_lo", "prod", "gated", "added", "sq_done",
                         "var_done", "rstd_done", "out_done"))
    stored = [sem(f"o_stored{s}", software_dma=True) for s in range(2)]
    with ExitStack() as st:
        raw = sb(st, "o_raw", [P, 2, D])
        wsp = sb(st, "o_wsp", [P, 2, KT, D], F32R)
        mt = sb(st, "o_mt", [P, 2, KT, P])
        msp = sb(st, "o_msp", [P, 2, 2, KT, P], F32R)
        xt = sb(st, "o_xt", [P, 2, D])
        yt = sb(st, "o_yt", [P, 2, D])
        ot = sb(st, "o_ot", [P, 2, D])
        sq = sb(st, "o_sq", [P, D])
        ss = sb(st, "o_ss", [P, 2, 4])
        gb = sb(st, "o_gb", [P, 2, D])
        nf = sb(st, "o_nf", [P, D])
        pp = [ps(st, f"o_pp{s}", [P, 2, 512]) for s in range(2)]

        def chunks(eng, step):
            step(0, 0, 0, 0, None)
            with eng.Fori(0, LAT // 2) as i:
                step(1, i, 2 * i + 1, 1, 2 * i)
                step(0, i + 1, 2 * i + 2, 1, 2 * i + 1)

        with nc.Block() as block:
            @block.sync
            def _(sp):
                for k in range(KT):
                    if k >= 2:
                        sp.wait_ge(w_lo, k - 1)
                    sp.dma_start(raw[:, k % 2, :], w_out[k * P:(k + 1) * P, :]).then_inc(w_loaded[k % 2], 16)
                sp.dma_start(gb[:, :, :], gate_d.rearrange("(a j) n -> a j n", a=1).broadcast_to([P, 2, D])).then_inc(const_loaded, 16)
                sp.dma_start(nf[:, :], norm_f.rearrange("(a n) -> a n", a=1).broadcast_to([P, D])).then_inc(const_loaded, 16)

                def step(s, n, c, j, lat):
                    wait_alone(sp, m_lo[s], n)
                    sp.dma_start(mt[:, s, :, :], m_d[:, :, bass.ds(c * P, P)].rearrange("k p t -> p k t")).then_inc(m_loaded[s], 16)
                    wait_alone(sp, added[s], n)
                    sp.dma_start(xt[:, s, :], x_prompt[0] if lat is None else x_sample[0][bass.ds(lat * P, P), :]
                                 ).then_inc(x_loaded[s], 16)
                chunks(sp, step)

            @block.gpsimd
            def _(pool):
                def step(s, n, c, j, lat):
                    wait_alone(pool, var_done[s], n + 1)
                    nc.gpsimd.tensor_tensor(ss[:, s, 2:3], ss[:, s, 1:2], ss[:, s, 3:4], ALU.pow).then_inc(rstd_done[s], 1)
                    wait_alone(pool, out_done[s], n + 1)
                    pool.dma_start(y_prompt[0] if lat is None else y_sample[0][bass.ds(lat * P, P), :], ot[:, s, :]
                                   ).then_inc(stored[s], 16)
                nc.gpsimd.memset(ss[:, :, 3:4], -0.5).then_inc(half_made, 1)
                pool.wait_ge(half_made, 1)
                chunks(pool, step)
                pool.wait_ge(stored[0], 16 * (LAT // 2 + 1))
                pool.wait_ge(stored[1], 16 * (LAT // 2))

            @block.scalar
            def _(act):
                for k in range(KT):
                    act.wait_ge(w_loaded[k % 2], 16 * (k // 2 + 1))
                    nc.scalar.activation(wsp[:, 0, k, :], raw[:, k % 2, :], ACT.Copy).then_inc(w_hi, 1)

                def step(s, n, c, j, lat):
                    act.wait_ge(m_loaded[s], 16 * n + 16)
                    wait(act, prod[s], n)
                    nc.scalar.activation(msp[:, s, 0, :, :], mt[:, s, :, :], ACT.Copy).then_inc(m_hi[s], 1)

                def late(s, n):
                    act.wait_ge(added[s], n + 1)
                    nc.scalar.activation(sq[:, :], yt[:, s, :], ACT.Square, accum_out=ss[:, s, 0:1]).then_inc(sq_done[s], 1)

                step(0, 0, 0, 0, None)
                with act.Fori(0, LAT // 2) as i:
                    step(1, i, 2 * i + 1, 1, 2 * i)
                    late(0, i)
                    step(0, i + 1, 2 * i + 2, 1, 2 * i + 1)
                    late(1, i)
                late(0, LAT // 2)

            @block.tensor
            def _(pe):
                pe.wait_ge(w_lo, KT)

                def step(s, n, c, j, lat):
                    pe.wait_ge(m_lo[s], n + 1)
                    wait(pe, gated[s], n)
                    for half in range(2):
                        for k in range(KT):
                            for q, (mp, wp) in enumerate(((1, 0), (0, 1), (0, 0))):
                                last = nc.tensor.matmul(pp[s][:, half, :], msp[:, s, mp, k, :],
                                                        wsp[:, wp, k, half * 512:(half + 1) * 512],
                                                        start=(k == 0 and q == 0), stop=(k == KT - 1 and q == 2))
                    last.then_inc(prod[s], 1)
                chunks(pe, step)

            @block.vector
            def _(dve):
                for k in range(KT):
                    dve.wait_ge(w_hi, k + 1)
                    nc.vector.tensor_tensor(wsp[:, 1, k, :], raw[:, k % 2, :], wsp[:, 0, k, :].bitcast(F32),
                                            ALU.subtract).then_inc(w_lo, 1)
                dve.wait_ge(const_loaded, 32)

                def step(s, n, c, j, lat):
                    dve.wait_ge(m_hi[s], n + 1)
                    nc.vector.tensor_tensor(msp[:, s, 1, :, :], mt[:, s, :, :], msp[:, s, 0, :, :].bitcast(F32),
                                            ALU.subtract).then_inc(m_lo[s], 1)

                def late(s, n, j):
                    dve.wait_ge(prod[s], n + 1)
                    wait(dve, out_done[s], n)
                    nc.vector.tensor_tensor(yt[:, s, :], pp[s][:, :, :].rearrange("p a n -> p (a n)"), gb[:, j, :],
                                            ALU.mult).then_inc(gated[s], 1)
                    dve.wait_ge(gated[s], n + 1)
                    dve.wait_ge(x_loaded[s], 16 * n + 16)
                    nc.vector.tensor_tensor(yt[:, s, :], yt[:, s, :], xt[:, s, :], ALU.add).then_inc(added[s], 1)
                    dve.wait_ge(sq_done[s], n + 1)
                    nc.vector.tensor_scalar(ss[:, s, 1:2], ss[:, s, 0:1], 1.0 / D, EPS, ALU.mult, ALU.add).then_inc(var_done[s], 1)
                    dve.wait_ge(rstd_done[s], n + 1)
                    wait(dve, stored[s], 16 * n)
                    nc.vector.scalar_tensor_tensor(out=ot[:, s, :], in0=yt[:, s, :], scalar=ss[:, s, 2:3], in1=nf[:, :],
                                                   op0=ALU.mult, op1=ALU.mult).then_inc(out_done[s], 1)

                step(0, 0, 0, 0, None)
                step(1, 0, 1, 1, 0)
                late(0, 0, 0)
                with dve.Fori(0, LAT // 2 - 1) as i:
                    step(0, i + 1, 2 * i + 2, 1, 2 * i + 1)
                    late(1, i, 1)
                    step(1, i + 1, 2 * i + 3, 1, 2 * i + 2)
                    late(0, i + 1, 1)
                step(0, LAT // 2, LAT, 1, LAT - 1)
                late(1, LAT // 2 - 1, 1)
                late(0, LAT // 2, 1)


_INS = ["x_prompt", "x_sample", "c", "state_C", "state_n", "state_m", "c_ctx", "norm_g", "w_ada", "b_ada", "w_in",
        "b_if", "g_sgu", "w_s", "b_s", "w_proj_a", "w_proj_b", "w_out", "norm_f"]
_OUTS = [(1, 128, 1024), (1, 2048, 1024), (1, 1, 2, 4, 256, 256), (1, 1, 2, 4, 256), (1, 1, 2, 4)]


def kernel(**inputs):
    import numpy as _np
    import concourse.bacc as _bacc
    from concourse.bass_utils import run_bass_kernel_spmd as _run

    nc = _bacc.Bacc("TRN2", target_bir_lowering=False, num_devices=1)
    arrays, args = {}, []
    for name in _INS:
        a = _np.ascontiguousarray(inputs[name])
        arrays[f"in_{name}"] = a
        args.append(nc.dram_tensor(f"in_{name}", a.shape, mybir.dt.from_np(a.dtype), kind="ExternalInput").ap())
    for i, shape in enumerate(_OUTS):
        args.append(nc.dram_tensor(f"out_{i}", shape, F32, kind="ExternalOutput").ap())
    build(nc, *args)
    r = _run(nc, [arrays], core_ids=[0])
    return tuple(r.results[0][f"out_{i}"] for i in range(len(_OUTS)))
```

```python
from contextlib import ExitStack

import concourse.bass as bass
from concourse import mybir

F32 = mybir.dt.float32
F32R = mybir.dt.float32r
ALU = mybir.AluOpType
ACT = mybir.ActivationFunctionType

P = 128
D = 1024
KT = D // P
H = 4
DH = D // H
HT = DH // P
N_IF = 2 * 2 * H
CTX = 1
LAT = 16
NC = CTX + LAT
TOK = NC * P
EPS = 1e-6
MASKED = -1.0e30
NB = -(-TOK // 512)
BLOCK_ENDS = [TOK * (b + 1) // NB // 16 * 16 for b in range(NB)]
BLOCKS = [(lo, hi - lo) for lo, hi in zip([0] + BLOCK_ENDS, BLOCK_ENDS)]
DE = DH + 1

Q0, K0, V0, O0, Z0 = (i * D for i in range(5))
IF0 = 5 * D
U0, VB0, ZB0, GA0, GB0 = (IF0 + N_IF + i * D for i in range(5))


def wait(eng, sem, value):
    if not (isinstance(value, int) and value <= 0):
        eng.wait_ge(sem, value)


passed = []


def wait_alone(eng, sem, value):
    if not isinstance(value, int):
        eng.wait_ge(sem, value)
        eng.sem_inc(passed[-1], 1)
    elif value > 0:
        eng.wait_ge(sem, value)


def build(nc, x_prompt, x_sample, c, state_C, state_n, state_m, c_ctx, norm_g, w_ada, b_ada, w_in, b_if,
          g_sgu, w_s, b_s, w_proj_a, w_proj_b, w_out, norm_f,
          y_prompt, y_sample, new_C, new_n, new_m):
    top = ExitStack()
    held = []

    def sem(name, software_dma=False):
        if software_dma:
            return top.enter_context(nc.semaphore(name))
        made = nc.semaphore(name)
        held.append((made, made.__enter__()))
        return held[-1][1]

    def stage_end():
        with nc.Block() as block:
            @block.gpsimd
            def _(pool):
                for _, s in held:
                    pool.sem_clear(s)
        while held:
            held.pop()[0].__exit__(None, None, None)

    def sb(stack, name, shape, dt=F32):
        return stack.enter_context(nc.sbuf_tensor(name, shape, dt))

    def ps(stack, name, shape):
        return stack.enter_context(nc.psum_tensor(name, shape, F32))

    def dram(name, shape):
        return nc.dram_tensor(name, shape, F32, kind="Internal").ap()

    w_in2 = w_in[0]
    qk_d = dram("qk_d", [KT, 2, P, TOK])
    gateA_d, u_d, sga_d, sgb_d, m_d = (
        dram(n, [KT, P, TOK]) for n in
        ("gateA_d", "u_d", "sga_d", "sgb_d", "m_d"))
    v_d = dram("v_d", [TOK, D])
    vb_d = dram("vb_d", [TOK, D])
    if_d = dram("if_d", [N_IF, TOK])
    cols_d = dram("cols_d", [6 * H, TOK])
    r_d = dram("r_d", [2 * H, TOK])
    sp_d = dram("sp_d", [2 * H, NC])
    gate_d = dram("gate_d", [2, D])

    with top:
        passed.append(top.enter_context(nc.semaphore("passed")))
        ident = sb(top, "ident", [P, P])
        mask = sb(top, "mask", [P, 2, P])
        modT = sb(top, "modT", [P, 3 * KT, 2])
        modA = sb(top, "modA", [P, KT, 2])
        with ExitStack() as st:
            hsp = sb(st, "hsp", [P, 2, KT, TOK], F32R)
            norm_phase(nc, sem, sb, ps, x_prompt, x_sample, c, c_ctx, w_ada, b_ada, norm_g, gate_d,
                       ident, mask, modT, modA, hsp)
            stage_end()
            streamed_products(nc, sem, sb, ps, "p", hsp, [
                Phase("if", w_in2, [IF0], [if_d]),
                Phase("qk", w_in2, [Q0, K0], [qk_d[:, 0], qk_d[:, 1]]),
                Phase("oz", w_in2, [O0, Z0], [gateA_d]),
                Phase("uz", w_in2, [U0, ZB0], [u_d]),
                Phase("gg", w_in2, [GA0, GB0], [sga_d, sgb_d]),
                Phase("nat", w_in2, [V0, VB0], [v_d, vb_d])])
            stage_end()
        cols = sb(top, "cols", [P, NC, 6 * H])
        spb = sb(top, "spb", [P, 2 * H, NC])
        gate_phase(nc, sem, sb, ps, if_d, b_if, state_m, cols_d, r_d, sp_d, new_m, ident, cols, spb)
        stage_end()
        with ExitStack() as st:
            ysp = sb(st, "ysp", [P, 2, KT, TOK], F32R)
            sgu_phase(nc, sem, sb, ps, vb_d, u_d, w_s, b_s, g_sgu, ident, ysp)
            stage_end()
            streamed_products(nc, sem, sb, ps, "b", ysp, [Phase("mg", w_proj_b[0], [0], [m_d], gain=sgb_d)])
            stage_end()
            mlstm_phase(nc, sem, sb, ps, qk_d, v_d, gateA_d, r_d, state_C, state_n, new_C, new_n,
                        ident, mask, cols, spb, ysp)
            stage_end()
            streamed_products(nc, sem, sb, ps, "a", ysp,
                              [Phase("mg", w_proj_a[0], [0], [m_d], gain=sga_d, add=True)])
            stage_end()
        out_phase(nc, sem, sb, ps, m_d, w_out[0], gate_d, x_prompt, x_sample, norm_f, y_prompt, y_sample)


def norm_phase(nc, sem, sb, ps, x_prompt, x_sample, c, c_ctx, w_ada, b_ada, norm_g, gate_d,
               ident, mask, modT, modA, hsp):
    def two(name):
        return [sem(f"n_{name}{s}") for s in range(2)]
    const_made, c_loaded, sig_done, silu_done = (sem(f"n_{n}") for n in ("const_made", "c_loaded", "sig_done", "silu_done"))
    mod_taken, mod_turned, mod_biased, mod_ready, gate_stored = (
        sem(f"n_{n}") for n in ("mod_taken", "mod_turned", "mod_biased", "mod_ready", "gate_stored"))
    wada_loaded, mod_mm = two("wada_loaded"), two("mod_mm")
    x_loaded, sq_done, var_done, rstd_done, scaled, turned, modulated, hi_done, lo_done = (
        two(n) for n in ("x_loaded", "sq_done", "var_done", "rstd_done", "scaled", "turned", "modulated",
                         "hi_done", "lo_done"))
    GRP = 4
    NG = 3 * KT // GRP
    with ExitStack() as st:
        cT = sb(st, "n_cT", [P, KT, 2])
        csig = sb(st, "n_csig", [P, KT, 2])
        csil = sb(st, "n_csil", [P, KT, 2])
        wada = sb(st, "n_wada", [P, 2, KT, GRP * P])
        rows = sb(st, "n_rows", [2, 2, GRP * P])
        badaT = sb(st, "n_badaT", [P, 3 * KT])
        gT = sb(st, "n_gT", [P, KT])
        xt = sb(st, "n_xt", [P, 2, D])
        sq = sb(st, "n_sq", [P, D])
        ss = sb(st, "n_ss", [P, 2, 4])
        hx = sb(st, "n_hx", [P, 2, KT, P])
        prow = ps(st, "n_prow", [2, 2, GRP * P])
        pmod = ps(st, "n_pmod", [P, 3 * KT, 2])
        pt = [ps(st, f"n_pt{s}", [P, KT, P]) for s in range(2)]

        def chunks(eng, front, back):
            front(0, 0, None, 0, 0)
            front(1, 0, 0, 1, CTX * P)
            back(0, 0, None, 0, 0)
            with eng.Fori(0, LAT // 2 - 1) as i:
                front(0, i + 1, 2 * i + 1, 1, (2 * i + 1 + CTX) * P)
                back(1, i, 2 * i, 1, (2 * i + CTX) * P)
                front(1, i + 1, 2 * i + 2, 1, (2 * i + 2 + CTX) * P)
                back(0, i + 1, 2 * i + 1, 1, (2 * i + 1 + CTX) * P)
            front(0, LAT // 2, LAT - 1, 1, (LAT - 1 + CTX) * P)
            back(1, LAT // 2 - 1, LAT - 2, 1, (LAT - 2 + CTX) * P)
            back(0, LAT // 2, LAT - 1, 1, (LAT - 1 + CTX) * P)

        def none(s, n, c, stream, t0):
            pass

        with nc.Block() as block:
            @block.sync
            def _(sp):
                with nc.allow_non_contiguous_dma("vectors onto partitions"):
                    sp.dma_start(cT[:, :, 0], c_ctx.rearrange("(k p) -> p k", p=P)).then_inc(c_loaded, 16)
                    sp.dma_start(cT[:, :, 1], c[0].rearrange("(k p) -> p k", p=P)).then_inc(c_loaded, 16)
                for g in range(NG):
                    s = g % 2
                    if g >= 2:
                        sp.wait_ge(mod_mm[s], g // 2)
                    sp.dma_start(wada[:, s, :, :],
                                 w_ada[0][:, g * GRP * P:(g + 1) * GRP * P].rearrange("(k p) n -> p k n", p=P)
                                 ).then_inc(wada_loaded[s], 16)
                with nc.allow_non_contiguous_dma("vectors onto partitions"):
                    sp.dma_start(badaT[:, :], b_ada[0].rearrange("(k p) -> p k", p=P)).then_inc(c_loaded, 16)
                    sp.dma_start(gT[:, :], norm_g[0].rearrange("(k p) -> p k", p=P)).then_inc(c_loaded, 16)

                def load(s, n, c, stream, t0):
                    wait_alone(sp, turned[s], n)
                    src = x_prompt[0] if c is None else x_sample[0][bass.ds(c * P, P), :]
                    sp.dma_start(xt[:, s, :], src).then_inc(x_loaded[s], 16)
                chunks(sp, load, none)
                with nc.allow_non_contiguous_dma("gate rows"):
                    for j in range(2):
                        sp.wait_ge(mod_ready, 2)
                        sp.dma_start(gate_d[j].rearrange("(k p) -> p k", p=P),
                                     modT[:, 2 * KT:, j]).then_inc(gate_stored, 16)
                sp.wait_ge(gate_stored, 32)

            @block.gpsimd
            def _(pool):
                nc.gpsimd.memset(ident[:, :], 0.0).then_inc(const_made, 1)
                nc.gpsimd.memset(mask[:, :, :], 0.0).then_inc(const_made, 1)
                nc.gpsimd.memset(ss[:, :, 3:4], -0.5).then_inc(const_made, 1)
                pool.wait_ge(const_made, 3)
                nc.gpsimd.affine_select(out=ident[:, :], in_=ident[:, :], compare_op=ALU.not_equal,
                                        fill=1.0, base=0, pattern=[[-1, P]],
                                        channel_multiplier=1).then_inc(const_made, 1)
                nc.gpsimd.affine_select(out=mask[:, 0, :], in_=mask[:, 0, :], compare_op=ALU.is_ge,
                                        fill=MASKED, base=0, pattern=[[1, P]],
                                        channel_multiplier=-1).then_inc(const_made, 1)
                nc.gpsimd.affine_select(out=mask[:, 1, :], in_=mask[:, 1, :], compare_op=ALU.is_ge,
                                        fill=MASKED, base=0, pattern=[[-1, P]],
                                        channel_multiplier=1).then_inc(const_made, 1)

                def rstd(s, n, c, stream, t0):
                    wait_alone(pool, var_done[s], n + 1)
                    nc.gpsimd.tensor_tensor(ss[:, s, 2:3], ss[:, s, 1:2], ss[:, s, 3:4], ALU.pow).then_inc(rstd_done[s], 1)

                def low(s, n, c, stream, t0):
                    wait_alone(pool, hi_done[s], n + 1)
                    nc.gpsimd.tensor_tensor(hsp[:, 1, :, bass.ds(t0, P)], hx[:, s, :, :],
                                            hsp[:, 0, :, bass.ds(t0, P)].bitcast(F32), ALU.subtract).then_inc(lo_done[s], 1)
                chunks(pool, rstd, low)

            @block.scalar
            def _(act):
                act.wait_ge(c_loaded, 32)
                nc.scalar.activation(csig[:, :, :], cT[:, :, :], ACT.Sigmoid).then_inc(sig_done, 1)

                def scale(s, n, c, stream, t0):
                    act.wait_ge(x_loaded[s], (n + 1) * 16)
                    nc.scalar.activation(sq[:, :], xt[:, s, :], ACT.Square, accum_out=ss[:, s, 0:1]).then_inc(sq_done[s], 1)
                    act.wait_ge(rstd_done[s], n + 1)
                    nc.scalar.activation(xt[:, s, :], xt[:, s, :], ACT.Copy, scale=ss[:, s, 2:3]).then_inc(scaled[s], 1)

                def high(s, n, c, stream, t0):
                    act.wait_ge(modulated[s], n + 1)
                    nc.scalar.activation(hsp[:, 0, :, bass.ds(t0, P)], hx[:, s, :, :], ACT.Copy).then_inc(hi_done[s], 1)
                chunks(act, scale, high)

            @block.vector
            def _(dve):
                dve.wait_ge(sig_done, 1)
                nc.vector.tensor_tensor(csil[:, :, :], cT[:, :, :], csig[:, :, :], ALU.mult).then_inc(silu_done, 1)
                for g in range(NG):
                    dve.wait_ge(mod_mm[g % 2], g // 2 + 1)
                    if g >= 2:
                        dve.wait_ge(mod_turned, g - 1)
                    nc.vector.tensor_copy(rows[:, g % 2, :], prow[:, g % 2, :]).then_inc(mod_taken, 1)
                dve.wait_ge(mod_turned, NG)
                dve.wait_ge(c_loaded, 64)
                nc.vector.tensor_tensor(modT[:, :, :], pmod[:, :, :],
                                        badaT[:, :].unsqueeze(2).broadcast_to([P, 3 * KT, 2]),
                                        ALU.add).then_inc(mod_biased, 1)
                dve.wait_ge(mod_biased, 1)
                for j in range(2):
                    nc.vector.scalar_tensor_tensor(out=modA[:, :, j], in0=modT[:, KT:2 * KT, j], scalar=1.0,
                                                   in1=gT[:, :], op0=ALU.add, op1=ALU.mult).then_inc(mod_ready, 1)
                dve.wait_ge(mod_ready, 2)

                def variance(s, n, c, stream, t0):
                    dve.wait_ge(sq_done[s], n + 1)
                    nc.vector.tensor_scalar(ss[:, s, 1:2], ss[:, s, 0:1], 1.0 / D, EPS, ALU.mult, ALU.add).then_inc(var_done[s], 1)

                def modulate(s, n, c, stream, t0):
                    dve.wait_ge(turned[s], n + 1)
                    wait(dve, lo_done[s], n)
                    for k in range(KT):
                        last = nc.vector.tensor_scalar(hx[:, s, k, :], pt[s][:, k, :], modA[:, k, stream:stream + 1],
                                                       modT[:, k, stream:stream + 1], ALU.mult, ALU.add)
                    last.then_inc(modulated[s], 1)
                chunks(dve, variance, modulate)

            @block.tensor
            def _(pe):
                def turn_mod(g):
                    pe.wait_ge(mod_taken, g + 1)
                    for n in range(GRP):
                        last = nc.tensor.transpose(pmod[:, g * GRP + n, :], rows[:, g % 2, n * P:(n + 1) * P], ident[0:2, 0:2])
                    last.then_inc(mod_turned, 1)
                pe.wait_ge(silu_done, 1)
                pe.wait_ge(const_made, 6)
                for g in range(NG):
                    s = g % 2
                    pe.wait_ge(wada_loaded[s], 16 * (g // 2 + 1))
                    if g >= 2:
                        pe.wait_ge(mod_taken, g - 1)
                    for k in range(KT):
                        last = nc.tensor.matmul(prow[:, s, :], csil[:, k, :], wada[:, s, k, :], start=(k == 0), stop=(k == KT - 1))
                    last.then_inc(mod_mm[s], 1)
                    if g:
                        turn_mod(g - 1)
                turn_mod(NG - 1)

                def turn(s, n, c, stream, t0):
                    pe.wait_ge(scaled[s], n + 1)
                    wait(pe, modulated[s], n)
                    for k in range(KT):
                        last = nc.tensor.transpose(pt[s][:, k, :], xt[:, s, k * P:(k + 1) * P], ident[:, :])
                    last.then_inc(turned[s], 1)
                chunks(pe, none, turn)
NP = 4
SETS = 2


class Phase:

    def __init__(self, kind, w, cols, outs, gain=None, add=False):
        self.kind, self.w, self.cols, self.outs, self.gain, self.add = kind, w, cols, outs, gain, add
        self.iters = {"if": 1, "nat": H, "mg": KT // (2 * SETS)}.get(kind, KT // SETS)
        blocks = (NC + 1) // 2 if kind == "nat" else NB
        self.last = blocks - 1
        self.steps = [(e, b) for e in ((1,) if kind == "if" else (0, 1)) for b in range(blocks)]
        self.n_ready = 1 if kind in ("if", "oz", "uz") else 2
        self.n_sig = {"oz": 2, "uz": 1, "mg": 32}.get(kind, 0)
        self.n_part = {"oz": 1, "uz": 1}.get(kind, 0)
        self.n_stored = 16 if kind in ("if", "oz", "uz", "nat") else 32

    def columns(self, e, i):
        if self.kind == "if":
            at = [IF0, IF0 + P]
        elif self.kind == "nat":
            at = [self.cols[e] + DH * i, self.cols[e] + DH * i + P]
        elif self.kind == "mg":
            at = [(4 * i + 2 * e) * P, (4 * i + 2 * e + 1) * P]
        else:
            at = [c0 + (2 * i + e) * P for c0 in self.cols]
        return [self.w[:, bass.ds(a, P)] for a in at]


class Count:

    def __init__(self, base, per):
        self.base, self.per = base, per

    def at(self, i, more=0):
        return self.base + more + (self.per * i if self.per else 0)


class Step:
    def __init__(self, e, b, p, done, ready, sig, part, stored):
        self.e, self.b, self.p = e, b, p
        self.done, self.ready, self.sig, self.part, self.stored = done, ready, sig, part, stored


def plan(phases):
    names = ("done", "ready", "sig", "part", "stored")
    base = {n: [0] * NP for n in names}
    used = [0] * SETS
    out = []
    for ph in phases:
        def adds(n, b):
            return {"done": 0 if b == ph.last else 1, "ready": ph.n_ready, "sig": ph.n_sig,
                    "part": ph.n_part, "stored": ph.n_stored}[n]
        per = {n: [sum(adds(n, b) for _, b in ph.steps if b % NP == p) for p in range(NP)] for n in names}
        so_far = {n: [0] * NP for n in names}
        steps = []
        for e, b in ph.steps:
            p = b % NP
            steps.append(Step(e, b, p, *(Count(base[n][p] + so_far[n][p], per[n][p]) for n in names)))
            for n in names:
                so_far[n][p] += adds(n, b)
        out.append((ph, steps, list(used)))
        for n in names:
            for p in range(NP):
                base[n][p] += per[n][p] * ph.iters
        for e in {e for e, _ in ph.steps}:
            used[e] += ph.iters
    return out, base["stored"]


def streamed_products(nc, sem, sb, ps, tag, res, phases):
    planned, stored_total = plan(phases)
    raw_loaded = sem(f"{tag}_raw_loaded")
    w_hi = sem(f"{tag}_w_hi")
    w_all_lo = sem(f"{tag}_w_lo")
    w_used = [sem(f"{tag}_w_used{e}") for e in range(SETS)]
    blk_done = [sem(f"{tag}_blk_done{p}") for p in range(NP)]
    ready = [sem(f"{tag}_ready{p}") for p in range(NP)]
    sig = [sem(f"{tag}_sig{p}") for p in range(NP)]
    part = [sem(f"{tag}_part{p}") for p in range(NP)]
    stored = [sem(f"{tag}_stored{p}", software_dma=True) for p in range(NP)]
    starts_with_if = phases[0].kind == "if"

    with ExitStack() as st:
        raw = sb(st, f"{tag}_raw", [P, KT, 2 * P])
        wsp = sb(st, f"{tag}_wsp", [P, SETS, 2, KT, 2 * P], F32R)
        stage = sb(st, f"{tag}_stage", [P, NP, 2, 512])
        bank = [[ps(st, f"{tag}_ps{p}{s}", [P, 512]) for s in range(2)] for p in range(NP)]

        def walk(eng, body):
            for ph, steps, used in planned:
                if ph.iters == 1:
                    for s in steps:
                        body(ph, s, 0, used)
                else:
                    with eng.Fori(0, ph.iters) as i:
                        for s in steps:
                            body(ph, s, i, used)

        def wait_products(eng, ph, s, i, used):
            if s.b == ph.last:
                eng.wait_ge(w_used[s.e], used[s.e] + i + 1)
            else:
                eng.wait_ge(blk_done[s.p], s.done.at(i, 1))

        def look_ahead(ph, s, i, used, split):
            if s.b != 1:
                return
            if ph.kind == "if":
                split(0, used[0], 1)
            elif s.e == 0:
                split(1, used[1] + i, used[0] + used[1] + 2 * i + 1)
            else:
                split(0, used[0] + i + 1, used[0] + used[1] + 2 * i + 2)

        with nc.Block() as block:
            @block.sync
            def _(sp):
                def load(n, columns):
                    wait_alone(sp, w_all_lo, n)
                    for h, src in enumerate(columns):
                        sp.dma_start(raw[:, :, h * P:(h + 1) * P],
                                     src.rearrange("(k p) n -> p k n", p=P)).then_inc(raw_loaded, 16)
                first = phases[0]
                load(0, first.columns(1 if starts_with_if else 0, 0))
                for at, (ph, steps, used) in enumerate(planned):
                    follow = phases[at + 1] if at + 1 < len(phases) else ph
                    n = used[0] + used[1]
                    if ph.kind == "if":
                        load(1, follow.columns(0, 0))
                        continue
                    if ph.iters > 1:
                        with sp.Fori(0, ph.iters - 1) as i:
                            load(n + 2 * i + 1, ph.columns(1, i))
                            load(n + 2 * i + 2, ph.columns(0, i + 1))
                    i = ph.iters - 1
                    load(n + 2 * i + 1, ph.columns(1, i))
                    load(n + 2 * i + 2, follow.columns(0, 0))

            @block.scalar
            def _(act):
                def split(e, n, n_all):
                    act.wait_ge(raw_loaded, 32 * (n_all + 1))
                    wait(act, w_used[e], n)
                    nc.scalar.activation(wsp[:, e, 0, :, :], raw[:, :, :], ACT.Copy).then_inc(w_hi, 1)

                def body(ph, s, i, used):
                    look_ahead(ph, s, i, used, split)
                    r, kind = s.p, ph.kind
                    if kind == "if":
                        return
                    if kind == "mg":
                        wait(act, stored[r], s.stored.at(i))
                        t0, width = BLOCKS[s.b]
                        for h in range(2):
                            act.dma_start(stage[:, r, h, 0:width],
                                          ph.gain[bass.ds(4 * i + 2 * s.e + h, 1), :, t0:t0 + width]
                                          .rearrange("a p t -> p (a t)")).then_inc(sig[r], 16)
                        return
                    wait_products(act, ph, s, i, used)
                    wait(act, stored[r], s.stored.at(i))
                    width = DH if kind == "nat" else BLOCKS[s.b][1]
                    A, B = (bank[r][h][:, 0:width] for h in range(2))
                    s0, s1 = (stage[:, r, h, 0:width] for h in range(2))
                    if kind == "nat":
                        alone = s.b == ph.last
                        nc.scalar.activation(s0, A, ACT.Copy).then_inc(ready[r], 2 if alone else 1)
                    elif kind == "qk":
                        nc.scalar.activation(s0, A, ACT.Copy, scale=DH ** -0.5).then_inc(ready[r], 1)
                    elif kind == "gg":
                        nc.scalar.activation(s0, A, ACT.Sigmoid).then_inc(ready[r], 1)
                        nc.scalar.activation(s1, B, ACT.Sigmoid).then_inc(ready[r], 1)
                    elif kind == "oz":
                        nc.scalar.activation(s0, A, ACT.Sigmoid).then_inc(sig[r], 1)
                        nc.scalar.activation(s1, B, ACT.Sigmoid).then_inc(sig[r], 1)
                    else:
                        nc.scalar.activation(s1, B, ACT.Sigmoid).then_inc(sig[r], 1)
                split(1 if starts_with_if else 0, 0, 0)
                walk(act, body)

            @block.vector
            def _(dve):
                def split(e, n, n_all):
                    dve.wait_ge(w_hi, n_all + 1)
                    nc.vector.tensor_tensor(wsp[:, e, 1, :, :], raw[:, :, :],
                                            wsp[:, e, 0, :, :].bitcast(F32), ALU.subtract).then_inc(w_all_lo, 1)

                def body(ph, s, i, used):
                    look_ahead(ph, s, i, used, split)
                    r, kind = s.p, ph.kind
                    width = DH if kind == "nat" else BLOCKS[s.b][1]
                    A, B = (bank[r][h][:, 0:width] for h in range(2))
                    s0, s1 = (stage[:, r, h, 0:width] for h in range(2))
                    if kind == "if":
                        wait_products(dve, ph, s, i, used)
                        wait(dve, stored[r], s.stored.at(i))
                        nc.vector.tensor_copy(stage[0:N_IF, r, 0, 0:width], bank[r][0][0:N_IF, 0:width]
                                              ).then_inc(ready[r], 1)
                    elif kind == "qk" or kind == "nat":
                        if kind == "nat" and s.b == ph.last:
                            return
                        wait_products(dve, ph, s, i, used)
                        wait(dve, stored[r], s.stored.at(i))
                        nc.vector.tensor_copy(s1, B).then_inc(ready[r], 1)
                    elif kind == "oz":
                        dve.wait_ge(sig[r], s.sig.at(i, 2))
                        nc.vector.tensor_tensor(s1, s1, B, ALU.mult).then_inc(part[r], 1)
                        dve.wait_ge(part[r], s.part.at(i, 1))
                        nc.vector.tensor_tensor(s0, s0, s1, ALU.mult).then_inc(ready[r], 1)
                    elif kind == "uz":
                        dve.wait_ge(sig[r], s.sig.at(i, 1))
                        nc.vector.tensor_tensor(s1, s1, B, ALU.mult).then_inc(part[r], 1)
                        dve.wait_ge(part[r], s.part.at(i, 1))
                        nc.vector.tensor_tensor(s0, s1, A, ALU.mult).then_inc(ready[r], 1)
                    elif kind == "mg":
                        dve.wait_ge(sig[r], s.sig.at(i, 32))
                        wait_products(dve, ph, s, i, used)
                        nc.vector.tensor_tensor(s0, s0, A, ALU.mult).then_inc(ready[r], 1)
                        nc.vector.tensor_tensor(s1, s1, B, ALU.mult).then_inc(ready[r], 1)
                split(1 if starts_with_if else 0, 0, 0)
                walk(dve, body)

            @block.tensor
            def _(pe):
                def body(ph, s, i, used):
                    if s.b == 0:
                        loads = (0 if ph.kind == "if" else used[0] + used[1] + 2 * i + s.e)
                        pe.wait_ge(w_all_lo, loads + 1)
                    wait(pe, ready[s.p], s.ready.at(i))
                    for h in range(1 if ph.kind == "if" else 2):
                        if ph.kind == "nat" and 2 * s.b + h >= NC:
                            continue
                        for k in range(KT):
                            for j, (wp, rp) in enumerate(((1, 0), (0, 1), (0, 0))):
                                flags = dict(start=(k == 0 and j == 0), stop=(k == KT - 1 and j == 2))
                                if ph.kind == "nat":
                                    t0 = (2 * s.b + h) * P
                                    last = nc.tensor.matmul(bank[s.p][h][:, 0:DH], res[:, rp, k, t0:t0 + P],
                                                            wsp[:, s.e, wp, k, :], **flags)
                                else:
                                    t0, width = BLOCKS[s.b]
                                    last = nc.tensor.matmul(bank[s.p][h][:, 0:width],
                                                            wsp[:, s.e, wp, k, h * P:(h + 1) * P],
                                                            res[:, rp, k, t0:t0 + width], **flags)
                    last.then_inc(w_used[s.e] if s.b == ph.last else blk_done[s.p], 1)
                walk(pe, body)

            @block.gpsimd
            def _(pool):
                def body(ph, s, i, used):
                    r, kind = s.p, ph.kind
                    wait_alone(pool, ready[r], s.ready.at(i, ph.n_ready))
                    if kind == "if":
                        t0, width = BLOCKS[s.b]
                        pool.dma_start(ph.outs[0][:, t0:t0 + width], stage[0:N_IF, r, 0, 0:width]
                                       ).then_inc(stored[r], 16)
                    elif kind == "nat":
                        n = min(2, NC - 2 * s.b)
                        pool.dma_start(ph.outs[s.e][2 * s.b * P:(2 * s.b + n) * P, bass.ds(DH * i, DH)]
                                       .rearrange("(c p) n -> p c n", p=P),
                                       stage[:, r, 0:n, 0:DH]).then_inc(stored[r], 16)
                    else:
                        t0, width = BLOCKS[s.b]
                        for h in range(ph.n_stored // 16):
                            out = ph.outs[0] if kind == "mg" else ph.outs[h]
                            tile = 4 * i + 2 * s.e + h if kind == "mg" else 2 * i + s.e
                            more = dict(accum_op=ALU.add) if ph.add else {}
                            pool.dma_start(out[bass.ds(tile, 1), :, t0:t0 + width].rearrange("a p t -> p (a t)"),
                                           stage[:, r, h, 0:width], **more).then_inc(stored[r], 16)
                walk(pool, body)
                for p in range(NP):
                    pool.wait_ge(stored[p], stored_total[p])


def gate_phase(nc, sem, sb, ps, if_d, b_if, state_m, cols_d, r_d, sp_d, new_m, ident, cols, spb):
    loaded = sem("g_loaded")
    chain = sem("g_chain")
    const_rows = sem("g_const")
    stored = sem("g_stored")
    back = sem("g_back")
    turned = sem("g_turned")
    taken = sem("g_taken")
    dsts = []
    with ExitStack() as st:
        li = sb(st, "g_li", [H, TOK])
        lf = sb(st, "g_lf", [H, TOK])
        t1 = sb(st, "g_t1", [H, TOK])
        keep = sb(st, "g_keep", [H, 2, NC, P])
        outs = [[sb(st, f"g_{n}{d}", [H, TOK]) for n in ("u", "sc", "em", "r")] for d in range(2)]
        m = sb(st, "g_m", [H, TOK])
        b = sb(st, "g_b", [H, TOK])
        ms = sb(st, "g_ms", [H, NC])
        spr = [sb(st, f"g_sp{d}", [H, NC]) for d in range(2)]
        bias = sb(st, "g_bias", [H, 2, 2])
        m0 = sb(st, "g_m0", [H, 2])
        mctx = sb(st, "g_mctx", [H, 2])
        rows = sb(st, "g_rows", [6 * H, TOK])
        pt = [ps(st, f"g_pt{s}", [P, 6 * H]) for s in range(2)]
        n_steps = 15
        per_dir_loads = 32

        def ch(x):
            return x.rearrange("h (c t) -> h c t", t=P)

        with nc.Block() as block:
            @block.gpsimd
            def _(pool):
                nc.gpsimd.memset(keep[:, :, :, :], 1.0).then_inc(const_rows, 1)
                pool.wait_ge(const_rows, 1)
                nc.gpsimd.memset(keep[:, 0, :, 0:1], 0.0).then_inc(const_rows, 1)
                nc.gpsimd.memset(keep[:, 1, :, P - 1:P], 0.0).then_inc(const_rows, 1)

            @block.sync
            def _(sp):
                with nc.allow_non_contiguous_dma("small vectors"):
                    sp.dma_start(bias[:, :, :], b_if[0].rearrange("d g h -> h d g")).then_inc(loaded, 16)
                    sp.dma_start(m0[:, :], state_m[0, 0].rearrange("d h -> h d")).then_inc(loaded, 16)
                for d in range(2):
                    if d:
                        sp.wait_ge(chain, n_steps)
                    sp.dma_start(li[:, :], if_d[2 * H * d:2 * H * d + H, :]).then_inc(loaded, 16)
                    sp.dma_start(lf[:, :], if_d[2 * H * d + H:2 * H * (d + 1), :]).then_inc(loaded, 16)
                for d in range(2):
                    sp.wait_ge(chain, n_steps * (d + 1))
                    for q in range(3):
                        sp.dma_start(cols_d[(2 * q + d) * H:(2 * q + d + 1) * H, :], outs[d][q][:, :]).then_inc(stored, 16)
                    sp.dma_start(r_d[d * H:(d + 1) * H, :], outs[d][3][:, :]).then_inc(stored, 16)
                    sp.dma_start(sp_d[d * H:(d + 1) * H, :], spr[d][:, :]).then_inc(stored, 16)
                with nc.allow_non_contiguous_dma("small vectors"):
                    sp.dma_start(new_m[0, 0].rearrange("d h -> h d"), mctx[:, :]).then_inc(stored, 16)
                sp.wait_ge(stored, 11 * 16)
                sp.dma_start(rows[:, :], cols_d).then_inc(back, 16)
                sp.dma_start(spb[:, :, :], sp_d.rearrange("(a d) c -> a d c", a=1).broadcast_to([P, 2 * H, NC])
                             ).then_inc(back, 16)
                sp.wait_ge(back, 32)

            @block.tensor
            def _(pe):
                pe.wait_ge(back, 32)
                for c in range(NC):
                    if c >= 2:
                        pe.wait_ge(taken, c - 1)
                    nc.tensor.transpose(pt[c % 2][:, :], rows[:, c * P:(c + 1) * P],
                                        ident[0:6 * H, 0:6 * H]).then_inc(turned, 1)

            def step_list(d):
                pass
            @block.scalar
            def _(act):
                for d in range(2):
                    n0 = n_steps * d
                    act.wait_ge(chain, n0 + 3)
                    nc.scalar.activation(t1[:, :], t1[:, :], ACT.Exp, scale=-1.0).then_inc(chain, 1)
                    act.wait_ge(chain, n0 + 4)
                    nc.scalar.activation(t1[:, :], t1[:, :], ACT.Ln, bias=1.0).then_inc(chain, 1)
                    act.wait_ge(chain, n0 + 12)
                    nc.scalar.activation(outs[d][1][:, :], outs[d][1][:, :], ACT.Exp).then_inc(chain, 1)
                    act.wait_ge(chain, n0 + 13)
                    nc.scalar.activation(outs[d][2][:, :], m[:, :], ACT.Exp, scale=-1.0).then_inc(chain, 1)

            @block.vector
            def _(dve):
                dve.wait_ge(const_rows, 3)
                for d in range(2):
                    n0 = n_steps * d
                    u, sc, em, r = outs[d]
                    bf, bi = bias[:, d, 1:2], bias[:, d, 0:1]

                    def rev(x):
                        return x[:, ::-1] if d else x
                    lat, ctx = slice(CTX * P, TOK), slice(0, CTX * P)
                    dve.wait_ge(loaded, 32 + 32 * (d + 1))
                    nc.vector.tensor_scalar(lf[:, :], lf[:, :], bf, None, ALU.add).then_inc(chain, 1)
                    dve.wait_ge(chain, n0 + 1)
                    nc.vector.tensor_scalar(li[:, :], li[:, :], bi, None, ALU.add).then_inc(chain, 1)
                    nc.vector.scalar_tensor_tensor(out=t1[:, :], in0=lf[:, :], scalar=-1.0, in1=lf[:, :],
                                                   op0=ALU.mult, op1=ALU.max).then_inc(chain, 1)
                    dve.wait_ge(chain, n0 + 5)
                    nc.vector.scalar_tensor_tensor(out=lf[:, :], in0=lf[:, :], scalar=0.0, in1=t1[:, :],
                                                   op0=ALU.min, op1=ALU.subtract).then_inc(chain, 1)
                    dve.wait_ge(chain, n0 + 6)
                    nc.vector.tensor_tensor_scan(rev(b[:, :]), rev(keep[:, d, :, :].rearrange("h c t -> h (c t)")),
                                                 rev(lf[:, :]), 0.0, ALU.mult, ALU.add).then_inc(chain, 1)
                    nc.vector.tensor_tensor_scan(rev(m[:, ctx]), rev(lf[:, ctx]), rev(li[:, ctx]), 0.0,
                                                 ALU.add, ALU.max).then_inc(chain, 1)
                    nc.vector.tensor_tensor_scan(rev(m[:, lat]), rev(lf[:, lat]), rev(li[:, lat]), m0[:, d:d + 1],
                                                 ALU.add, ALU.max).then_inc(chain, 1)
                    dve.wait_ge(chain, n0 + 9)
                    end = 0 if d else P - 1
                    firsts, rest, before = ((CTX + LAT - 1, slice(CTX, NC - 1), slice(CTX + 1, NC)) if d else
                                            (CTX, slice(CTX + 1, NC), slice(CTX, NC - 1)))
                    nc.vector.memset(ms[:, 0:CTX], 0.0)
                    nc.vector.tensor_copy(ms[:, firsts:firsts + 1], m0[:, d:d + 1])
                    nc.vector.tensor_copy(ms[:, rest], ch(m[:, :])[:, before, end])
                    nc.vector.tensor_copy(mctx[:, d:d + 1], m[:, end:end + 1])
                    nc.vector.tensor_tensor(u[:, :], li[:, :], b[:, :], ALU.subtract)
                    nc.vector.tensor_tensor(r[:, :], b[:, :], m[:, :], ALU.subtract).then_inc(chain, 2)
                    dve.wait_ge(chain, n0 + 11)
                    nc.vector.tensor_tensor(ch(sc[:, :]), ch(r[:, :]), ms[:, :].unsqueeze(2).broadcast_to([H, NC, P]),
                                            ALU.add).then_inc(chain, 1)
                    dve.wait_ge(chain, n0 + 14)
                    nc.vector.tensor_copy(spr[d][:, :], ch(sc[:, :])[:, :, end]).then_inc(chain, 1)
                    dve.wait_ge(chain, n0 + 15)
                for c in range(NC):
                    dve.wait_ge(turned, c + 1)
                    nc.vector.tensor_copy(cols[:, c, :], pt[c % 2][:, :]).then_inc(taken, 1)


def sgu_phase(nc, sem, sb, ps, vb_d, u_d, w_s, b_s, g_sgu, ident, ysp):
    def two(name):
        return [sem(f"s_{name}{s}") for s in range(2)]
    half_made = sem("s_half_made")
    const_loaded, w_turned, w_taken = sem("s_const"), sem("s_w_turned"), sem("s_w_taken")
    v_loaded, u_loaded, sq_done, var_done, rstd_done, v_scaled, mixed, mix_read, biased, gated, hi_done, lo_done = (
        two(n) for n in ("v_loaded", "u_loaded", "sq_done", "var_done", "rstd_done", "v_scaled", "mixed",
                         "mix_read", "biased", "gated", "hi_done", "lo_done"))
    with ExitStack() as st:
        ws = sb(st, "s_ws", [P, H, P])
        wsT = sb(st, "s_wsT", [P, H, P])
        bsb = sb(st, "s_bsb", [P, H, P])
        gcol = sb(st, "s_gcol", [P, KT])
        vt = sb(st, "s_vt", [P, 2, D])
        ut = sb(st, "s_ut", [P, 2, KT, P])
        sq = sb(st, "s_sq", [P, D])
        ss = sb(st, "s_ss", [P, 2, 4])
        yt = sb(st, "s_yt", [P, 2, KT, P])
        pm = [ps(st, f"s_pm{s}", [P, KT, P]) for s in range(2)]
        pw = ps(st, "s_pw", [P, H, P])

        def chunks(eng, front, back):
            front(0, 0, 0)
            with eng.Fori(0, (NC - 1) // 2) as i:
                front(1, i, 2 * i + 1)
                back(0, i, 2 * i)
                front(0, i + 1, 2 * i + 2)
                back(1, i, 2 * i + 1)
            back(0, (NC - 1) // 2, NC - 1)

        def none(s, n, c):
            pass

        with nc.Block() as block:
            @block.sync
            def _(sp):
                sp.dma_start(ws[:, :, :], w_s[0].rearrange("g t s -> t g s")).then_inc(const_loaded, 16)
                sp.dma_start(bsb[:, :, :], b_s[0].rearrange("(a g) t -> a g t", a=1).broadcast_to([P, H, P])
                             ).then_inc(const_loaded, 16)
                with nc.allow_non_contiguous_dma("vector onto partitions"):
                    sp.dma_start(gcol[:, :], g_sgu[0].rearrange("(k p) -> p k", p=P)).then_inc(const_loaded, 16)

                def load_v(s, n, c):
                    wait_alone(sp, mixed[s], n)
                    sp.dma_start(vt[:, s, :], vb_d[bass.ds(c * P, P), :]).then_inc(v_loaded[s], 16)

                def load_u(s, n, c):
                    wait_alone(sp, gated[s], n)
                    sp.dma_start(ut[:, s, :, :], u_d[:, :, bass.ds(c * P, P)].rearrange("k p t -> p k t")
                                 ).then_inc(u_loaded[s], 16)
                chunks(sp, load_v, load_u)

            @block.gpsimd
            def _(pool):
                def rstd(s, n, c):
                    wait_alone(pool, var_done[s], n + 1)
                    nc.gpsimd.tensor_tensor(ss[:, s, 2:3], ss[:, s, 1:2], ss[:, s, 3:4], ALU.pow).then_inc(rstd_done[s], 1)

                def low(s, n, c):
                    wait_alone(pool, hi_done[s], n + 1)
                    nc.gpsimd.tensor_tensor(ysp[:, 1, :, bass.ds(c * P, P)], yt[:, s, :, :],
                                            ysp[:, 0, :, bass.ds(c * P, P)].bitcast(F32), ALU.subtract).then_inc(lo_done[s], 1)
                nc.gpsimd.memset(ss[:, :, 3:4], -0.5).then_inc(half_made, 1)
                pool.wait_ge(half_made, 1)
                chunks(pool, rstd, low)

            @block.scalar
            def _(act):
                def scale(s, n, c):
                    act.wait_ge(v_loaded[s], 16 * n + 16)
                    nc.scalar.activation(sq[:, :], vt[:, s, :], ACT.Square, accum_out=ss[:, s, 0:1]).then_inc(sq_done[s], 1)
                    act.wait_ge(rstd_done[s], n + 1)
                    nc.scalar.activation(vt[:, s, :], vt[:, s, :], ACT.Copy, scale=ss[:, s, 2:3]).then_inc(v_scaled[s], 1)

                def high(s, n, c):
                    act.wait_ge(gated[s], n + 1)
                    nc.scalar.activation(ysp[:, 0, :, bass.ds(c * P, P)], yt[:, s, :, :], ACT.Copy).then_inc(hi_done[s], 1)
                chunks(act, scale, high)

            @block.tensor
            def _(pe):
                pe.wait_ge(const_loaded, 48)
                for g in range(H):
                    last = nc.tensor.transpose(pw[:, g, :], ws[:, g, :], ident[:, :])
                last.then_inc(w_turned, 1)
                pe.wait_ge(w_taken, 1)

                def mix(s, n, c):
                    pe.wait_ge(v_scaled[s], n + 1)
                    wait(pe, mix_read[s], n)
                    for k in range(KT):
                        last = nc.tensor.matmul(pm[s][:, k, :], vt[:, s, k * P:(k + 1) * P], wsT[:, k // HT, :],
                                                start=True, stop=True)
                    last.then_inc(mixed[s], 1)
                chunks(pe, none, mix)

            @block.vector
            def _(dve):
                dve.wait_ge(w_turned, 1)
                nc.vector.tensor_copy(wsT[:, :, :], pw[:, :, :]).then_inc(w_taken, 1)

                def variance(s, n, c):
                    dve.wait_ge(sq_done[s], n + 1)
                    nc.vector.tensor_scalar(ss[:, s, 1:2], ss[:, s, 0:1], 1.0 / D, EPS, ALU.mult, ALU.add).then_inc(var_done[s], 1)

                def gate(s, n, c):
                    dve.wait_ge(mixed[s], n + 1)
                    wait(dve, lo_done[s], n)
                    for k in range(KT):
                        last = nc.vector.scalar_tensor_tensor(out=yt[:, s, k, :], in0=pm[s][:, k, :], scalar=gcol[:, k:k + 1],
                                                              in1=bsb[:, k // HT, :], op0=ALU.mult, op1=ALU.add)
                    last.then_inc(mix_read[s], 1)
                    dve.wait_ge(mix_read[s], n + 1)
                    dve.wait_ge(u_loaded[s], 16 * n + 16)
                    nc.vector.tensor_tensor(yt[:, s, :, :], yt[:, s, :, :], ut[:, s, :, :], ALU.mult).then_inc(gated[s], 1)
                chunks(dve, variance, gate)


def mlstm_phase(nc, sem, sb, ps, qk_d, v_d, gate_d, r_d, state_C, state_n, new_C, new_n,
                ident, mask, cols, spb, ysp):
    def per(name, n=2):
        return [sem(f"m_{name}{d}") for d in range(n)]

    SL = 3
    qk_loaded, r_loaded, v_loaded, c_done = ([[sem(f"m_{n}{d}{s}") for s in range(SL)] for d in range(2)]
                                             for n in ("qk_loaded", "r_loaded", "v_loaded", "c_done"))
    raw_loaded, n_loaded, st_turned, st_taken = per("raw_loaded"), sem("m_n_loaded"), sem("m_st_turned"), sem("m_st_taken")
    ones_made = sem("m_ones")
    g_loaded, lo_done = ([[sem(f"m_{n}{d}{s}", software_dma=n == "g_loaded") for s in range(2)] for d in range(2)]
                         for n in ("g_loaded", "lo_done"))
    (sk_done, masked, e_done, p_done, ke_done, inter_done, inter_read, intra_done, x_done, neg_done, den_done,
     rec_done, c_updated, h_done, hi_done) = (per(n) for n in (
         "sk_done", "masked", "e_done", "p_done", "ke_done", "inter_done", "inter_read", "intra_done",
         "x_done", "neg_done", "den_done", "rec_done", "c_updated", "h_done", "hi_done"))
    hT_done, gated = sem("m_hT_done"), sem("m_gated")
    ctx_c_taken, ctx_stored = sem("m_ctx_c_taken"), sem("m_ctx_stored", software_dma=True)
    HALF = LAT // 2

    with ExitStack() as st:
        qkt = sb(st, "m_qkt", [P, 2, SL, HT, 2, P])
        vt = sb(st, "m_vt", [P, 2, SL, DE])
        rt = sb(st, "m_rt", [P, 2, SL, P])
        gt = sb(st, "m_gt", [P, 2, 2, HT, P])
        pr = sb(st, "m_pr", [P, 2, P])
        ke = sb(st, "m_ke", [P, 2, DH])
        it = sb(st, "m_it", [P, 2, DE])
        xt = sb(st, "m_xt", [P, 2, DE])
        hs = sb(st, "m_hs", [P, 2, DH])
        dn = sb(st, "m_dn", [P, 2, 2])
        hst = sb(st, "m_hst", [P, NC, DH])
        cc = hst[:, HALF:HALF + 3, :].rearrange("p a n -> p (a n)")[:, 0:HT * DE].rearrange("p (a n) -> p a n", a=HT)
        C = sb(st, "m_C", [P, 2 * H, HT, DE])
        psk = [ps(st, f"m_psk{d}", [P, 3, P]) for d in range(2)]
        pnu = [ps(st, f"m_pnu{d}", [P, DE]) for d in range(2)]
        pin = ps(st, "m_pin", [P, DE])
        phT = ps(st, "m_phT", [P, 2, HT, P])
        pc = ps(st, "m_pc", [P, 2, 512])

        raw = hst[:, 0:2 * HT, :].rearrange("p (j a) k -> p j a k", a=HT)
        with nc.Block() as block:
            @block.sync
            def _(sp):
                with nc.allow_non_contiguous_dma("normalisers"):
                    for j in range(2 * H):
                        d, h = j // H, j % H
                        sp.dma_start(C[:, j, :, DH], state_n[0, 0, d, h].rearrange("(a p) -> p a", p=P)
                                     ).then_inc(n_loaded, 16)
                for j in range(2 * H):
                    if j >= 2:
                        sp.wait_ge(st_turned, j - 1)
                    sp.dma_start(raw[:, j % 2, :, :], state_C[0, 0, j // H, j % H].rearrange("(a p) k -> p a k", p=P)
                                 ).then_inc(raw_loaded[j % 2], 16)
                sp.wait_ge(n_loaded, 2 * H * 16)

            @block.gpsimd
            def _(pool):
                nc.gpsimd.memset(vt[:, :, :, DH:DE], 1.0).then_inc(ones_made, 1)
                pool.wait_ge(ones_made, 1)

            @block.tensor
            def _(pe):
                for j in range(2 * H):
                    pe.wait_ge(raw_loaded[j % 2], 16 * (j // 2 + 1))
                    if j >= 2:
                        pe.wait_ge(st_taken, j - 1)
                    for a in range(HT):
                        for b in range(HT):
                            last = nc.tensor.transpose(pc[:, j % 2, b * DH + a * P:b * DH + (a + 1) * P],
                                                       raw[:, j % 2, a, b * P:(b + 1) * P], ident[:, :])
                    last.then_inc(st_turned, 1)

            @block.vector
            def _(dve):
                for j in range(2 * H):
                    dve.wait_ge(st_turned, j + 1)
                    nc.vector.tensor_copy(C[:, j, :, 0:DH], pc[:, j % 2, :].rearrange("p (b v) -> p b v", b=HT)
                                          ).then_inc(st_taken, 1)

        class Step:

            def __init__(self, h, j=None, slot=2, pair=0, join=False, first=True):
                self.h, self.ctx, self.join, self.s = h, j is None, join, slot
                self.slot_keys = h * (LAT + 1) + (0 if first else j)
                self.slot_inter = h * LAT + (0 if first else j - 1)
                if j is None:
                    self.uses, self.n, self.l, self.c = h, h * (LAT + 1), h * LAT, (0, 0)
                    self.f, self.t = (h * HALF, h * (HALF + 1)), h * (HALF + 1)
                    self.finish, self.gs, self.g = (1,), 1, (h * (HALF // 2), h * (HALF // 2 + 1))
                else:
                    self.uses, self.n, self.l = h * HALF + pair, h * (LAT + 1) + 1 + j, h * LAT + j
                    self.c = (j + CTX, NC - 1 - j)
                    self.f, self.t = (h * HALF + j - HALF, h * (HALF + 1) + 1 + j - HALF), h * (HALF + 1) + 1 + j - HALF
                    self.finish = (0, 1) if join else ()
                    self.gs, nth = slot, pair - HALF // 2
                    self.g = (h * (HALF // 2) + nth, h * (HALF // 2 + slot) + nth + slot)

        def latent(h, at, i=0):
            return Step(h, 2 * i + at, at % 2, i + at // 2, at >= HALF, at < 2)

        def walk(eng, turn):
            with eng.Fori(0, H) as h:
                ctx = Step(h)
                turn(None, ctx, None)
                turn(ctx, latent(h, 0), None)
                turn(latent(h, 0), latent(h, 1), ctx)
                with eng.Fori(0, (HALF - 2) // 2) as i:
                    for j in (1, 2):
                        turn(latent(h, j, i), latent(h, j + 1, i), None)
                turn(latent(h, HALF - 1), latent(h, HALF), None)
                turn(latent(h, HALF), latent(h, HALF + 1), None)
                with eng.Fori(0, (HALF - 2) // 2) as i:
                    for j in (HALF + 1, HALF + 2):
                        turn(latent(h, j, i), latent(h, j + 1, i), latent(h, j - 1, i))
                turn(latent(h, LAT - 1), None, latent(h, LAT - 2))
                turn(None, None, latent(h, LAT - 1))

        def flat(x):
            return x.rearrange("p a n -> p (a n)")

        with nc.Block() as block:
            @block.sync
            def _(sp):
                def turn(cur, w, prev):
                    if w is None:
                        return
                    s, h = w.s, w.h
                    for d in range(2):
                        wait_alone(sp, ke_done[d], w.slot_keys)
                        sp.dma_start(rt[:, d, s, :], r_d[bass.ds(H * d + h, 1), bass.ds(w.c[d] * P, P)].broadcast_to([P, P])
                                     ).then_inc(r_loaded[d][s], 16)
                    for d in range(2):
                        wait_alone(sp, inter_done[d], w.slot_inter)
                        sp.dma_start(qkt[:, d, s, :, :, :].rearrange("p a r t -> p (a r) t"),
                                     qk_d[bass.ds(HT * h, HT), :, :, bass.ds(w.c[d] * P, P)].rearrange("a r p t -> p (a r) t")).then_inc(qk_loaded[d][s], 16)
                    for d in range(2):
                        wait_alone(sp, c_done[d][s], w.uses)
                        sp.dma_start(vt[:, d, s, 0:DH], v_d[bass.ds(w.c[d] * P, P), bass.ds(h * DH, DH)]
                                     ).then_inc(v_loaded[d][s], 16)
                walk(sp, turn)

            def col(w, d, q):
                return cols[:, bass.ds(w.c[d], 1), bass.ds((2 * q + d) * H + w.h, 1)].rearrange("p a b -> p (a b)")

            def out_tile(w, d, part):
                return ysp[:, part, bass.ds(HT * w.h, HT), bass.ds(w.c[d] * P, P)]

            @block.tensor
            def _(pe):
                def scores(w, d):
                    s = w.s
                    pe.wait_ge(qk_loaded[d][s], 16 * w.uses + 16)
                    wait(pe, ke_done[d], w.n)
                    for a in range(HT):
                        nc.tensor.matmul(psk[d][:, 0, :], qkt[:, d, s, a, 1, :], qkt[:, d, s, a, 0, :], start=(a == 0), stop=(a == HT - 1))
                    for a in range(HT):
                        last = nc.tensor.transpose(psk[d][:, 1 + a, :], qkt[:, d, s, a, 1, :], ident[:, :])
                    last.then_inc(sk_done[d], 1)

                def from_state(w, d):
                    wait(pe, c_updated[d], w.l)
                    wait(pe, inter_read[1 - d], w.l + d)
                    for a in range(HT):
                        last = nc.tensor.matmul(pin[:, :], qkt[:, d, w.s, a, 0, :],
                                                flat(C[:, bass.ds(H * d + w.h, 1), a, :]),
                                                start=(a == 0), stop=(a == HT - 1))
                    last.then_inc(inter_done[d], 1)

                def within(w, d):
                    pe.wait_ge(v_loaded[d][w.s], 16 * w.uses + 16)
                    pe.wait_ge(p_done[d], w.n + 1)
                    wait(pe, x_done[d], w.n)
                    nc.tensor.matmul(pnu[d][:, :], pr[:, d, :], vt[:, d, w.s, :], start=True, stop=True).then_inc(intra_done[d], 1)

                def own_state(w, d):
                    s = w.s
                    pe.wait_ge(ke_done[d], w.n + 1)
                    if w.ctx and d == 0:
                        wait(pe, c_updated[1], w.l)
                    elif w.ctx:
                        pe.wait_ge(ctx_c_taken, 2 * w.h + 1)
                    elif d == 0:
                        pe.wait_ge(ctx_c_taken, 2 * w.h + 2)
                        wait(pe, c_updated[1], w.l)
                    else:
                        pe.wait_ge(c_updated[0], w.l + 1)
                    for a in range(HT):
                        if w.ctx:
                            nc.tensor.matmul(pc[:, a, 0:DH], vt[:, d, s, a * P:(a + 1) * P], ke[:, d, :], start=True, stop=True)
                            last = nc.tensor.matmul(pc[:, a, DH:DE], ke[:, d, a * P:(a + 1) * P], vt[:, d, s, DH:DE],
                                                    start=True, stop=True)
                        else:
                            last = nc.tensor.matmul(pc[:, a, 0:DE], ke[:, d, a * P:(a + 1) * P], vt[:, d, s, :],
                                                    start=True, stop=True)
                    last.then_inc(c_done[d][s], 1)

                def turn(cur, nxt, prev):
                    for d in range(2):
                        if cur and not cur.ctx:
                            from_state(cur, d)
                        if cur:
                            within(cur, d)
                    if cur:
                        own_state(cur, 0)
                    if prev and prev.finish:
                        for d in prev.finish:
                            pe.wait_ge(h_done[d], prev.n + 1)
                        wait(pe, gated, prev.t)
                        for d in prev.finish:
                            for a in range(HT):
                                last = nc.tensor.transpose(phT[:, d, a, :], hs[:, d, a * P:(a + 1) * P], ident[:, :])
                        last.then_inc(hT_done, 1)
                    if nxt:
                        scores(nxt, 0)
                    if cur:
                        own_state(cur, 1)
                    if nxt:
                        scores(nxt, 1)
                walk(pe, turn)

            @block.vector
            def _(dve):
                def exponents(w, d):
                    s = w.s
                    wait_alone(dve, r_loaded[d][s], 16 * w.uses + 16)
                    nc.vector.scalar_tensor_tensor(out=rt[:, d, s, :], in0=rt[:, d, s, :], scalar=col(w, d, 0), in1=mask[:, d, :],
                                                   op0=ALU.add, op1=ALU.add).then_inc(masked[d], 1)

                def probs(w, d):
                    dve.wait_ge(sk_done[d], w.n + 1)
                    dve.wait_ge(e_done[d], w.n + 1)
                    wait(dve, intra_done[d], w.n)
                    nc.vector.tensor_tensor(pr[:, d, :], psk[d][:, 0, :], rt[:, d, w.s, :], ALU.mult).then_inc(p_done[d], 1)

                def update(w, d):
                    dve.wait_ge(c_done[d][w.s], w.uses + 1)
                    if w.ctx:
                        if d == 0:
                            wait(dve, ctx_stored, 64 * w.h)
                        else:
                            dve.wait_ge(ctx_stored, 64 * w.h + 32)
                        nc.vector.tensor_copy(cc[:, :, :], pc[:, :, 0:DE]).then_inc(ctx_c_taken, 1)
                    else:
                        Cs = C[:, bass.ds(H * d + w.h, 1), :, :].rearrange("p a b n -> p (a b) n")
                        nc.vector.scalar_tensor_tensor(out=Cs, in0=Cs,
                                                       scalar=flat(spb[:, bass.ds(H * d + w.h, 1), bass.ds(w.c[d], 1)]),
                                                       in1=pc[:, :, 0:DE], op0=ALU.mult, op1=ALU.add).then_inc(c_updated[d], 1)

                def num(w, d):
                    dve.wait_ge(intra_done[d], w.n + 1)
                    if w.ctx:
                        nc.vector.tensor_copy(xt[:, d, :], pnu[d][:, :]).then_inc(x_done[d], 1)
                    else:
                        dve.wait_ge(inter_read[d], w.l + 1)
                        nc.vector.tensor_tensor(xt[:, d, :], pnu[d][:, :], it[:, d, :], ALU.add).then_inc(x_done[d], 1)

                def den(w):
                    for d in range(2):
                        wait_alone(dve, x_done[d], w.n + 1)
                        nc.vector.scalar_tensor_tensor(out=dn[:, d, 1:2], in0=xt[:, d, DH:DE], scalar=-1.0, in1=col(w, d, 2),
                                                       op0=ALU.mult, op1=ALU.max).then_inc(neg_done[d], 1)
                    for d in range(2):
                        dve.wait_ge(neg_done[d], w.n + 1)
                        nc.vector.tensor_tensor(dn[:, d, 0:1], dn[:, d, 1:2], xt[:, d, DH:DE], ALU.max).then_inc(den_done[d], 1)
                    for d in range(2):
                        dve.wait_ge(den_done[d], w.n + 1)
                        nc.vector.reciprocal(dn[:, d, 1:2], dn[:, d, 0:1]).then_inc(rec_done[d], 1)

                def out(w, d):
                    dve.wait_ge(rec_done[d], w.n + 1)
                    mine = flat(hst[:, bass.ds(w.c[d], 1), :])
                    if d in w.finish:
                        if w.ctx:
                            dve.wait_ge(h_done[0], w.n + 1)
                        else:
                            dve.wait_ge(h_done[1 - d], w.h * (LAT + 1) + 1 + HALF)
                        wait(dve, hT_done, w.t)
                        nc.vector.scalar_tensor_tensor(out=hs[:, d, :], in0=xt[:, d, 0:DH], scalar=dn[:, d, 1:2], in1=mine,
                                                       op0=ALU.mult, op1=ALU.add).then_inc(h_done[d], 1)
                    else:
                        nc.vector.tensor_scalar(mine, xt[:, d, 0:DH], dn[:, d, 1:2], None, ALU.mult).then_inc(h_done[d], 1)

                def gate(w):
                    dve.wait_ge(hT_done, w.t + 1)
                    for d in w.finish:
                        dve.wait_ge(g_loaded[d][w.gs], 16 * w.g[d] + 16)
                    ds = slice(w.finish[0], 2)
                    nc.vector.tensor_tensor(gt[:, w.gs, ds, :, :], phT[:, ds, :, :], gt[:, w.gs, ds, :, :], ALU.mult
                                            ).then_inc(gated, 1)

                def turn(cur, nxt, prev):
                    if nxt:
                        exponents(nxt, 0)
                        exponents(nxt, 1)
                    if cur:
                        num(cur, 0)
                        num(cur, 1)
                        update(cur, 0)
                        den(cur)
                        out(cur, 0)
                        out(cur, 1)
                    if prev and prev.finish:
                        gate(prev)
                    if nxt:
                        probs(nxt, 0)
                    if cur:
                        update(cur, 1)
                    if nxt:
                        probs(nxt, 1)
                    if prev and prev.ctx:
                        wait_alone(dve, ctx_stored, 64 * prev.h + 64)
                walk(dve, turn)

            @block.scalar
            def _(act):
                def weights(w, d):
                    act.wait_ge(masked[d], w.n + 1)
                    nc.scalar.activation(rt[:, d, w.s, :], rt[:, d, w.s, :], ACT.Exp).then_inc(e_done[d], 1)

                def inter(w, d):
                    act.wait_ge(inter_done[d], w.l + 1)
                    wait(act, x_done[d], w.n)
                    nc.scalar.activation(it[:, d, :], pin[:, :], ACT.Copy, scale=col(w, d, 1)).then_inc(inter_read[d], 1)

                def keys(w, d):
                    act.wait_ge(p_done[d], w.n + 1)
                    if w.ctx:
                        wait(act, c_done[d][1], w.h * HALF)
                    elif w.s == 0:
                        wait(act, c_done[d][1], w.uses)
                        act.wait_ge(c_done[d][2], w.h + 1)
                    else:
                        act.wait_ge(c_done[d][0], w.uses + 1)
                    end = 0 if d else P - 1
                    nc.scalar.activation(ke[:, d, :], psk[d][:, 1:3, :].rearrange("p a t -> p (a t)"), ACT.Copy,
                                         scale=rt[:, d, w.s, end:end + 1]).then_inc(ke_done[d], 1)

                def turn(cur, nxt, prev):
                    if cur and not cur.ctx:
                        inter(cur, 0)
                    if cur:
                        keys(cur, 0)
                        keys(cur, 1)
                    if cur and not cur.ctx:
                        inter(cur, 1)
                    if nxt:
                        weights(nxt, 0)
                        weights(nxt, 1)
                    for d in prev.finish if prev else ():
                        act.wait_ge(gated, prev.t + 1)
                        nc.scalar.activation(out_tile(prev, d, 0), gt[:, prev.gs, d, :, :], ACT.Copy).then_inc(hi_done[d], 1)
                walk(act, turn)

            @block.gpsimd
            def _(pool):
                def turn(cur, nxt, prev):
                    if cur and cur.ctx:
                        for d in range(2):
                            wait_alone(pool, ctx_c_taken, 2 * cur.h + d + 1)
                            pool.dma_start(new_C[0, 0, d][bass.ds(cur.h, 1)].rearrange("a (v p) k -> p (a v) k", p=P),
                                           cc[:, :, 0:DH]).then_inc(ctx_stored, 16)
                            with nc.allow_non_contiguous_dma("normalisers"):
                                pool.dma_start(new_n[0, 0, d][bass.ds(cur.h, 1)].rearrange("a (v p) -> p (a v)", p=P),
                                               cc[:, :, DH]).then_inc(ctx_stored, 16)
                    for d in prev.finish if prev else ():
                        wait_alone(pool, hi_done[d], prev.f[d] + 1)
                        nc.gpsimd.tensor_tensor(out_tile(prev, d, 1), gt[:, prev.gs, d, :, :], out_tile(prev, d, 0).bitcast(F32),
                                                ALU.subtract).then_inc(lo_done[d][prev.gs], 1)
                    for d in nxt.finish if nxt else ():
                        wait_alone(pool, lo_done[d][nxt.gs], nxt.g[d])
                        pool.dma_start(gt[:, nxt.gs, d, :, :], gate_d[bass.ds(HT * nxt.h, HT), :, bass.ds(nxt.c[d] * P, P)]
                                       .rearrange("a p t -> p a t")).then_inc(g_loaded[d][nxt.gs], 16)
                walk(pool, turn)
                pool.wait_ge(ctx_stored, 64 * H)


def out_phase(nc, sem, sb, ps, m_d, w_out, gate_d, x_prompt, x_sample, norm_f, y_prompt, y_sample):
    def two(name):
        return [sem(f"o_{name}{s}") for s in range(2)]
    half_made = sem("o_half_made")
    w_loaded, w_hi, w_lo, const_loaded = two("w_loaded"), sem("o_w_hi"), sem("o_w_lo"), sem("o_const")
    m_loaded, x_loaded, m_hi, m_lo, prod, gated, added, sq_done, var_done, rstd_done, out_done = (
        two(n) for n in ("m_loaded", "x_loaded", "m_hi", "m_lo", "prod", "gated", "added", "sq_done",
                         "var_done", "rstd_done", "out_done"))
    stored = [sem(f"o_stored{s}", software_dma=True) for s in range(2)]
    with ExitStack() as st:
        raw = sb(st, "o_raw", [P, 2, D])
        wsp = sb(st, "o_wsp", [P, 2, KT, D], F32R)
        mt = sb(st, "o_mt", [P, 2, KT, P])
        msp = sb(st, "o_msp", [P, 2, 2, KT, P], F32R)
        xt = sb(st, "o_xt", [P, 2, D])
        yt = sb(st, "o_yt", [P, 2, D])
        ot = sb(st, "o_ot", [P, 2, D])
        sq = sb(st, "o_sq", [P, D])
        ss = sb(st, "o_ss", [P, 2, 4])
        gb = sb(st, "o_gb", [P, 2, D])
        nf = sb(st, "o_nf", [P, D])
        pp = [ps(st, f"o_pp{s}", [P, 2, 512]) for s in range(2)]

        def chunks(eng, step):
            step(0, 0, 0, 0, None)
            with eng.Fori(0, LAT // 2) as i:
                step(1, i, 2 * i + 1, 1, 2 * i)
                step(0, i + 1, 2 * i + 2, 1, 2 * i + 1)

        with nc.Block() as block:
            @block.sync
            def _(sp):
                for k in range(KT):
                    if k >= 2:
                        sp.wait_ge(w_lo, k - 1)
                    sp.dma_start(raw[:, k % 2, :], w_out[k * P:(k + 1) * P, :]).then_inc(w_loaded[k % 2], 16)
                sp.dma_start(gb[:, :, :], gate_d.rearrange("(a j) n -> a j n", a=1).broadcast_to([P, 2, D])).then_inc(const_loaded, 16)
                sp.dma_start(nf[:, :], norm_f.rearrange("(a n) -> a n", a=1).broadcast_to([P, D])).then_inc(const_loaded, 16)

                def step(s, n, c, j, lat):
                    wait_alone(sp, m_lo[s], n)
                    sp.dma_start(mt[:, s, :, :], m_d[:, :, bass.ds(c * P, P)].rearrange("k p t -> p k t")).then_inc(m_loaded[s], 16)
                    wait_alone(sp, added[s], n)
                    sp.dma_start(xt[:, s, :], x_prompt[0] if lat is None else x_sample[0][bass.ds(lat * P, P), :]
                                 ).then_inc(x_loaded[s], 16)
                chunks(sp, step)

            @block.gpsimd
            def _(pool):
                def step(s, n, c, j, lat):
                    wait_alone(pool, var_done[s], n + 1)
                    nc.gpsimd.tensor_tensor(ss[:, s, 2:3], ss[:, s, 1:2], ss[:, s, 3:4], ALU.pow).then_inc(rstd_done[s], 1)
                    wait_alone(pool, out_done[s], n + 1)
                    pool.dma_start(y_prompt[0] if lat is None else y_sample[0][bass.ds(lat * P, P), :], ot[:, s, :]
                                   ).then_inc(stored[s], 16)
                nc.gpsimd.memset(ss[:, :, 3:4], -0.5).then_inc(half_made, 1)
                pool.wait_ge(half_made, 1)
                chunks(pool, step)
                pool.wait_ge(stored[0], 16 * (LAT // 2 + 1))
                pool.wait_ge(stored[1], 16 * (LAT // 2))

            @block.scalar
            def _(act):
                for k in range(KT):
                    act.wait_ge(w_loaded[k % 2], 16 * (k // 2 + 1))
                    nc.scalar.activation(wsp[:, 0, k, :], raw[:, k % 2, :], ACT.Copy).then_inc(w_hi, 1)

                def step(s, n, c, j, lat):
                    act.wait_ge(m_loaded[s], 16 * n + 16)
                    wait(act, prod[s], n)
                    nc.scalar.activation(msp[:, s, 0, :, :], mt[:, s, :, :], ACT.Copy).then_inc(m_hi[s], 1)

                def late(s, n):
                    act.wait_ge(added[s], n + 1)
                    nc.scalar.activation(sq[:, :], yt[:, s, :], ACT.Square, accum_out=ss[:, s, 0:1]).then_inc(sq_done[s], 1)

                step(0, 0, 0, 0, None)
                with act.Fori(0, LAT // 2) as i:
                    step(1, i, 2 * i + 1, 1, 2 * i)
                    late(0, i)
                    step(0, i + 1, 2 * i + 2, 1, 2 * i + 1)
                    late(1, i)
                late(0, LAT // 2)

            @block.tensor
            def _(pe):
                pe.wait_ge(w_lo, KT)

                def step(s, n, c, j, lat):
                    pe.wait_ge(m_lo[s], n + 1)
                    wait(pe, gated[s], n)
                    for half in range(2):
                        for k in range(KT):
                            for q, (mp, wp) in enumerate(((1, 0), (0, 1), (0, 0))):
                                last = nc.tensor.matmul(pp[s][:, half, :], msp[:, s, mp, k, :],
                                                        wsp[:, wp, k, half * 512:(half + 1) * 512],
                                                        start=(k == 0 and q == 0), stop=(k == KT - 1 and q == 2))
                    last.then_inc(prod[s], 1)
                chunks(pe, step)

            @block.vector
            def _(dve):
                for k in range(KT):
                    dve.wait_ge(w_hi, k + 1)
                    nc.vector.tensor_tensor(wsp[:, 1, k, :], raw[:, k % 2, :], wsp[:, 0, k, :].bitcast(F32),
                                            ALU.subtract).then_inc(w_lo, 1)
                dve.wait_ge(const_loaded, 32)

                def step(s, n, c, j, lat):
                    dve.wait_ge(m_hi[s], n + 1)
                    nc.vector.tensor_tensor(msp[:, s, 1, :, :], mt[:, s, :, :], msp[:, s, 0, :, :].bitcast(F32),
                                            ALU.subtract).then_inc(m_lo[s], 1)

                def late(s, n, j):
                    dve.wait_ge(prod[s], n + 1)
                    wait(dve, out_done[s], n)
                    nc.vector.tensor_tensor(yt[:, s, :], pp[s][:, :, :].rearrange("p a n -> p (a n)"), gb[:, j, :],
                                            ALU.mult).then_inc(gated[s], 1)
                    dve.wait_ge(gated[s], n + 1)
                    dve.wait_ge(x_loaded[s], 16 * n + 16)
                    nc.vector.tensor_tensor(yt[:, s, :], yt[:, s, :], xt[:, s, :], ALU.add).then_inc(added[s], 1)
                    dve.wait_ge(sq_done[s], n + 1)
                    nc.vector.tensor_scalar(ss[:, s, 1:2], ss[:, s, 0:1], 1.0 / D, EPS, ALU.mult, ALU.add).then_inc(var_done[s], 1)
                    dve.wait_ge(rstd_done[s], n + 1)
                    wait(dve, stored[s], 16 * n)
                    nc.vector.scalar_tensor_tensor(out=ot[:, s, :], in0=yt[:, s, :], scalar=ss[:, s, 2:3], in1=nf[:, :],
                                                   op0=ALU.mult, op1=ALU.mult).then_inc(out_done[s], 1)

                step(0, 0, 0, 0, None)
                step(1, 0, 1, 1, 0)
                late(0, 0, 0)
                with dve.Fori(0, LAT // 2 - 1) as i:
                    step(0, i + 1, 2 * i + 2, 1, 2 * i + 1)
                    late(1, i, 1)
                    step(1, i + 1, 2 * i + 3, 1, 2 * i + 2)
                    late(0, i + 1, 1)
                step(0, LAT // 2, LAT, 1, LAT - 1)
                late(1, LAT // 2 - 1, 1)
                late(0, LAT // 2, 1)


_INS = ["x_prompt", "x_sample", "c", "state_C", "state_n", "state_m", "c_ctx", "norm_g", "w_ada", "b_ada", "w_in",
        "b_if", "g_sgu", "w_s", "b_s", "w_proj_a", "w_proj_b", "w_out", "norm_f"]
_OUTS = [(1, 128, 1024), (1, 2048, 1024), (1, 1, 2, 4, 256, 256), (1, 1, 2, 4, 256), (1, 1, 2, 4)]


def kernel(**inputs):
    import numpy as _np
    import concourse.bacc as _bacc
    from concourse.bass_utils import run_bass_kernel_spmd as _run

    nc = _bacc.Bacc("TRN2", target_bir_lowering=False, num_devices=1)
    arrays, args = {}, []
    for name in _INS:
        a = _np.ascontiguousarray(inputs[name])
        arrays[f"in_{name}"] = a
        args.append(nc.dram_tensor(f"in_{name}", a.shape, mybir.dt.from_np(a.dtype), kind="ExternalInput").ap())
    for i, shape in enumerate(_OUTS):
        args.append(nc.dram_tensor(f"out_{i}", shape, F32, kind="ExternalOutput").ap())
    build(nc, *args)
    r = _run(nc, [arrays], core_ids=[0])
    return tuple(r.results[0][f"out_{i}"] for i in range(len(_OUTS)))
```

```python
from contextlib import ExitStack

import concourse.bass as bass
from concourse import mybir

F32 = mybir.dt.float32
F32R = mybir.dt.float32r
ALU = mybir.AluOpType
ACT = mybir.ActivationFunctionType

P = 128
D = 1024
KT = D // P
H = 4
DH = D // H
HT = DH // P
N_IF = 2 * 2 * H
CTX = 1
LAT = 16
NC = CTX + LAT
TOK = NC * P
EPS = 1e-6
MASKED = -1.0e30
LOWEST = -3.0e38
NB = -(-TOK // 512)
BLOCK_ENDS = [TOK * (b + 1) // NB // 16 * 16 for b in range(NB)]
BLOCKS = [(lo, hi - lo) for lo, hi in zip([0] + BLOCK_ENDS, BLOCK_ENDS)]
DE = DH + 1

Q0, K0, V0, O0, Z0 = (i * D for i in range(5))
IF0 = 5 * D
U0, VB0, ZB0, GA0, GB0 = (IF0 + N_IF + i * D for i in range(5))


def wait(eng, sem, value):
    if not (isinstance(value, int) and value <= 0):
        eng.wait_ge(sem, value)


passed = []


def wait_alone(eng, sem, value):
    if not isinstance(value, int):
        eng.wait_ge(sem, value)
        eng.sem_inc(passed[-1], 1)
    elif value > 0:
        eng.wait_ge(sem, value)


def build(nc, x_prompt, x_sample, c, state_C, state_n, state_m, c_ctx, norm_g, w_ada, b_ada, w_in, b_if,
          g_sgu, w_s, b_s, w_proj_a, w_proj_b, w_out, norm_f,
          y_prompt, y_sample, new_C, new_n, new_m):
    top = ExitStack()
    held = []

    def sem(name, software_dma=False):
        if software_dma:
            return top.enter_context(nc.semaphore(name))
        made = nc.semaphore(name)
        held.append((made, made.__enter__()))
        return held[-1][1]

    def stage_end():
        with nc.Block() as block:
            @block.gpsimd
            def _(pool):
                for _, s in held:
                    pool.sem_clear(s)
        while held:
            held.pop()[0].__exit__(None, None, None)

    def sb(stack, name, shape, dt=F32):
        return stack.enter_context(nc.sbuf_tensor(name, shape, dt))

    def ps(stack, name, shape):
        return stack.enter_context(nc.psum_tensor(name, shape, F32))

    def dram(name, shape):
        return nc.dram_tensor(name, shape, F32, kind="Internal").ap()

    w_in2 = w_in[0]
    qk_d = dram("qk_d", [KT, 2, P, TOK])
    gateA_d, u_d, sga_d, sgb_d, m_d = (
        dram(n, [KT, P, TOK]) for n in
        ("gateA_d", "u_d", "sga_d", "sgb_d", "m_d"))
    v_d = dram("v_d", [TOK, D])
    vb_d = dram("vb_d", [TOK, D])
    if_d = dram("if_d", [N_IF, TOK])
    cols_d = dram("cols_d", [6 * H, TOK])
    r_d = dram("r_d", [2 * H, TOK])
    sp_d = dram("sp_d", [2 * H, NC])
    ends_d = dram("ends_d", [2, 2, H, NC])
    before_d = dram("before_d", [2, H, NC])
    gate_d = dram("gate_d", [2, D])

    with top:
        passed.append(top.enter_context(nc.semaphore("passed")))
        ident = sb(top, "ident", [P, P])
        mask = sb(top, "mask", [P, 2, P])
        modT = sb(top, "modT", [P, 3 * KT, 2])
        modA = sb(top, "modA", [P, KT, 2])
        with ExitStack() as st:
            hsp = sb(st, "hsp", [P, 2, KT, TOK], F32R)
            norm_phase(nc, sem, sb, ps, x_prompt, x_sample, c, c_ctx, w_ada, b_ada, norm_g, gate_d,
                       ident, mask, modT, modA, hsp)
            stage_end()
            gates = GateRows(nc, sem, sb, st, if_d, b_if, state_m, ends_d, before_d, cols_d, r_d, sp_d, new_m)
            streamed_products(nc, sem, sb, ps, "p", hsp, [
                Phase("if", w_in2, [IF0], [if_d]),
                Phase("qk", w_in2, [Q0, K0], [qk_d[:, 0], qk_d[:, 1]]),
                Phase("oz", w_in2, [O0, Z0], [gateA_d]),
                Phase("uz", w_in2, [U0, ZB0], [u_d]),
                Phase("gg", w_in2, [GA0, GB0], [sga_d, sgb_d]),
                Phase("nat", w_in2, [V0, VB0], [v_d, vb_d])], gates)
            stage_end()
        cols = sb(top, "cols", [P, NC, 6 * H])
        spb = sb(top, "spb", [P, 2 * H, NC])
        with ExitStack() as st:
            ysp = sb(st, "ysp", [P, 2, KT, TOK], F32R)
            sgu_phase(nc, sem, sb, ps, vb_d, u_d, w_s, b_s, g_sgu, cols_d, sp_d, ident, cols, spb, ysp)
            stage_end()
            streamed_products(nc, sem, sb, ps, "b", ysp, [Phase("mg", w_proj_b[0], [0], [m_d], gain=sgb_d)])
            stage_end()
            mlstm_phase(nc, sem, sb, ps, qk_d, v_d, gateA_d, r_d, state_C, state_n, new_C, new_n,
                        ident, mask, cols, spb, ysp)
            stage_end()
            streamed_products(nc, sem, sb, ps, "a", ysp,
                              [Phase("mg", w_proj_a[0], [0], [m_d], gain=sga_d, add=True)])
            stage_end()
        out_phase(nc, sem, sb, ps, m_d, w_out[0], gate_d, x_prompt, x_sample, norm_f, y_prompt, y_sample)


def norm_phase(nc, sem, sb, ps, x_prompt, x_sample, c, c_ctx, w_ada, b_ada, norm_g, gate_d,
               ident, mask, modT, modA, hsp):
    def two(name):
        return [sem(f"n_{name}{s}") for s in range(2)]
    const_made, c_loaded, sig_done, silu_done = (sem(f"n_{n}") for n in ("const_made", "c_loaded", "sig_done", "silu_done"))
    mod_taken, mod_turned, mod_biased, mod_ready, gate_stored = (
        sem(f"n_{n}") for n in ("mod_taken", "mod_turned", "mod_biased", "mod_ready", "gate_stored"))
    wada_loaded, mod_mm = two("wada_loaded"), two("mod_mm")
    x_loaded, sq_done, var_done, rstd_done, scaled, turned, modulated, hi_done, lo_done = (
        two(n) for n in ("x_loaded", "sq_done", "var_done", "rstd_done", "scaled", "turned", "modulated",
                         "hi_done", "lo_done"))
    GRP = 4
    NG = 3 * KT // GRP
    with ExitStack() as st:
        cT = sb(st, "n_cT", [P, KT, 2])
        csig = sb(st, "n_csig", [P, KT, 2])
        csil = sb(st, "n_csil", [P, KT, 2])
        wada = sb(st, "n_wada", [P, 2, KT, GRP * P])
        rows = sb(st, "n_rows", [2, 2, GRP * P])
        badaT = sb(st, "n_badaT", [P, 3 * KT])
        gT = sb(st, "n_gT", [P, KT])
        xt = sb(st, "n_xt", [P, 2, D])
        sq = sb(st, "n_sq", [P, D])
        ss = sb(st, "n_ss", [P, 2, 4])
        hx = sb(st, "n_hx", [P, 2, KT, P])
        prow = ps(st, "n_prow", [2, 2, GRP * P])
        pmod = ps(st, "n_pmod", [P, 3 * KT, 2])
        pt = [ps(st, f"n_pt{s}", [P, KT, P]) for s in range(2)]

        def none(s, n, c, stream, t0):
            pass

        def chunks(eng, front=none, last=none, scale=none, middle=none, end=none):
            def latent(step, s, n, c):
                step(s, n, c, 1, (c + CTX) * P)
            front(0, 0, None, 0, 0)
            scale(0, 0, None, 0, 0)
            latent(front, 1, 0, 0)
            latent(scale, 1, 0, 0)
            middle(0, 0, None, 0, 0)
            latent(front, 0, 1, 1)
            last(0, 0, None, 0, 0)
            latent(scale, 0, 1, 1)
            latent(middle, 1, 0, 0)
            end(0, 0, None, 0, 0)
            with eng.Fori(0, LAT // 2 - 1) as i:
                latent(front, 1, i + 1, 2 * i + 2)
                latent(last, 1, i, 2 * i)
                latent(scale, 1, i + 1, 2 * i + 2)
                latent(middle, 0, i + 1, 2 * i + 1)
                latent(end, 1, i, 2 * i)
                latent(front, 0, i + 2, 2 * i + 3)
                latent(last, 0, i + 1, 2 * i + 1)
                latent(scale, 0, i + 2, 2 * i + 3)
                latent(middle, 1, i + 1, 2 * i + 2)
                latent(end, 0, i + 1, 2 * i + 1)
            latent(last, 1, LAT // 2 - 1, LAT - 2)
            latent(middle, 0, LAT // 2, LAT - 1)
            latent(end, 1, LAT // 2 - 1, LAT - 2)
            latent(last, 0, LAT // 2, LAT - 1)
            latent(end, 0, LAT // 2, LAT - 1)

        with nc.Block() as block:
            @block.sync
            def _(sp):
                with nc.allow_non_contiguous_dma("vectors onto partitions"):
                    sp.dma_start(cT[:, :, 0], c_ctx.rearrange("(k p) -> p k", p=P)).then_inc(c_loaded, 16)
                    sp.dma_start(cT[:, :, 1], c[0].rearrange("(k p) -> p k", p=P)).then_inc(c_loaded, 16)
                for g in range(NG):
                    s = g % 2
                    if g >= 2:
                        sp.wait_ge(mod_mm[s], g // 2)
                    sp.dma_start(wada[:, s, :, :],
                                 w_ada[0][:, g * GRP * P:(g + 1) * GRP * P].rearrange("(k p) n -> p k n", p=P)
                                 ).then_inc(wada_loaded[s], 16)
                with nc.allow_non_contiguous_dma("vectors onto partitions"):
                    sp.dma_start(badaT[:, :], b_ada[0].rearrange("(k p) -> p k", p=P)).then_inc(c_loaded, 16)
                    sp.dma_start(gT[:, :], norm_g[0].rearrange("(k p) -> p k", p=P)).then_inc(c_loaded, 16)

                def load(s, n, c, stream, t0):
                    wait_alone(sp, turned[s], n)
                    src = x_prompt[0] if c is None else x_sample[0][bass.ds(c * P, P), :]
                    sp.dma_start(xt[:, s, :], src).then_inc(x_loaded[s], 16)
                chunks(sp, front=load)
                with nc.allow_non_contiguous_dma("gate rows"):
                    for j in range(2):
                        sp.wait_ge(mod_ready, 2)
                        sp.dma_start(gate_d[j].rearrange("(k p) -> p k", p=P),
                                     modT[:, 2 * KT:, j]).then_inc(gate_stored, 16)
                sp.wait_ge(gate_stored, 32)

            @block.gpsimd
            def _(pool):
                nc.gpsimd.memset(ident[:, :], 0.0).then_inc(const_made, 1)
                nc.gpsimd.memset(mask[:, :, :], 0.0).then_inc(const_made, 1)
                nc.gpsimd.memset(ss[:, :, 3:4], -0.5).then_inc(const_made, 1)
                pool.wait_ge(const_made, 3)
                nc.gpsimd.affine_select(out=ident[:, :], in_=ident[:, :], compare_op=ALU.not_equal,
                                        fill=1.0, base=0, pattern=[[-1, P]],
                                        channel_multiplier=1).then_inc(const_made, 1)
                nc.gpsimd.affine_select(out=mask[:, 0, :], in_=mask[:, 0, :], compare_op=ALU.is_ge,
                                        fill=MASKED, base=0, pattern=[[1, P]],
                                        channel_multiplier=-1).then_inc(const_made, 1)
                nc.gpsimd.affine_select(out=mask[:, 1, :], in_=mask[:, 1, :], compare_op=ALU.is_ge,
                                        fill=MASKED, base=0, pattern=[[-1, P]],
                                        channel_multiplier=1).then_inc(const_made, 1)

                def rstd(s, n, c, stream, t0):
                    wait_alone(pool, var_done[s], n + 1)
                    nc.gpsimd.tensor_tensor(ss[:, s, 2:3], ss[:, s, 1:2], ss[:, s, 3:4], ALU.pow).then_inc(rstd_done[s], 1)
                chunks(pool, front=rstd)

            @block.scalar
            def _(act):
                act.wait_ge(c_loaded, 32)
                nc.scalar.activation(csig[:, :, :], cT[:, :, :], ACT.Sigmoid).then_inc(sig_done, 1)

                def square(s, n, c, stream, t0):
                    act.wait_ge(x_loaded[s], (n + 1) * 16)
                    nc.scalar.activation(sq[:, :], xt[:, s, :], ACT.Square, accum_out=ss[:, s, 0:1]).then_inc(sq_done[s], 1)

                def scale(s, n, c, stream, t0):
                    act.wait_ge(rstd_done[s], n + 1)
                    nc.scalar.activation(xt[:, s, :], xt[:, s, :], ACT.Copy, scale=ss[:, s, 2:3]).then_inc(scaled[s], 1)

                def high(s, n, c, stream, t0):
                    act.wait_ge(modulated[s], n + 1)
                    nc.scalar.activation(hsp[:, 0, :, bass.ds(t0, P)], hx[:, s, :, :], ACT.Copy).then_inc(hi_done[s], 1)
                chunks(act, front=square, last=high, scale=scale)

            @block.vector
            def _(dve):
                dve.wait_ge(sig_done, 1)
                nc.vector.tensor_tensor(csil[:, :, :], cT[:, :, :], csig[:, :, :], ALU.mult).then_inc(silu_done, 1)
                for g in range(NG):
                    dve.wait_ge(mod_mm[g % 2], g // 2 + 1)
                    if g >= 2:
                        dve.wait_ge(mod_turned, g - 1)
                    nc.vector.tensor_copy(rows[:, g % 2, :], prow[:, g % 2, :]).then_inc(mod_taken, 1)
                dve.wait_ge(mod_turned, NG)
                dve.wait_ge(c_loaded, 64)
                nc.vector.tensor_tensor(modT[:, :, :], pmod[:, :, :],
                                        badaT[:, :].unsqueeze(2).broadcast_to([P, 3 * KT, 2]),
                                        ALU.add).then_inc(mod_biased, 1)
                dve.wait_ge(mod_biased, 1)
                for j in range(2):
                    nc.vector.scalar_tensor_tensor(out=modA[:, :, j], in0=modT[:, KT:2 * KT, j], scalar=1.0,
                                                   in1=gT[:, :], op0=ALU.add, op1=ALU.mult).then_inc(mod_ready, 1)
                dve.wait_ge(mod_ready, 2)

                def variance(s, n, c, stream, t0):
                    dve.wait_ge(sq_done[s], n + 1)
                    nc.vector.tensor_scalar(ss[:, s, 1:2], ss[:, s, 0:1], 1.0 / D, EPS, ALU.mult, ALU.add).then_inc(var_done[s], 1)

                def modulate(s, n, c, stream, t0):
                    dve.wait_ge(turned[s], n + 1)
                    wait(dve, lo_done[s], n)
                    for k in range(KT):
                        last = nc.vector.tensor_scalar(hx[:, s, k, :], pt[s][:, k, :], modA[:, k, stream:stream + 1],
                                                       modT[:, k, stream:stream + 1], ALU.mult, ALU.add)
                    last.then_inc(modulated[s], 1)

                def low(s, n, c, stream, t0):
                    dve.wait_ge(hi_done[s], n + 1)
                    nc.vector.tensor_tensor(hsp[:, 1, :, bass.ds(t0, P)], hx[:, s, :, :],
                                            hsp[:, 0, :, bass.ds(t0, P)].bitcast(F32), ALU.subtract).then_inc(lo_done[s], 1)
                chunks(dve, front=variance, middle=modulate, end=low)

            @block.tensor
            def _(pe):
                def turn_mod(g):
                    pe.wait_ge(mod_taken, g + 1)
                    for n in range(GRP):
                        last = nc.tensor.transpose(pmod[:, g * GRP + n, :], rows[:, g % 2, n * P:(n + 1) * P], ident[0:2, 0:2])
                    last.then_inc(mod_turned, 1)
                pe.wait_ge(silu_done, 1)
                pe.wait_ge(const_made, 6)
                for g in range(NG):
                    s = g % 2
                    pe.wait_ge(wada_loaded[s], 16 * (g // 2 + 1))
                    if g >= 2:
                        pe.wait_ge(mod_taken, g - 1)
                    for k in range(KT):
                        last = nc.tensor.matmul(prow[:, s, :], csil[:, k, :], wada[:, s, k, :], start=(k == 0), stop=(k == KT - 1))
                    last.then_inc(mod_mm[s], 1)
                    if g:
                        turn_mod(g - 1)
                turn_mod(NG - 1)

                def turn(s, n, c, stream, t0):
                    pe.wait_ge(scaled[s], n + 1)
                    wait(pe, modulated[s], n)
                    for k in range(KT):
                        last = nc.tensor.transpose(pt[s][:, k, :], xt[:, s, k * P:(k + 1) * P], ident[:, :])
                    last.then_inc(turned[s], 1)
                chunks(pe, middle=turn)
NP = 4
SETS = 2


class Phase:

    def __init__(self, kind, w, cols, outs, gain=None, add=False):
        self.kind, self.w, self.cols, self.outs, self.gain, self.add = kind, w, cols, outs, gain, add
        self.iters = {"if": 1, "nat": H, "mg": KT // (2 * SETS)}.get(kind, KT // SETS)
        blocks = (NC + 1) // 2 if kind == "nat" else NB
        self.last = blocks - 1
        self.steps = [(e, b) for e in ((1,) if kind == "if" else (0, 1)) for b in range(blocks)]
        self.n_ready = 1 if kind in ("if", "oz", "uz") else 2
        self.n_sig = {"oz": 2, "uz": 1, "mg": 32}.get(kind, 0)
        self.n_part = {"oz": 1, "uz": 1}.get(kind, 0)
        self.n_stored = 16 if kind in ("if", "oz", "uz", "nat") else 32

    def columns(self, e, i):
        if self.kind == "if":
            at = [IF0, IF0 + P]
        elif self.kind == "nat":
            at = [self.cols[e] + DH * i, self.cols[e] + DH * i + P]
        elif self.kind == "mg":
            at = [(4 * i + 2 * e) * P, (4 * i + 2 * e + 1) * P]
        else:
            at = [c0 + (2 * i + e) * P for c0 in self.cols]
        return [self.w[:, bass.ds(a, P)] for a in at]


class Count:

    def __init__(self, base, per):
        self.base, self.per = base, per

    def at(self, i, more=0):
        return self.base + more + (self.per * i if self.per else 0)


class Step:
    def __init__(self, e, b, p, done, ready, sig, part, stored):
        self.e, self.b, self.p = e, b, p
        self.done, self.ready, self.sig, self.part, self.stored = done, ready, sig, part, stored


def plan(phases):
    names = ("done", "ready", "sig", "part", "stored")
    base = {n: [0] * NP for n in names}
    used = [0] * SETS
    out = []
    for ph in phases:
        def adds(n, b):
            return {"done": 0 if b == ph.last else 1, "ready": ph.n_ready, "sig": ph.n_sig,
                    "part": ph.n_part, "stored": ph.n_stored}[n]
        per = {n: [sum(adds(n, b) for _, b in ph.steps[p::NP]) for p in range(NP)] for n in names}
        so_far = {n: [0] * NP for n in names}
        steps = []
        for at, (e, b) in enumerate(ph.steps):
            p = at % NP
            steps.append(Step(e, b, p, *(Count(base[n][p] + so_far[n][p], per[n][p]) for n in names)))
            for n in names:
                so_far[n][p] += adds(n, b)
        out.append((ph, steps, list(used)))
        for n in names:
            for p in range(NP):
                base[n][p] += per[n][p] * ph.iters
        for e in {e for e, _ in ph.steps}:
            used[e] += ph.iters
    return out, base["stored"]


def streamed_products(nc, sem, sb, ps, tag, res, phases, gates=None):
    planned, stored_total = plan(phases)
    raw_loaded = sem(f"{tag}_raw_loaded")
    w_hi = sem(f"{tag}_w_hi")
    w_all_lo = sem(f"{tag}_w_lo")
    w_used = [sem(f"{tag}_w_used{e}") for e in range(SETS)]
    blk_done = [sem(f"{tag}_blk_done{p}") for p in range(NP)]
    ready = [sem(f"{tag}_ready{p}") for p in range(NP)]
    sig = [sem(f"{tag}_sig{p}") for p in range(NP)]
    part = [sem(f"{tag}_part{p}") for p in range(NP)]
    stored = [sem(f"{tag}_stored{p}", software_dma=True) for p in range(NP)]
    starts_with_if = phases[0].kind == "if"

    with ExitStack() as st:
        raw = sb(st, f"{tag}_raw", [P, KT, 2 * P])
        wsp = sb(st, f"{tag}_wsp", [P, SETS, 2, KT, 2 * P], F32R)
        stage = sb(st, f"{tag}_stage", [P, NP, 2, 512])
        bank = [[ps(st, f"{tag}_ps{p}{s}", [P, 512]) for s in range(2)] for p in range(NP)]

        def walk(eng, body, after=None):
            for ph, steps, used in planned:
                if ph.iters == 1:
                    for s in steps:
                        body(ph, s, 0, used)
                else:
                    with eng.Fori(0, ph.iters) as i:
                        for s in steps:
                            body(ph, s, i, used)
                if after:
                    after(ph.kind)

        def wait_products(eng, ph, s, i, used):
            if s.b == ph.last:
                eng.wait_ge(w_used[s.e], used[s.e] + i + 1)
            else:
                eng.wait_ge(blk_done[s.p], s.done.at(i, 1))

        def look_ahead(ph, s, i, used, split):
            if s.b != 1:
                return
            if ph.kind == "if":
                split(0, used[0], 1)
            elif s.e == 0:
                split(1, used[1] + i, used[0] + used[1] + 2 * i + 1)
            else:
                split(0, used[0] + i + 1, used[0] + used[1] + 2 * i + 2)

        with nc.Block() as block:
            @block.sync
            def _(sp):
                def load(n, columns):
                    wait_alone(sp, w_all_lo, n)
                    for h, src in enumerate(columns):
                        sp.dma_start(raw[:, :, h * P:(h + 1) * P],
                                     src.rearrange("(k p) n -> p k n", p=P)).then_inc(raw_loaded, 16)
                first = phases[0]
                load(0, first.columns(1 if starts_with_if else 0, 0))
                for at, (ph, steps, used) in enumerate(planned):
                    follow = phases[at + 1] if at + 1 < len(phases) else ph
                    n = used[0] + used[1]
                    if ph.kind == "if":
                        load(1, follow.columns(0, 0))
                        continue
                    if ph.iters > 1:
                        with sp.Fori(0, ph.iters - 1) as i:
                            load(n + 2 * i + 1, ph.columns(1, i))
                            load(n + 2 * i + 2, ph.columns(0, i + 1))
                    i = ph.iters - 1
                    load(n + 2 * i + 1, ph.columns(1, i))
                    load(n + 2 * i + 2, follow.columns(0, 0))
                    if gates:
                        if ph.kind == "qk":
                            for p in range(NP):
                                sp.wait_ge(stored[p], 16 * sum(b % NP == p for b in range(NB)))
                        gates.sync(sp, ph.kind)

            @block.scalar
            def _(act):
                def split(e, n, n_all):
                    act.wait_ge(raw_loaded, 32 * (n_all + 1))
                    wait(act, w_used[e], n)
                    nc.scalar.activation(wsp[:, e, 0, :, :], raw[:, :, :], ACT.Copy).then_inc(w_hi, 1)

                def body(ph, s, i, used):
                    look_ahead(ph, s, i, used, split)
                    r, kind = s.p, ph.kind
                    if kind == "if":
                        return
                    if kind == "mg":
                        wait(act, stored[r], s.stored.at(i))
                        t0, width = BLOCKS[s.b]
                        for h in range(2):
                            act.dma_start(stage[:, r, h, 0:width],
                                          ph.gain[bass.ds(4 * i + 2 * s.e + h, 1), :, t0:t0 + width]
                                          .rearrange("a p t -> p (a t)")).then_inc(sig[r], 16)
                        return
                    wait_products(act, ph, s, i, used)
                    wait(act, stored[r], s.stored.at(i))
                    width = DH if kind == "nat" else BLOCKS[s.b][1]
                    A, B = (bank[r][h][:, 0:width] for h in range(2))
                    s0, s1 = (stage[:, r, h, 0:width] for h in range(2))
                    if kind == "nat":
                        alone = s.b == ph.last
                        nc.scalar.activation(s0, A, ACT.Copy).then_inc(ready[r], 2 if alone else 1)
                    elif kind == "qk":
                        nc.scalar.activation(s0, A, ACT.Copy, scale=DH ** -0.5).then_inc(ready[r], 1)
                    elif kind == "gg":
                        nc.scalar.activation(s0, A, ACT.Sigmoid).then_inc(ready[r], 1)
                        nc.scalar.activation(s1, B, ACT.Sigmoid).then_inc(ready[r], 1)
                    elif kind == "oz":
                        nc.scalar.activation(s0, A, ACT.Sigmoid).then_inc(sig[r], 1)
                        nc.scalar.activation(s1, B, ACT.Sigmoid).then_inc(sig[r], 1)
                    else:
                        nc.scalar.activation(s1, B, ACT.Sigmoid).then_inc(sig[r], 1)
                split(1 if starts_with_if else 0, 0, 0)
                walk(act, body, gates and (lambda kind: gates.scalar(act, kind)))

            @block.vector
            def _(dve):
                def split(e, n, n_all):
                    dve.wait_ge(w_hi, n_all + 1)
                    nc.vector.tensor_tensor(wsp[:, e, 1, :, :], raw[:, :, :],
                                            wsp[:, e, 0, :, :].bitcast(F32), ALU.subtract).then_inc(w_all_lo, 1)

                def body(ph, s, i, used):
                    look_ahead(ph, s, i, used, split)
                    r, kind = s.p, ph.kind
                    width = DH if kind == "nat" else BLOCKS[s.b][1]
                    A, B = (bank[r][h][:, 0:width] for h in range(2))
                    s0, s1 = (stage[:, r, h, 0:width] for h in range(2))
                    if kind == "if":
                        wait_products(dve, ph, s, i, used)
                        wait(dve, stored[r], s.stored.at(i))
                        nc.vector.tensor_copy(stage[0:N_IF, r, 0, 0:width], bank[r][0][0:N_IF, 0:width]
                                              ).then_inc(ready[r], 1)
                    elif kind == "qk" or kind == "nat":
                        if kind == "nat" and s.b == ph.last:
                            return
                        wait_products(dve, ph, s, i, used)
                        wait(dve, stored[r], s.stored.at(i))
                        nc.vector.tensor_copy(s1, B).then_inc(ready[r], 1)
                    elif kind == "oz":
                        dve.wait_ge(sig[r], s.sig.at(i, 2))
                        nc.vector.tensor_tensor(s1, s1, B, ALU.mult).then_inc(part[r], 1)
                        dve.wait_ge(part[r], s.part.at(i, 1))
                        nc.vector.tensor_tensor(s0, s0, s1, ALU.mult).then_inc(ready[r], 1)
                    elif kind == "uz":
                        dve.wait_ge(sig[r], s.sig.at(i, 1))
                        nc.vector.tensor_tensor(s1, s1, B, ALU.mult).then_inc(part[r], 1)
                        dve.wait_ge(part[r], s.part.at(i, 1))
                        nc.vector.tensor_tensor(s0, s1, A, ALU.mult).then_inc(ready[r], 1)
                    elif kind == "mg":
                        dve.wait_ge(sig[r], s.sig.at(i, 32))
                        wait_products(dve, ph, s, i, used)
                        nc.vector.tensor_tensor(s0, s0, A, ALU.mult).then_inc(ready[r], 1)
                        nc.vector.tensor_tensor(s1, s1, B, ALU.mult).then_inc(ready[r], 1)
                split(1 if starts_with_if else 0, 0, 0)
                walk(dve, body, gates and (lambda kind: gates.vector(dve, kind)))

            @block.tensor
            def _(pe):
                def body(ph, s, i, used):
                    if s.b == 0:
                        loads = (0 if ph.kind == "if" else used[0] + used[1] + 2 * i + s.e)
                        pe.wait_ge(w_all_lo, loads + 1)
                    wait(pe, ready[s.p], s.ready.at(i))
                    for h in range(1 if ph.kind == "if" else 2):
                        if ph.kind == "nat" and 2 * s.b + h >= NC:
                            continue
                        for k in range(KT):
                            for j, (wp, rp) in enumerate(((1, 0), (0, 1), (0, 0))):
                                flags = dict(start=(k == 0 and j == 0), stop=(k == KT - 1 and j == 2))
                                if ph.kind == "nat":
                                    t0 = (2 * s.b + h) * P
                                    last = nc.tensor.matmul(bank[s.p][h][:, 0:DH], res[:, rp, k, t0:t0 + P],
                                                            wsp[:, s.e, wp, k, :], **flags)
                                else:
                                    t0, width = BLOCKS[s.b]
                                    last = nc.tensor.matmul(bank[s.p][h][:, 0:width],
                                                            wsp[:, s.e, wp, k, h * P:(h + 1) * P],
                                                            res[:, rp, k, t0:t0 + width], **flags)
                    last.then_inc(w_used[s.e] if s.b == ph.last else blk_done[s.p], 1)
                walk(pe, body)

            @block.gpsimd
            def _(pool):
                def body(ph, s, i, used):
                    r, kind = s.p, ph.kind
                    wait_alone(pool, ready[r], s.ready.at(i, ph.n_ready))
                    if kind == "if":
                        t0, width = BLOCKS[s.b]
                        pool.dma_start(ph.outs[0][:, t0:t0 + width], stage[0:N_IF, r, 0, 0:width]
                                       ).then_inc(stored[r], 16)
                    elif kind == "nat":
                        n = min(2, NC - 2 * s.b)
                        pool.dma_start(ph.outs[s.e][2 * s.b * P:(2 * s.b + n) * P, bass.ds(DH * i, DH)]
                                       .rearrange("(c p) n -> p c n", p=P),
                                       stage[:, r, 0:n, 0:DH]).then_inc(stored[r], 16)
                    else:
                        t0, width = BLOCKS[s.b]
                        for h in range(ph.n_stored // 16):
                            out = ph.outs[0] if kind == "mg" else ph.outs[h]
                            tile = 4 * i + 2 * s.e + h if kind == "mg" else 2 * i + s.e
                            more = dict(accum_op=ALU.add) if ph.add else {}
                            pool.dma_start(out[bass.ds(tile, 1), :, t0:t0 + width].rearrange("a p t -> p (a t)"),
                                           stage[:, r, h, 0:width], **more).then_inc(stored[r], 16)
                walk(pool, body)
                for p in range(NP):
                    pool.wait_ge(stored[p], stored_total[p])


class GateRows:

    def __init__(self, nc, sem, sb, st, if_d, b_if, state_m, ends_d, before_d, cols_d, r_d, sp_d, new_m):
        self.nc, self.if_d, self.b_if, self.state_m = nc, if_d, b_if, state_m
        self.ends_d, self.before_d, self.cols_d, self.r_d, self.sp_d, self.new_m = ends_d, before_d, cols_d, r_d, sp_d, new_m
        R = H * NC
        self.li, self.lf, self.t, self.b, self.g, self.sc, self.em = (
            sb(st, f"g_{n}", [R, 2, P]) for n in ("li", "lf", "t", "b", "g", "sc", "em"))
        self.ones, self.zeros = sb(st, "g_ones", [R, P]), sb(st, "g_zeros", [R, P])
        self.bias = sb(st, "g_bias", [R, 2, 2])
        self.ends = sb(st, "g_ends", [R, 2, 2])
        self.ends_h = sb(st, "g_ends_h", [H, 2, 2, NC])
        self.m0 = sb(st, "g_m0", [H, 2])
        self.m_h = sb(st, "g_m_h", [H, 2, NC])
        self.ms_h = sb(st, "g_ms_h", [H, 2, NC])
        self.ms = sb(st, "g_ms", [R, 2])
        self.loaded, self.chain, self.exps, self.ends_there, self.before_there, self.stored = (
            sem(f"g_{n}") for n in ("loaded", "chain", "exps", "ends_there", "before_there", "stored"))

    def sync(self, sp, kind):
        nc, by_row = self.nc, "(d h) (c t) -> (h c) d t"
        if kind == "qk":
            with nc.allow_non_contiguous_dma("small vectors"):
                for h in range(H):
                    sp.dma_start(self.bias[h * NC:(h + 1) * NC, :, :],
                                 self.b_if[0][:, :, h].rearrange("(a d) g -> a d g", a=1).broadcast_to([NC, 2, 2])
                                 ).then_inc(self.loaded, 16)
                sp.dma_start(self.m0[:, :], self.state_m[0, 0].rearrange("d h -> h d")).then_inc(self.loaded, 16)
            rows = self.if_d.rearrange("(d g h) (c t) -> g (h c) d t", d=2, g=2, t=P)
            sp.dma_start(self.li[:, :, :], rows[0]).then_inc(self.loaded, 16)
            sp.dma_start(self.lf[:, :, :], rows[1]).then_inc(self.loaded, 16)
        elif kind == "oz":
            sp.wait_ge(self.chain, 8)
            with nc.allow_non_contiguous_dma("one value of a row"):
                sp.dma_start(self.ends_d.rearrange("d e h c -> (h c) (d e)"), self.ends.rearrange("r d e -> r (d e)")
                             ).then_inc(self.stored, 16)
            sp.wait_ge(self.stored, 16)
            sp.dma_start(self.ends_h.rearrange("h d e c -> h (d e) c"), self.ends_d.rearrange("d e h c -> h (d e) c")
                         ).then_inc(self.ends_there, 16)
        elif kind == "uz":
            sp.wait_ge(self.chain, 10)
            sp.dma_start(self.before_d.rearrange("d h c -> h d c"), self.ms_h[:, :, :]).then_inc(self.stored, 16)
            with nc.allow_non_contiguous_dma("one value of a row"):
                sp.dma_start(self.new_m[0, 0].rearrange("d h -> h d"), self.m_h[:, :, 0]).then_inc(self.stored, 16)
                sp.wait_ge(self.stored, 48)
                sp.dma_start(self.ms[:, :], self.before_d.rearrange("d h c -> (h c) d")).then_inc(self.before_there, 16)
        elif kind == "gg":
            sp.wait_ge(self.chain, 13)
            sp.wait_ge(self.exps, 5)
            for q, x in enumerate((self.li, self.sc, self.em)):
                sp.dma_start(self.cols_d[2 * q * H:2 * (q + 1) * H, :].rearrange(by_row, d=2, t=P), x[:, :, :]
                             ).then_inc(self.stored, 16)
            sp.dma_start(self.r_d.rearrange(by_row, d=2, t=P), self.t[:, :, :]).then_inc(self.stored, 16)
            with nc.allow_non_contiguous_dma("one value of a row"):
                for d in range(2):
                    end = 0 if d else P - 1
                    sp.dma_start(self.sp_d[d * H:(d + 1) * H, :].rearrange("h c -> (h c)").unsqueeze(1),
                                 self.sc[:, d, end:end + 1]).then_inc(self.stored, 16)
            sp.wait_ge(self.stored, 16 * 9)

    def scalar(self, act, kind):
        nc = self.nc
        if kind == "oz":
            act.wait_ge(self.chain, 2)
            nc.scalar.activation(self.t[:, :, :], self.t[:, :, :], ACT.Exp, scale=-1.0).then_inc(self.exps, 1)
            act.wait_ge(self.exps, 1)
            nc.scalar.activation(self.t[:, :, :], self.t[:, :, :], ACT.Ln, bias=1.0).then_inc(self.exps, 1)
        elif kind == "gg":
            act.wait_ge(self.before_there, 16)
            act.wait_ge(self.chain, 12)
            for d in range(2):
                nc.scalar.activation(self.sc[:, d, :], self.t[:, d, :], ACT.Exp, bias=self.ms[:, d:d + 1]).then_inc(self.exps, 1)
            act.wait_ge(self.chain, 13)
            nc.scalar.activation(self.em[:, :, :], self.em[:, :, :], ACT.Exp, scale=-1.0).then_inc(self.exps, 1)

    def vector(self, dve, kind):
        nc, chain = self.nc, self.chain

        def rev(x, d):
            return x[:, ::-1] if d else x
        if kind == "oz":
            nc.vector.memset(self.ones[:, :], 1.0)
            nc.vector.memset(self.zeros[:, :], 0.0)
            dve.wait_ge(self.loaded, 16 * (H + 3))
            for d in range(2):
                nc.vector.tensor_scalar(self.li[:, d, :], self.li[:, d, :], self.bias[:, d, 0:1], None, ALU.add)
                last = nc.vector.tensor_scalar(self.lf[:, d, :], self.lf[:, d, :], self.bias[:, d, 1:2], None, ALU.add)
            last.then_inc(chain, 1)
            dve.wait_ge(chain, 1)
            nc.vector.scalar_tensor_tensor(out=self.t[:, :, :], in0=self.lf[:, :, :], scalar=-1.0, in1=self.lf[:, :, :],
                                           op0=ALU.mult, op1=ALU.max).then_inc(chain, 1)
            dve.wait_ge(self.exps, 2)
            nc.vector.scalar_tensor_tensor(out=self.lf[:, :, :], in0=self.lf[:, :, :], scalar=0.0, in1=self.t[:, :, :],
                                           op0=ALU.min, op1=ALU.subtract).then_inc(chain, 1)
            dve.wait_ge(chain, 3)
            for d in range(2):
                last = nc.vector.tensor_tensor_scan(rev(self.b[:, d, :], d), self.ones[:, :], rev(self.lf[:, d, :], d),
                                                    0.0, ALU.mult, ALU.add)
            last.then_inc(chain, 1)
            dve.wait_ge(chain, 4)
            nc.vector.tensor_tensor(self.li[:, :, :], self.li[:, :, :], self.b[:, :, :], ALU.subtract).then_inc(chain, 1)
            dve.wait_ge(chain, 5)
            for d in range(2):
                last = nc.vector.tensor_tensor_scan(rev(self.g[:, d, :], d), self.zeros[:, :], rev(self.li[:, d, :], d),
                                                    LOWEST, ALU.add, ALU.max)
            last.then_inc(chain, 1)
            dve.wait_ge(chain, 6)
            for d in range(2):
                end = slice(0, 1) if d else slice(P - 1, P)
                nc.vector.tensor_copy(self.ends[:, d, 0:1], self.b[:, d, end])
                last = nc.vector.tensor_tensor(self.ends[:, d, 1:2], self.b[:, d, end], self.g[:, d, end], ALU.add)
            last.then_inc(chain, 2)
        elif kind == "uz":
            dve.wait_ge(self.ends_there, 16)
            m, m0 = self.m_h, self.m0
            for d in range(2):
                for part, start in ((slice(0, CTX), 0.0), (slice(CTX, NC), m0[:, d:d + 1])):
                    last = nc.vector.tensor_tensor_scan(rev(m[:, d, part], d), rev(self.ends_h[:, d, 0, part], d),
                                                        rev(self.ends_h[:, d, 1, part], d), start, ALU.add, ALU.max)
            last.then_inc(chain, 1)
            dve.wait_ge(chain, 9)
            nc.vector.memset(self.ms_h[:, :, 0:CTX], 0.0)
            nc.vector.tensor_copy(self.ms_h[:, 0, CTX:CTX + 1], m0[:, 0:1])
            nc.vector.tensor_copy(self.ms_h[:, 1, NC - 1:NC], m0[:, 1:2])
            nc.vector.tensor_copy(self.ms_h[:, 0, CTX + 1:NC], m[:, 0, CTX:NC - 1])
            nc.vector.tensor_copy(self.ms_h[:, 1, CTX:NC - 1], m[:, 1, CTX + 1:NC]).then_inc(chain, 1)
        elif kind == "gg":
            dve.wait_ge(self.before_there, 16)
            for d in range(2):
                last = nc.vector.tensor_scalar(self.g[:, d, :], self.g[:, d, :], self.ms[:, d:d + 1], None, ALU.max)
            last.then_inc(chain, 1)
            dve.wait_ge(chain, 11)
            nc.vector.tensor_scalar(self.t[:, :, :], self.g[:, :, :], -1.0, None, ALU.mult).then_inc(chain, 1)
            nc.vector.tensor_tensor(self.em[:, :, :], self.g[:, :, :], self.b[:, :, :], ALU.add).then_inc(chain, 1)


def sgu_phase(nc, sem, sb, ps, vb_d, u_d, w_s, b_s, g_sgu, cols_d, sp_d, ident, cols, spb, ysp):
    rows_loaded, rows_turned = sem("s_rows_loaded"), sem("s_rows_turned")
    def two(name):
        return [sem(f"s_{name}{s}") for s in range(2)]
    half_made = sem("s_half_made")
    const_loaded, w_turned, w_taken = sem("s_const"), sem("s_w_turned"), sem("s_w_taken")
    v_loaded, u_loaded, sq_done, var_done, rstd_done, v_scaled, mixed, mix_read, biased, gated, hi_done, lo_done = (
        two(n) for n in ("v_loaded", "u_loaded", "sq_done", "var_done", "rstd_done", "v_scaled", "mixed",
                         "mix_read", "biased", "gated", "hi_done", "lo_done"))
    with ExitStack() as st:
        ws = sb(st, "s_ws", [P, H, P])
        wsT = sb(st, "s_wsT", [P, H, P])
        bsb = sb(st, "s_bsb", [P, H, P])
        gcol = sb(st, "s_gcol", [P, KT])
        vt = sb(st, "s_vt", [P, 2, D])
        ut = sb(st, "s_ut", [P, 2, KT, P])
        sq = sb(st, "s_sq", [P, D])
        ss = sb(st, "s_ss", [P, 2, 4])
        yt = sb(st, "s_yt", [P, 2, KT, P])
        pm = [ps(st, f"s_pm{s}", [P, KT, P]) for s in range(2)]
        rows = sb(st, "s_rows", [6 * H, TOK])
        pw = ps(st, "s_pw", [P, H, P])
        prow = ps(st, "s_prow", [P, NC, 6 * H])

        def none(s, n, c):
            pass

        def chunks(eng, front=none, last=none, scale=none, middle=none, end=none):
            front(0, 0, 0)
            scale(0, 0, 0)
            front(1, 0, 1)
            scale(1, 0, 1)
            middle(0, 0, 0)
            with eng.Fori(0, (NC - 3) // 2) as i:
                front(0, i + 1, 2 * i + 2)
                last(0, i, 2 * i)
                scale(0, i + 1, 2 * i + 2)
                middle(1, i, 2 * i + 1)
                end(0, i, 2 * i)
                front(1, i + 1, 2 * i + 3)
                last(1, i, 2 * i + 1)
                scale(1, i + 1, 2 * i + 3)
                middle(0, i + 1, 2 * i + 2)
                end(1, i, 2 * i + 1)
            front(0, NC // 2, NC - 1)
            last(0, NC // 2 - 1, NC - 3)
            scale(0, NC // 2, NC - 1)
            middle(1, NC // 2 - 1, NC - 2)
            end(0, NC // 2 - 1, NC - 3)
            last(1, NC // 2 - 1, NC - 2)
            middle(0, NC // 2, NC - 1)
            end(1, NC // 2 - 1, NC - 2)
            last(0, NC // 2, NC - 1)
            end(0, NC // 2, NC - 1)

        with nc.Block() as block:
            @block.sync
            def _(sp):
                sp.dma_start(ws[:, :, :], w_s[0].rearrange("g t s -> t g s")).then_inc(const_loaded, 16)
                sp.dma_start(bsb[:, :, :], b_s[0].rearrange("(a g) t -> a g t", a=1).broadcast_to([P, H, P])
                             ).then_inc(const_loaded, 16)
                sp.dma_start(rows[:, :], cols_d).then_inc(rows_loaded, 16)
                sp.dma_start(spb[:, :, :], sp_d.rearrange("(a d) c -> a d c", a=1).broadcast_to([P, 2 * H, NC])
                             ).then_inc(rows_loaded, 16)
                with nc.allow_non_contiguous_dma("vector onto partitions"):
                    sp.dma_start(gcol[:, :], g_sgu[0].rearrange("(k p) -> p k", p=P)).then_inc(const_loaded, 16)

                def load_v(s, n, c):
                    wait_alone(sp, mixed[s], n)
                    sp.dma_start(vt[:, s, :], vb_d[bass.ds(c * P, P), :]).then_inc(v_loaded[s], 16)

                def load_u(s, n, c):
                    wait_alone(sp, gated[s], n)
                    sp.dma_start(ut[:, s, :, :], u_d[:, :, bass.ds(c * P, P)].rearrange("k p t -> p k t")
                                 ).then_inc(u_loaded[s], 16)
                chunks(sp, front=load_v, middle=load_u)
                sp.wait_ge(rows_loaded, 32)

            @block.gpsimd
            def _(pool):
                def rstd(s, n, c):
                    wait_alone(pool, var_done[s], n + 1)
                    nc.gpsimd.tensor_tensor(ss[:, s, 2:3], ss[:, s, 1:2], ss[:, s, 3:4], ALU.pow).then_inc(rstd_done[s], 1)
                nc.gpsimd.memset(ss[:, :, 3:4], -0.5).then_inc(half_made, 1)
                pool.wait_ge(half_made, 1)
                chunks(pool, front=rstd)

            @block.scalar
            def _(act):
                def square(s, n, c):
                    act.wait_ge(v_loaded[s], 16 * n + 16)
                    nc.scalar.activation(sq[:, :], vt[:, s, :], ACT.Square, accum_out=ss[:, s, 0:1]).then_inc(sq_done[s], 1)

                def scale(s, n, c):
                    act.wait_ge(rstd_done[s], n + 1)
                    nc.scalar.activation(vt[:, s, :], vt[:, s, :], ACT.Copy, scale=ss[:, s, 2:3]).then_inc(v_scaled[s], 1)

                def high(s, n, c):
                    act.wait_ge(gated[s], n + 1)
                    nc.scalar.activation(ysp[:, 0, :, bass.ds(c * P, P)], yt[:, s, :, :], ACT.Copy).then_inc(hi_done[s], 1)
                chunks(act, front=square, last=high, scale=scale)

            @block.tensor
            def _(pe):
                pe.wait_ge(const_loaded, 48)
                for g in range(H):
                    last = nc.tensor.transpose(pw[:, g, :], ws[:, g, :], ident[:, :])
                last.then_inc(w_turned, 1)
                pe.wait_ge(rows_loaded, 32)
                for c in range(NC):
                    last = nc.tensor.transpose(prow[:, c, :], rows[:, c * P:(c + 1) * P], ident[0:6 * H, 0:6 * H])
                last.then_inc(rows_turned, 1)
                pe.wait_ge(w_taken, 1)

                def mix(s, n, c):
                    pe.wait_ge(v_scaled[s], n + 1)
                    wait(pe, mix_read[s], n)
                    for k in range(KT):
                        last = nc.tensor.matmul(pm[s][:, k, :], vt[:, s, k * P:(k + 1) * P], wsT[:, k // HT, :],
                                                start=True, stop=True)
                    last.then_inc(mixed[s], 1)
                chunks(pe, middle=mix)

            @block.vector
            def _(dve):
                dve.wait_ge(w_turned, 1)
                nc.vector.tensor_copy(wsT[:, :, :], pw[:, :, :]).then_inc(w_taken, 1)
                dve.wait_ge(rows_turned, 1)
                nc.vector.tensor_copy(cols[:, :, :], prow[:, :, :])

                def variance(s, n, c):
                    dve.wait_ge(sq_done[s], n + 1)
                    nc.vector.tensor_scalar(ss[:, s, 1:2], ss[:, s, 0:1], 1.0 / D, EPS, ALU.mult, ALU.add).then_inc(var_done[s], 1)

                def gate(s, n, c):
                    dve.wait_ge(mixed[s], n + 1)
                    wait(dve, lo_done[s], n)
                    for k in range(KT):
                        last = nc.vector.scalar_tensor_tensor(out=yt[:, s, k, :], in0=pm[s][:, k, :], scalar=gcol[:, k:k + 1],
                                                              in1=bsb[:, k // HT, :], op0=ALU.mult, op1=ALU.add)
                    last.then_inc(mix_read[s], 1)
                    dve.wait_ge(mix_read[s], n + 1)
                    dve.wait_ge(u_loaded[s], 16 * n + 16)
                    nc.vector.tensor_tensor(yt[:, s, :, :], yt[:, s, :, :], ut[:, s, :, :], ALU.mult).then_inc(gated[s], 1)

                def low(s, n, c):
                    dve.wait_ge(hi_done[s], n + 1)
                    nc.vector.tensor_tensor(ysp[:, 1, :, bass.ds(c * P, P)], yt[:, s, :, :],
                                            ysp[:, 0, :, bass.ds(c * P, P)].bitcast(F32), ALU.subtract).then_inc(lo_done[s], 1)
                chunks(dve, front=variance, middle=gate, end=low)


def mlstm_phase(nc, sem, sb, ps, qk_d, v_d, gate_d, r_d, state_C, state_n, new_C, new_n,
                ident, mask, cols, spb, ysp):
    def per(name, n=2):
        return [sem(f"m_{name}{d}") for d in range(n)]

    SL = 3
    qk_loaded, r_loaded, v_loaded, c_done = ([[sem(f"m_{n}{d}{s}") for s in range(SL)] for d in range(2)]
                                             for n in ("qk_loaded", "r_loaded", "v_loaded", "c_done"))
    raw_loaded, n_loaded, st_turned, st_taken = per("raw_loaded"), sem("m_n_loaded"), sem("m_st_turned"), sem("m_st_taken")
    ones_made = sem("m_ones")
    g_loaded, lo_done = ([[sem(f"m_{n}{d}{s}", software_dma=n == "g_loaded") for s in range(2)] for d in range(2)]
                         for n in ("g_loaded", "lo_done"))
    (sk_done, masked, e_done, p_done, ke_done, inter_done, inter_read, intra_done, x_done, neg_done, den_done,
     rec_done, c_updated, h_done, hi_done) = (per(n) for n in (
         "sk_done", "masked", "e_done", "p_done", "ke_done", "inter_done", "inter_read", "intra_done",
         "x_done", "neg_done", "den_done", "rec_done", "c_updated", "h_done", "hi_done"))
    hT_done, gated = sem("m_hT_done"), sem("m_gated")
    ctx_c_taken, ctx_stored = sem("m_ctx_c_taken"), sem("m_ctx_stored", software_dma=True)
    HALF = LAT // 2

    with ExitStack() as st:
        qkt = sb(st, "m_qkt", [P, 2, SL, HT, 2, P])
        vt = sb(st, "m_vt", [P, 2, SL, DE])
        rt = sb(st, "m_rt", [P, 2, SL, P])
        gt = sb(st, "m_gt", [P, 2, 2, HT, P])
        pr = sb(st, "m_pr", [P, 2, P])
        ke = sb(st, "m_ke", [P, 2, DH])
        it = sb(st, "m_it", [P, 2, DE])
        xt = sb(st, "m_xt", [P, 2, DE])
        hs = sb(st, "m_hs", [P, 2, DH])
        dn = sb(st, "m_dn", [P, 2, 2])
        hst = sb(st, "m_hst", [P, NC, DH])
        cc = hst[:, HALF:HALF + 3, :].rearrange("p a n -> p (a n)")[:, 0:HT * DE].rearrange("p (a n) -> p a n", a=HT)
        C = sb(st, "m_C", [P, 2 * H, HT, DE])
        psk = [ps(st, f"m_psk{d}", [P, 3, P]) for d in range(2)]
        pnu = [ps(st, f"m_pnu{d}", [P, DE]) for d in range(2)]
        pin = ps(st, "m_pin", [P, DE])
        phT = ps(st, "m_phT", [P, 2, HT, P])
        pc = ps(st, "m_pc", [P, 2, 512])

        raw = hst[:, 0:2 * HT, :].rearrange("p (j a) k -> p j a k", a=HT)
        with nc.Block() as block:
            @block.sync
            def _(sp):
                with nc.allow_non_contiguous_dma("normalisers"):
                    for j in range(2 * H):
                        d, h = j // H, j % H
                        sp.dma_start(C[:, j, :, DH], state_n[0, 0, d, h].rearrange("(a p) -> p a", p=P)
                                     ).then_inc(n_loaded, 16)
                for j in range(2 * H):
                    if j >= 2:
                        sp.wait_ge(st_turned, j - 1)
                    sp.dma_start(raw[:, j % 2, :, :], state_C[0, 0, j // H, j % H].rearrange("(a p) k -> p a k", p=P)
                                 ).then_inc(raw_loaded[j % 2], 16)
                sp.wait_ge(n_loaded, 2 * H * 16)

            @block.gpsimd
            def _(pool):
                nc.gpsimd.memset(vt[:, :, :, DH:DE], 1.0).then_inc(ones_made, 1)
                pool.wait_ge(ones_made, 1)

            @block.tensor
            def _(pe):
                for j in range(2 * H):
                    pe.wait_ge(raw_loaded[j % 2], 16 * (j // 2 + 1))
                    if j >= 2:
                        pe.wait_ge(st_taken, j - 1)
                    for a in range(HT):
                        for b in range(HT):
                            last = nc.tensor.transpose(pc[:, j % 2, b * DH + a * P:b * DH + (a + 1) * P],
                                                       raw[:, j % 2, a, b * P:(b + 1) * P], ident[:, :])
                    last.then_inc(st_turned, 1)

            @block.vector
            def _(dve):
                for j in range(2 * H):
                    dve.wait_ge(st_turned, j + 1)
                    nc.vector.tensor_copy(C[:, j, :, 0:DH], pc[:, j % 2, :].rearrange("p (b v) -> p b v", b=HT)
                                          ).then_inc(st_taken, 1)

        class Step:

            def __init__(self, h, j=None, slot=2, pair=0, join=False, first=True):
                self.h, self.ctx, self.s = h, j is None, slot
                self.slot_keys = h * (LAT + 1) + (0 if first else j)
                self.slot_inter = h * LAT + (0 if first else j - 1)
                if j is None:
                    self.uses, self.n, self.l, self.c = h, h * (LAT + 1), h * LAT, (0, 0)
                    self.f, self.t = (h * HALF, h * (HALF + 1)), h * (HALF + 1)
                    self.finish, self.gs, self.g = (1,), 1, (h * (HALF // 2), h * (HALF // 2 + 1))
                else:
                    self.uses, self.n, self.l = h * HALF + pair, h * (LAT + 1) + 1 + j, h * LAT + j
                    self.c = (j + CTX, NC - 1 - j)
                    self.f, self.t = (h * HALF + j - HALF, h * (HALF + 1) + 1 + j - HALF), h * (HALF + 1) + 1 + j - HALF
                    self.finish = (0, 1) if join else ()
                    self.gs, nth = slot, pair - HALF // 2
                    self.g = (h * (HALF // 2) + nth, h * (HALF // 2 + slot) + nth + slot)

        def latent(h, at, i=0):
            return Step(h, 2 * i + at, at % 2, i + at // 2, at >= HALF, at < 2)

        def walk(eng, turn):
            with eng.Fori(0, H) as h:
                ctx = Step(h)
                turn(None, ctx, None)
                turn(ctx, latent(h, 0), None)
                turn(latent(h, 0), latent(h, 1), ctx)
                with eng.Fori(0, (HALF - 2) // 2) as i:
                    for j in (1, 2):
                        turn(latent(h, j, i), latent(h, j + 1, i), None)
                turn(latent(h, HALF - 1), latent(h, HALF), None)
                turn(latent(h, HALF), latent(h, HALF + 1), None)
                with eng.Fori(0, (HALF - 2) // 2) as i:
                    for j in (HALF + 1, HALF + 2):
                        turn(latent(h, j, i), latent(h, j + 1, i), latent(h, j - 1, i))
                turn(latent(h, LAT - 1), None, latent(h, LAT - 2))
                turn(None, None, latent(h, LAT - 1))

        def flat(x):
            return x.rearrange("p a n -> p (a n)")

        with nc.Block() as block:
            @block.sync
            def _(sp):
                def turn(cur, w, prev):
                    if w is None:
                        return
                    s, h = w.s, w.h
                    for d in range(2):
                        wait_alone(sp, ke_done[d], w.slot_keys)
                        sp.dma_start(rt[:, d, s, :], r_d[bass.ds(H * d + h, 1), bass.ds(w.c[d] * P, P)].broadcast_to([P, P])
                                     ).then_inc(r_loaded[d][s], 16)
                    for d in range(2):
                        wait_alone(sp, inter_done[d], w.slot_inter)
                        sp.dma_start(qkt[:, d, s, :, :, :].rearrange("p a r t -> p (a r) t"),
                                     qk_d[bass.ds(HT * h, HT), :, :, bass.ds(w.c[d] * P, P)].rearrange("a r p t -> p (a r) t")).then_inc(qk_loaded[d][s], 16)
                    for d in range(2):
                        wait_alone(sp, c_done[d][s], w.uses)
                        sp.dma_start(vt[:, d, s, 0:DH], v_d[bass.ds(w.c[d] * P, P), bass.ds(h * DH, DH)]
                                     ).then_inc(v_loaded[d][s], 16)
                walk(sp, turn)

            def col(w, d, q):
                return cols[:, bass.ds(w.c[d], 1), bass.ds((2 * q + d) * H + w.h, 1)].rearrange("p a b -> p (a b)")

            def out_tile(w, d, part):
                return ysp[:, part, bass.ds(HT * w.h, HT), bass.ds(w.c[d] * P, P)]

            @block.tensor
            def _(pe):
                def scores(w, d):
                    s = w.s
                    pe.wait_ge(qk_loaded[d][s], 16 * w.uses + 16)
                    wait(pe, ke_done[d], w.n)
                    for a in range(HT):
                        nc.tensor.matmul(psk[d][:, 0, :], qkt[:, d, s, a, 1, :], qkt[:, d, s, a, 0, :], start=(a == 0), stop=(a == HT - 1))
                    for a in range(HT):
                        last = nc.tensor.transpose(psk[d][:, 1 + a, :], qkt[:, d, s, a, 1, :], ident[:, :])
                    last.then_inc(sk_done[d], 1)

                def from_state(w, d):
                    wait(pe, c_updated[d], w.l)
                    wait(pe, inter_read[1 - d], w.l + d)
                    for a in range(HT):
                        last = nc.tensor.matmul(pin[:, :], qkt[:, d, w.s, a, 0, :],
                                                flat(C[:, bass.ds(H * d + w.h, 1), a, :]),
                                                start=(a == 0), stop=(a == HT - 1))
                    last.then_inc(inter_done[d], 1)

                def within(w, d):
                    pe.wait_ge(v_loaded[d][w.s], 16 * w.uses + 16)
                    pe.wait_ge(p_done[d], w.n + 1)
                    wait(pe, x_done[d], w.n)
                    nc.tensor.matmul(pnu[d][:, :], pr[:, d, :], vt[:, d, w.s, :], start=True, stop=True).then_inc(intra_done[d], 1)

                def own_state(w, d):
                    s = w.s
                    pe.wait_ge(ke_done[d], w.n + 1)
                    if w.ctx and d == 0:
                        wait(pe, c_updated[1], w.l)
                    elif w.ctx:
                        pe.wait_ge(ctx_c_taken, 2 * w.h + 1)
                    elif d == 0:
                        pe.wait_ge(ctx_c_taken, 2 * w.h + 2)
                        wait(pe, c_updated[1], w.l)
                    else:
                        pe.wait_ge(c_updated[0], w.l + 1)
                    for a in range(HT):
                        if w.ctx:
                            nc.tensor.matmul(pc[:, a, 0:DH], vt[:, d, s, a * P:(a + 1) * P], ke[:, d, :], start=True, stop=True)
                            last = nc.tensor.matmul(pc[:, a, DH:DE], ke[:, d, a * P:(a + 1) * P], vt[:, d, s, DH:DE],
                                                    start=True, stop=True)
                        else:
                            last = nc.tensor.matmul(pc[:, a, 0:DE], ke[:, d, a * P:(a + 1) * P], vt[:, d, s, :],
                                                    start=True, stop=True)
                    last.then_inc(c_done[d][s], 1)

                def turn(cur, nxt, prev):
                    if cur and not cur.ctx:
                        from_state(cur, 0)
                    if cur:
                        within(cur, 0)
                    if cur and not cur.ctx:
                        from_state(cur, 1)
                    if cur:
                        within(cur, 1)
                        own_state(cur, 0)
                    if prev and prev.finish:
                        for d in prev.finish:
                            pe.wait_ge(h_done[d], prev.n + 1)
                        wait(pe, gated, prev.t)
                        for d in prev.finish:
                            for a in range(HT):
                                last = nc.tensor.transpose(phT[:, d, a, :], hs[:, d, a * P:(a + 1) * P], ident[:, :])
                        last.then_inc(hT_done, 1)
                    if nxt:
                        scores(nxt, 0)
                    if cur:
                        own_state(cur, 1)
                    if nxt:
                        scores(nxt, 1)
                walk(pe, turn)

            @block.vector
            def _(dve):
                def exponents(w, d):
                    s = w.s
                    wait_alone(dve, r_loaded[d][s], 16 * w.uses + 16)
                    nc.vector.scalar_tensor_tensor(out=rt[:, d, s, :], in0=rt[:, d, s, :], scalar=col(w, d, 0), in1=mask[:, d, :],
                                                   op0=ALU.add, op1=ALU.add).then_inc(masked[d], 1)

                def probs(w, d):
                    dve.wait_ge(sk_done[d], w.n + 1)
                    dve.wait_ge(e_done[d], w.n + 1)
                    wait(dve, intra_done[d], w.n)
                    nc.vector.tensor_tensor(pr[:, d, :], psk[d][:, 0, :], rt[:, d, w.s, :], ALU.mult).then_inc(p_done[d], 1)

                def update(w, d):
                    dve.wait_ge(c_done[d][w.s], w.uses + 1)
                    if w.ctx:
                        if d == 0:
                            wait(dve, ctx_stored, 64 * w.h)
                        else:
                            dve.wait_ge(ctx_stored, 64 * w.h + 32)
                        nc.vector.tensor_copy(cc[:, :, :], pc[:, :, 0:DE]).then_inc(ctx_c_taken, 1)
                    else:
                        Cs = C[:, bass.ds(H * d + w.h, 1), :, :].rearrange("p a b n -> p (a b) n")
                        nc.vector.scalar_tensor_tensor(out=Cs, in0=Cs,
                                                       scalar=flat(spb[:, bass.ds(H * d + w.h, 1), bass.ds(w.c[d], 1)]),
                                                       in1=pc[:, :, 0:DE], op0=ALU.mult, op1=ALU.add).then_inc(c_updated[d], 1)

                def num(w, d):
                    dve.wait_ge(intra_done[d], w.n + 1)
                    if w.ctx:
                        nc.vector.tensor_copy(xt[:, d, :], pnu[d][:, :]).then_inc(x_done[d], 1)
                    else:
                        dve.wait_ge(inter_read[d], w.l + 1)
                        nc.vector.tensor_tensor(xt[:, d, :], pnu[d][:, :], it[:, d, :], ALU.add).then_inc(x_done[d], 1)

                def den(w):
                    for d in range(2):
                        wait_alone(dve, x_done[d], w.n + 1)
                        nc.vector.scalar_tensor_tensor(out=dn[:, d, 1:2], in0=xt[:, d, DH:DE], scalar=-1.0, in1=col(w, d, 2),
                                                       op0=ALU.mult, op1=ALU.max).then_inc(neg_done[d], 1)
                    for d in range(2):
                        dve.wait_ge(neg_done[d], w.n + 1)
                        nc.vector.tensor_tensor(dn[:, d, 0:1], dn[:, d, 1:2], xt[:, d, DH:DE], ALU.max).then_inc(den_done[d], 1)
                    for d in range(2):
                        dve.wait_ge(den_done[d], w.n + 1)
                        nc.vector.reciprocal(dn[:, d, 1:2], dn[:, d, 0:1]).then_inc(rec_done[d], 1)

                def out(w, d):
                    dve.wait_ge(rec_done[d], w.n + 1)
                    mine = flat(hst[:, bass.ds(w.c[d], 1), :])
                    if d in w.finish:
                        if w.ctx:
                            dve.wait_ge(h_done[0], w.n + 1)
                        else:
                            dve.wait_ge(h_done[1 - d], w.h * (LAT + 1) + 1 + HALF)
                        wait(dve, hT_done, w.t)
                        nc.vector.scalar_tensor_tensor(out=hs[:, d, :], in0=xt[:, d, 0:DH], scalar=dn[:, d, 1:2], in1=mine,
                                                       op0=ALU.mult, op1=ALU.add).then_inc(h_done[d], 1)
                    else:
                        nc.vector.tensor_scalar(mine, xt[:, d, 0:DH], dn[:, d, 1:2], None, ALU.mult).then_inc(h_done[d], 1)

                def gate(w):
                    dve.wait_ge(hT_done, w.t + 1)
                    for d in w.finish:
                        dve.wait_ge(g_loaded[d][w.gs], 16 * w.g[d] + 16)
                    ds = slice(w.finish[0], 2)
                    nc.vector.tensor_tensor(gt[:, w.gs, ds, :, :], phT[:, ds, :, :], gt[:, w.gs, ds, :, :], ALU.mult
                                            ).then_inc(gated, 1)

                def turn(cur, nxt, prev):
                    if nxt:
                        exponents(nxt, 0)
                        exponents(nxt, 1)
                    if cur:
                        num(cur, 0)
                        num(cur, 1)
                        update(cur, 0)
                        den(cur)
                        out(cur, 0)
                        out(cur, 1)
                    if prev and prev.finish:
                        gate(prev)
                    if nxt:
                        probs(nxt, 0)
                    if cur:
                        update(cur, 1)
                    if nxt:
                        probs(nxt, 1)
                    if prev and prev.ctx:
                        wait_alone(dve, ctx_stored, 64 * prev.h + 64)
                walk(dve, turn)

            @block.scalar
            def _(act):
                def weights(w, d):
                    act.wait_ge(masked[d], w.n + 1)
                    nc.scalar.activation(rt[:, d, w.s, :], rt[:, d, w.s, :], ACT.Exp).then_inc(e_done[d], 1)

                def inter(w, d):
                    act.wait_ge(inter_done[d], w.l + 1)
                    wait(act, x_done[d], w.n)
                    nc.scalar.activation(it[:, d, :], pin[:, :], ACT.Copy, scale=col(w, d, 1)).then_inc(inter_read[d], 1)

                def keys(w, d):
                    act.wait_ge(p_done[d], w.n + 1)
                    if w.ctx:
                        wait(act, c_done[d][1], w.h * HALF)
                    elif w.s == 0:
                        wait(act, c_done[d][1], w.uses)
                        act.wait_ge(c_done[d][2], w.h + 1)
                    else:
                        act.wait_ge(c_done[d][0], w.uses + 1)
                    end = 0 if d else P - 1
                    nc.scalar.activation(ke[:, d, :], psk[d][:, 1:3, :].rearrange("p a t -> p (a t)"), ACT.Copy,
                                         scale=rt[:, d, w.s, end:end + 1]).then_inc(ke_done[d], 1)

                def turn(cur, nxt, prev):
                    if cur and not cur.ctx:
                        inter(cur, 0)
                    if cur:
                        keys(cur, 0)
                        keys(cur, 1)
                    if cur and not cur.ctx:
                        inter(cur, 1)
                    if nxt:
                        weights(nxt, 0)
                        weights(nxt, 1)
                    for d in prev.finish if prev else ():
                        act.wait_ge(gated, prev.t + 1)
                        nc.scalar.activation(out_tile(prev, d, 0), gt[:, prev.gs, d, :, :], ACT.Copy).then_inc(hi_done[d], 1)
                walk(act, turn)

            @block.gpsimd
            def _(pool):
                def turn(cur, nxt, prev):
                    if cur and cur.ctx:
                        for d in range(2):
                            wait_alone(pool, ctx_c_taken, 2 * cur.h + d + 1)
                            pool.dma_start(new_C[0, 0, d][bass.ds(cur.h, 1)].rearrange("a (v p) k -> p (a v) k", p=P),
                                           cc[:, :, 0:DH]).then_inc(ctx_stored, 16)
                            with nc.allow_non_contiguous_dma("normalisers"):
                                pool.dma_start(new_n[0, 0, d][bass.ds(cur.h, 1)].rearrange("a (v p) -> p (a v)", p=P),
                                               cc[:, :, DH]).then_inc(ctx_stored, 16)
                    for d in prev.finish if prev else ():
                        wait_alone(pool, hi_done[d], prev.f[d] + 1)
                        nc.gpsimd.tensor_tensor(out_tile(prev, d, 1), gt[:, prev.gs, d, :, :], out_tile(prev, d, 0).bitcast(F32),
                                                ALU.subtract).then_inc(lo_done[d][prev.gs], 1)
                    for d in nxt.finish if nxt else ():
                        wait_alone(pool, lo_done[d][nxt.gs], nxt.g[d])
                        pool.dma_start(gt[:, nxt.gs, d, :, :], gate_d[bass.ds(HT * nxt.h, HT), :, bass.ds(nxt.c[d] * P, P)]
                                       .rearrange("a p t -> p a t")).then_inc(g_loaded[d][nxt.gs], 16)
                walk(pool, turn)
                pool.wait_ge(ctx_stored, 64 * H)


def out_phase(nc, sem, sb, ps, m_d, w_out, gate_d, x_prompt, x_sample, norm_f, y_prompt, y_sample):
    def two(name):
        return [sem(f"o_{name}{s}") for s in range(2)]
    half_made = sem("o_half_made")
    w_loaded, w_hi, w_lo, const_loaded = [sem(f"o_w_loaded{k}") for k in range(KT)], sem("o_w_hi"), sem("o_w_lo"), sem("o_const")
    m_loaded, x_loaded, m_hi, m_lo, prod, gated, added, sq_done, var_done, rstd_done, out_done = (
        two(n) for n in ("m_loaded", "x_loaded", "m_hi", "m_lo", "prod", "gated", "added", "sq_done",
                         "var_done", "rstd_done", "out_done"))
    stored = [sem(f"o_stored{s}", software_dma=True) for s in range(2)]
    with ExitStack() as st:
        raw = sb(st, "o_raw", [P, KT, D])
        wsp = sb(st, "o_wsp", [P, 2, KT, D], F32R)
        mt = sb(st, "o_mt", [P, 2, KT, P])
        msp = sb(st, "o_msp", [P, 2, 2, KT, P], F32R)
        xt = sb(st, "o_xt", [P, 2, D])
        yt = sb(st, "o_yt", [P, 2, D])
        ot = sb(st, "o_ot", [P, 2, D])
        sq = sb(st, "o_sq", [P, D])
        ss = sb(st, "o_ss", [P, 2, 4])
        gb = sb(st, "o_gb", [P, 2, D])
        nf = sb(st, "o_nf", [P, D])
        pp = [ps(st, f"o_pp{s}", [P, 2, 512]) for s in range(2)]

        def chunks(eng, step):
            step(0, 0, 0, 0, None)
            with eng.Fori(0, LAT // 2) as i:
                step(1, i, 2 * i + 1, 1, 2 * i)
                step(0, i + 1, 2 * i + 2, 1, 2 * i + 1)

        with nc.Block() as block:
            @block.sync
            def _(sp):
                def step(s, n, c, j, lat):
                    wait_alone(sp, m_lo[s], n)
                    sp.dma_start(mt[:, s, :, :], m_d[:, :, bass.ds(c * P, P)].rearrange("k p t -> p k t")).then_inc(m_loaded[s], 16)
                    wait_alone(sp, added[s], n)
                    sp.dma_start(xt[:, s, :], x_prompt[0] if lat is None else x_sample[0][bass.ds(lat * P, P), :]
                                 ).then_inc(x_loaded[s], 16)
                chunks(sp, step)

            @block.gpsimd
            def _(pool):
                def step(s, n, c, j, lat):
                    wait_alone(pool, var_done[s], n + 1)
                    nc.gpsimd.tensor_tensor(ss[:, s, 2:3], ss[:, s, 1:2], ss[:, s, 3:4], ALU.pow).then_inc(rstd_done[s], 1)
                    wait_alone(pool, out_done[s], n + 1)
                    pool.dma_start(y_prompt[0] if lat is None else y_sample[0][bass.ds(lat * P, P), :], ot[:, s, :]
                                   ).then_inc(stored[s], 16)
                nc.gpsimd.memset(ss[:, :, 3:4], -0.5).then_inc(half_made, 1)
                pool.wait_ge(half_made, 1)
                chunks(pool, step)
                pool.wait_ge(stored[0], 16 * (LAT // 2 + 1))
                pool.wait_ge(stored[1], 16 * (LAT // 2))

            @block.scalar
            def _(act):
                for k in range(KT):
                    act.dma_start(raw[:, k, :], w_out[k * P:(k + 1) * P, :]).then_inc(w_loaded[k], 16)
                act.dma_start(gb[:, :, :], gate_d.rearrange("(a j) n -> a j n", a=1).broadcast_to([P, 2, D])).then_inc(const_loaded, 16)
                act.dma_start(nf[:, :], norm_f.rearrange("(a n) -> a n", a=1).broadcast_to([P, D])).then_inc(const_loaded, 16)

                def step(s, n, c, j, lat):
                    act.wait_ge(m_loaded[s], 16 * n + 16)
                    wait(act, prod[s], n)
                    nc.scalar.activation(msp[:, s, 0, :, :], mt[:, s, :, :], ACT.Copy).then_inc(m_hi[s], 1)

                def late(s, n):
                    act.wait_ge(added[s], n + 1)
                    nc.scalar.activation(sq[:, :], yt[:, s, :], ACT.Square, accum_out=ss[:, s, 0:1]).then_inc(sq_done[s], 1)

                step(0, 0, 0, 0, None)
                for k in range(KT):
                    act.wait_ge(w_loaded[k], 16)
                    nc.scalar.activation(wsp[:, 0, k, :], raw[:, k, :], ACT.Copy).then_inc(w_hi, 1)
                with act.Fori(0, LAT // 2) as i:
                    step(1, i, 2 * i + 1, 1, 2 * i)
                    late(0, i)
                    step(0, i + 1, 2 * i + 2, 1, 2 * i + 1)
                    late(1, i)
                late(0, LAT // 2)

            @block.tensor
            def _(pe):
                def step(s, n, c, j, lat):
                    pe.wait_ge(m_lo[s], n + 1)
                    wait(pe, gated[s], n)
                    for half in range(2):
                        for k in range(KT):
                            if lat is None and half == 0:
                                pe.wait_ge(w_lo, k + 1)
                            for q, (mp, wp) in enumerate(((1, 0), (0, 1), (0, 0))):
                                last = nc.tensor.matmul(pp[s][:, half, :], msp[:, s, mp, k, :],
                                                        wsp[:, wp, k, half * 512:(half + 1) * 512],
                                                        start=(k == 0 and q == 0), stop=(k == KT - 1 and q == 2))
                    last.then_inc(prod[s], 1)
                chunks(pe, step)

            @block.vector
            def _(dve):
                def step(s, n, c, j, lat):
                    dve.wait_ge(m_hi[s], n + 1)
                    nc.vector.tensor_tensor(msp[:, s, 1, :, :], mt[:, s, :, :], msp[:, s, 0, :, :].bitcast(F32),
                                            ALU.subtract).then_inc(m_lo[s], 1)

                def late(s, n, j):
                    dve.wait_ge(prod[s], n + 1)
                    wait(dve, out_done[s], n)
                    nc.vector.tensor_tensor(yt[:, s, :], pp[s][:, :, :].rearrange("p a n -> p (a n)"), gb[:, j, :],
                                            ALU.mult).then_inc(gated[s], 1)
                    dve.wait_ge(gated[s], n + 1)
                    dve.wait_ge(x_loaded[s], 16 * n + 16)
                    nc.vector.tensor_tensor(yt[:, s, :], yt[:, s, :], xt[:, s, :], ALU.add).then_inc(added[s], 1)
                    dve.wait_ge(sq_done[s], n + 1)
                    nc.vector.tensor_scalar(ss[:, s, 1:2], ss[:, s, 0:1], 1.0 / D, EPS, ALU.mult, ALU.add).then_inc(var_done[s], 1)
                    dve.wait_ge(rstd_done[s], n + 1)
                    wait(dve, stored[s], 16 * n)
                    nc.vector.scalar_tensor_tensor(out=ot[:, s, :], in0=yt[:, s, :], scalar=ss[:, s, 2:3], in1=nf[:, :],
                                                   op0=ALU.mult, op1=ALU.mult).then_inc(out_done[s], 1)

                step(0, 0, 0, 0, None)
                for k in range(KT):
                    dve.wait_ge(w_hi, k + 1)
                    nc.vector.tensor_tensor(wsp[:, 1, k, :], raw[:, k, :], wsp[:, 0, k, :].bitcast(F32),
                                            ALU.subtract).then_inc(w_lo, 1)
                step(1, 0, 1, 1, 0)
                dve.wait_ge(const_loaded, 32)
                late(0, 0, 0)
                with dve.Fori(0, LAT // 2 - 1) as i:
                    step(0, i + 1, 2 * i + 2, 1, 2 * i + 1)
                    late(1, i, 1)
                    step(1, i + 1, 2 * i + 3, 1, 2 * i + 2)
                    late(0, i + 1, 1)
                step(0, LAT // 2, LAT, 1, LAT - 1)
                late(1, LAT // 2 - 1, 1)
                late(0, LAT // 2, 1)


_INS = ["x_prompt", "x_sample", "c", "state_C", "state_n", "state_m", "c_ctx", "norm_g", "w_ada", "b_ada", "w_in",
        "b_if", "g_sgu", "w_s", "b_s", "w_proj_a", "w_proj_b", "w_out", "norm_f"]
_OUTS = [(1, 128, 1024), (1, 2048, 1024), (1, 1, 2, 4, 256, 256), (1, 1, 2, 4, 256), (1, 1, 2, 4)]


def kernel(**inputs):
    import numpy as _np
    import concourse.bacc as _bacc
    from concourse.bass_utils import run_bass_kernel_spmd as _run

    nc = _bacc.Bacc("TRN2", target_bir_lowering=False, num_devices=1)
    arrays, args = {}, []
    for name in _INS:
        a = _np.ascontiguousarray(inputs[name])
        arrays[f"in_{name}"] = a
        args.append(nc.dram_tensor(f"in_{name}", a.shape, mybir.dt.from_np(a.dtype), kind="ExternalInput").ap())
    for i, shape in enumerate(_OUTS):
        args.append(nc.dram_tensor(f"out_{i}", shape, F32, kind="ExternalOutput").ap())
    build(nc, *args)
    r = _run(nc, [arrays], core_ids=[0])
    return tuple(r.results[0][f"out_{i}"] for i in range(len(_OUTS)))
```
